# Optimizing a Trainium2 kernel written in Bass

```python
import jax
import jax.numpy as jnp
from jax import lax
import numpy as np

D_MODEL = 1024
BATCH = 1
SEQ = 512
DEPTH = 2

N_EVEN = (DEPTH + 1) // 2
N_ODD = DEPTH // 2
NORM_EPS = 1e-6
D_FF = 4 * D_MODEL

LRU_WIDTH = D_MODEL // 2
LRU_BLOCKS = 8
LRU_BLOCK = LRU_WIDTH // LRU_BLOCKS
CONV_WIDTH = 4
LRU_C = 8.0

RWKV_WIDTH = D_MODEL // 2
RWKV_HEAD = 64
RWKV_HEADS = RWKV_WIDTH // RWKV_HEAD
DECAY_LORA = 64
AAA_LORA = 64
GATE_LORA = 128
RWKV_LN_EPS = 64e-5
RWKV_COLS = 3 * RWKV_WIDTH + DECAY_LORA + AAA_LORA + GATE_LORA
AB_IN = 2 * LRU_WIDTH + RWKV_COLS

RET_HEADS = 4
RET_QK = D_MODEL
RET_V = 2 * D_MODEL
RET_DK = RET_QK // RET_HEADS
RET_DV = RET_V // RET_HEADS
RET_CHUNK = 128
RET_EPS = 1e-6
ROPE_BASE = 10000.0
RET_IN = 2 * RET_QK + 2 * RET_V

kernel_name = "hybrid_rglru_rwkv7_retention_trunk"

def rms_norm(x, g, eps=NORM_EPS):
    xf = x.astype(jnp.float32)
    y = xf * lax.rsqrt(jnp.mean(xf * xf, axis=-1, keepdims=True) + eps)
    return (y * g.astype(jnp.float32)).astype(x.dtype)

def sq_relu_mlp(x, w_in, w_out):
    return jnp.square(jax.nn.relu(x @ w_in)) @ w_out

def causal_depthwise_conv(u, w, b):
    k = w.shape[0]
    out = lax.conv_general_dilated(
        u, w[:, None, :], window_strides=(1,), padding=[(k - 1, 0)],
        dimension_numbers=("NWC", "WIO", "NWC"), feature_group_count=u.shape[-1])
    return out + b

def rg_lru(u, wa, ba, wx, bx, lam):
    b_, t, w = u.shape
    ub = u.reshape(b_, t, LRU_BLOCKS, LRU_BLOCK)
    r = jax.nn.sigmoid((jnp.einsum("btnc,ncd->btnd", ub, wa).reshape(b_, t, w) + ba).astype(jnp.float32))
    i = jax.nn.sigmoid((jnp.einsum("btnc,ncd->btnd", ub, wx).reshape(b_, t, w) + bx).astype(jnp.float32))
    log_a = -LRU_C * r * jax.nn.softplus(-lam.astype(jnp.float32))
    a = jnp.exp(log_a)
    drive = jnp.sqrt(-jnp.expm1(2.0 * log_a)) * (i * u.astype(jnp.float32))

    def combine(lhs, rhs):
        a1, b1 = lhs
        a2, b2 = rhs
        return a1 * a2, a2 * b1 + b2

    _, h = lax.associative_scan(combine, (a, drive), axis=1)
    return h

def rwkv7_time_mix(cols, w0, w2, a0, a2, g2, k_k, k_a, r_k, ln_w, ln_b):
    f32 = jnp.float32
    cols = cols.astype(f32)
    b_, t, _ = cols.shape
    hs = (b_, t, RWKV_HEADS, RWKV_HEAD)
    o = RWKV_WIDTH
    r = cols[..., 0:o]
    k = cols[..., o:2 * o]
    v = cols[..., 2 * o:3 * o]
    dw = cols[..., 3 * o:3 * o + DECAY_LORA]
    da = cols[..., 3 * o + DECAY_LORA:3 * o + DECAY_LORA + AAA_LORA]
    dg = cols[..., 3 * o + DECAY_LORA + AAA_LORA:]

    w_log = -jax.nn.softplus(-(w0 + jnp.tanh(dw) @ w2)) - 0.5
    decay = jnp.exp(-jnp.exp(w_log))
    a = jax.nn.sigmoid(a0 + da @ a2)
    g = jax.nn.sigmoid(dg) @ g2
    kk = (k * k_k).reshape(hs)
    kk = kk / jnp.maximum(jnp.sqrt(jnp.sum(kk * kk, axis=-1, keepdims=True)), 1e-12)
    k = k * (1.0 + (a - 1.0) * k_a)

    r_h, k_h, v_h = r.reshape(hs), k.reshape(hs), v.reshape(hs)
    w_h, a_h = decay.reshape(hs), a.reshape(hs)
    z_h = -kk
    b_h = kk * a_h

    def step(s, inp):
        r_t, w_t, k_t, v_t, z_t, bb_t = inp
        sz = jnp.einsum("bhij,bhj->bhi", s, z_t)
        s = s * w_t[:, :, None, :] + sz[..., None] * bb_t[:, :, None, :] + v_t[..., None] * k_t[:, :, None, :]
        return s, jnp.einsum("bhij,bhj->bhi", s, r_t)

    tm = lambda arr: jnp.moveaxis(arr, 1, 0)
    s0 = jnp.zeros((b_, RWKV_HEADS, RWKV_HEAD, RWKV_HEAD), f32)
    _, y = lax.scan(step, s0, (tm(r_h), tm(w_h), tm(k_h), tm(v_h), tm(z_h), tm(b_h)))
    y = jnp.moveaxis(y, 0, 1)

    mu = jnp.mean(y, axis=-1, keepdims=True)
    var = jnp.mean(jnp.square(y - mu), axis=-1, keepdims=True)
    yn = ((y - mu) * lax.rsqrt(var + RWKV_LN_EPS)).reshape(b_, t, RWKV_WIDTH) * ln_w + ln_b
    bonus = jnp.sum(r_h * k_h * r_k.reshape(RWKV_HEADS, RWKV_HEAD), axis=-1, keepdims=True) * v_h
    return (yn + bonus.reshape(b_, t, RWKV_WIDTH)) * g

def mixer_ab(h, w_in, w_out, conv_w, conv_b, wa, ba, wx, bx, lam,
             mu, w0, w2, a0, a2, g2, k_k, k_a, r_k, ln_w, ln_b):
    u = h @ w_in
    ax = u[..., :LRU_WIDTH]
    ag = u[..., LRU_WIDTH:2 * LRU_WIDTH]
    bc = u[..., 2 * LRU_WIDTH:]
    ax = causal_depthwise_conv(ax, conv_w, conv_b)
    ya = rg_lru(ax, wa, ba, wx, bx, lam) * jax.nn.gelu(ag.astype(jnp.float32))
    prev = jnp.pad(bc, ((0, 0), (1, 0), (0, 0)))[:, :-1]
    bc = bc + (prev - bc) * mu
    yb = rwkv7_time_mix(bc, w0, w2, a0, a2, g2, k_k, k_a, r_k, ln_w, ln_b)
    y = jnp.concatenate([ya, yb], axis=-1).astype(h.dtype)
    return y @ w_out

def rotary(x, pos):
    half = x.shape[-1] // 2
    inv = 1.0 / (ROPE_BASE ** (jnp.arange(half, dtype=jnp.float32) / half))
    ang = pos.astype(jnp.float32)[:, None] * inv[None, :]
    cos = jnp.cos(ang)[:, None, :]
    sin = jnp.sin(ang)[:, None, :]
    x1, x2 = x[..., :half], x[..., half:]
    return jnp.concatenate([x1 * cos - x2 * sin, x2 * cos + x1 * sin], axis=-1)

def retention_chunkwise(q, k, v):
    f32 = jnp.float32
    b_, t, h, _ = q.shape
    c = RET_CHUNK
    nc = t // c
    log_g = jnp.log1p(-jnp.power(2.0, -5.0 - jnp.arange(h, dtype=f32)))
    idx = jnp.arange(c, dtype=f32)
    rel = idx[:, None] - idx[None, :]
    intra = jnp.where(rel >= 0, jnp.exp(log_g[:, None, None] * jnp.maximum(rel, 0.0)), 0.0)
    q_dec = jnp.exp(log_g[:, None] * (idx + 1.0)).T[None, :, :, None]
    k_dec = jnp.exp(log_g[:, None] * (c - 1.0 - idx)).T[None, :, :, None]
    chunk_dec = jnp.exp(log_g * c)[None, :, None, None]

    def to_chunks(arr):
        return jnp.moveaxis(arr.reshape(b_, nc, c, h, arr.shape[-1]), 1, 0)

    def step(state, inp):
        qc, kc, vc = inp
        s = jnp.einsum("bihd,bjhd->bhij", qc, kc) * intra[None]
        inner = jnp.einsum("bhij,bjhe->bihe", s, vc)
        cross = jnp.einsum("bihd,bhde->bihe", qc, state) * q_dec
        state = state * chunk_dec + jnp.einsum("bjhd,bjhe->bhde", kc * k_dec, vc)
        return state, inner + cross

    s0 = jnp.zeros((b_, h, q.shape[-1], v.shape[-1]), f32)
    _, out = lax.scan(step, s0, (to_chunks(q), to_chunks(k), to_chunks(v)))
    return jnp.moveaxis(out, 0, 1).reshape(b_, t, h, v.shape[-1])

def mixer_ret(h, w_in, w_out, pos):
    f32 = jnp.float32
    b_, t, _ = h.shape
    u = h @ w_in
    q = u[..., :RET_QK].reshape(b_, t, RET_HEADS, RET_DK).astype(f32)
    k = u[..., RET_QK:2 * RET_QK].reshape(b_, t, RET_HEADS, RET_DK).astype(f32)
    v = u[..., 2 * RET_QK:2 * RET_QK + RET_V].reshape(b_, t, RET_HEADS, RET_DV).astype(f32)
    g = u[..., 2 * RET_QK + RET_V:].astype(f32)
    q = rotary(q, pos)
    k = rotary(k, pos) * (RET_DK ** -0.5)
    y = retention_chunkwise(q, k, v)
    y = y * lax.rsqrt(jnp.mean(y * y, axis=-1, keepdims=True) + RET_EPS)
    y = jax.nn.silu(g) * y.reshape(b_, t, RET_V)
    return y.astype(h.dtype) @ w_out

def setup_inputs(seed: int = 0) -> dict:
    key = jax.random.key(seed)
    ks = jax.random.split(key, 32)
    f32 = jnp.float32

    def nrm(k, shape, scale):
        return jax.random.normal(k, shape, f32) * scale

    def gain(k, shape):
        return 1.0 + 0.05 * jax.random.normal(k, shape, f32)

    lam_u = jax.random.uniform(ks[14], (N_EVEN, LRU_WIDTH), f32, 0.9, 0.999)
    a_base = lam_u ** (1.0 / LRU_C)
    lru_lambda = jnp.log(a_base) - jnp.log1p(-a_base)

    return {
        "x": nrm(ks[0], (BATCH, SEQ, D_MODEL), 1.0),
        "norm_mix_pre": gain(ks[1], (DEPTH, D_MODEL)),
        "norm_mix_post": gain(ks[2], (DEPTH, D_MODEL)),
        "norm_ffn_pre": gain(ks[3], (DEPTH, D_MODEL)),
        "norm_ffn_post": gain(ks[4], (DEPTH, D_MODEL)),
        "ffn_w_in": nrm(ks[5], (DEPTH, D_MODEL, D_FF), D_MODEL ** -0.5),
        "ffn_w_out": nrm(ks[6], (DEPTH, D_FF, D_MODEL), D_FF ** -0.5),
        "ab_w_in": nrm(ks[7], (N_EVEN, D_MODEL, AB_IN), D_MODEL ** -0.5),
        "ab_w_out": nrm(ks[8], (N_EVEN, LRU_WIDTH + RWKV_WIDTH, D_MODEL), (LRU_WIDTH + RWKV_WIDTH) ** -0.5),
        "lru_conv_w": nrm(ks[9], (N_EVEN, CONV_WIDTH, LRU_WIDTH), CONV_WIDTH ** -0.5),
        "lru_conv_b": nrm(ks[10], (N_EVEN, LRU_WIDTH), 0.01),
        "lru_wa": nrm(ks[11], (N_EVEN, LRU_BLOCKS, LRU_BLOCK, LRU_BLOCK), LRU_BLOCK ** -0.5),
        "lru_ba": nrm(ks[12], (N_EVEN, LRU_WIDTH), 0.01),
        "lru_wx": nrm(ks[13], (N_EVEN, LRU_BLOCKS, LRU_BLOCK, LRU_BLOCK), LRU_BLOCK ** -0.5),
        "lru_bx": nrm(ks[15], (N_EVEN, LRU_WIDTH), 0.01),
        "lru_lambda": lru_lambda,
        "rwkv_mu": jax.random.uniform(ks[16], (N_EVEN, RWKV_COLS), f32, 0.0, 1.0),
        "rwkv_w0": jax.random.uniform(ks[17], (N_EVEN, RWKV_WIDTH), f32, -6.0, -1.0),
        "rwkv_w2": nrm(ks[18], (N_EVEN, DECAY_LORA, RWKV_WIDTH), 0.5 * DECAY_LORA ** -0.5),
        "rwkv_a0": nrm(ks[19], (N_EVEN, RWKV_WIDTH), 0.1),
        "rwkv_a2": nrm(ks[20], (N_EVEN, AAA_LORA, RWKV_WIDTH), 0.5 * AAA_LORA ** -0.5),
        "rwkv_g2": nrm(ks[21], (N_EVEN, GATE_LORA, RWKV_WIDTH), GATE_LORA ** -0.5),
        "rwkv_k_k": 0.85 + nrm(ks[22], (N_EVEN, RWKV_WIDTH), 0.05),
        "rwkv_k_a": 1.0 + nrm(ks[23], (N_EVEN, RWKV_WIDTH), 0.05),
        "rwkv_r_k": nrm(ks[24], (N_EVEN, RWKV_WIDTH), 0.1),
        "rwkv_ln_w": gain(ks[25], (N_EVEN, RWKV_WIDTH)),
        "rwkv_ln_b": nrm(ks[26], (N_EVEN, RWKV_WIDTH), 0.01),
        "ret_w_in": nrm(ks[27], (N_ODD, D_MODEL, RET_IN), D_MODEL ** -0.5),
        "ret_w_out": nrm(ks[28], (N_ODD, RET_V, D_MODEL), RET_V ** -0.5),
    }

def reference(x, norm_mix_pre, norm_mix_post, norm_ffn_pre, norm_ffn_post, ffn_w_in, ffn_w_out,
              ab_w_in, ab_w_out, lru_conv_w, lru_conv_b, lru_wa, lru_ba, lru_wx, lru_bx, lru_lambda,
              rwkv_mu, rwkv_w0, rwkv_w2, rwkv_a0, rwkv_a2, rwkv_g2, rwkv_k_k, rwkv_k_a, rwkv_r_k,
              rwkv_ln_w, rwkv_ln_b, ret_w_in, ret_w_out):
    pos = jnp.arange(x.shape[1], dtype=jnp.int32)
    h = x
    for layer in range(DEPTH):
        hn = rms_norm(h, norm_mix_pre[layer])
        if layer % 2 == 0:
            e = layer // 2
            m = mixer_ab(hn, ab_w_in[e], ab_w_out[e], lru_conv_w[e], lru_conv_b[e],
                         lru_wa[e], lru_ba[e], lru_wx[e], lru_bx[e], lru_lambda[e],
                         rwkv_mu[e], rwkv_w0[e], rwkv_w2[e], rwkv_a0[e], rwkv_a2[e], rwkv_g2[e],
                         rwkv_k_k[e], rwkv_k_a[e], rwkv_r_k[e], rwkv_ln_w[e], rwkv_ln_b[e])
        else:
            o = layer // 2
            m = mixer_ret(hn, ret_w_in[o], ret_w_out[o], pos)
        h = h + rms_norm(m, norm_mix_post[layer])
        f = sq_relu_mlp(rms_norm(h, norm_ffn_pre[layer]), ffn_w_in[layer], ffn_w_out[layer])
        h = h + rms_norm(f, norm_ffn_post[layer])
    return h


_drawn_inputs = setup_inputs


def setup_inputs(seed=0):
    import zlib

    import numpy as np

    out = dict(_drawn_inputs(seed))
    spreads = {}
    factors = {'lru_ba': 40.544, 'lru_bx': 27.177, 'rwkv_w2': 3.142, 'rwkv_ln_b': 6.186}
    for name, (base, spread) in spreads.items():
        noise = np.random.default_rng([zlib.crc32(name.encode()), seed]).standard_normal(out[name].shape)
        drawn = base * np.exp(spread * noise) if base else spread * noise
        out[name] = jnp.asarray(drawn.astype(out[name].dtype))
    for name, factor in factors.items():
        out[name] = (out[name] * factor).astype(out[name].dtype)
    return out
```

```python
from contextlib import ExitStack

import numpy as np

import concourse.bass as bass
from concourse import mybir

F32 = mybir.dt.float32
F32R = mybir.dt.float32r
ALU = mybir.AluOpType
ACT = mybir.ActivationFunctionType

P = 128
D = 1024
T = 512
KT = D // P
TT = T // P
FF = 4 * D
EPS = 1e-6
C = 64
NCH = T // C
PAIRS = 4
LRU_C = 8.0
LN_EPS = 64e-5
EXP_HALF = float(np.exp(-0.5))
RET_HEADS = 4
RET_DV = 512
CHUNK = 2048
QUARTERS = 4

AB_CHUNK = 0
AB_TURN = 4
FFN0_CHUNK = AB_CHUNK + 1 + AB_TURN * PAIRS
RET_CHUNK0 = FFN0_CHUNK + 8 * QUARTERS
FFN1_CHUNK = RET_CHUNK0 + 8 * RET_HEADS
ALL_CHUNKS = FFN1_CHUNK + 8 * QUARTERS

V_NORM = 0
V_MU_LORA = 2 * 4 * KT
V_LAM = V_MU_LORA + 2
V_ONE = V_LAM + PAIRS
NVEC = V_ONE + 1

P_W2A2, P_G2, P_WA, P_WX, P_VEC = 0, 128, 256, 320, 384
(Q_MUR, Q_MUK, Q_MUV, Q_W0, Q_A0, Q_KK, Q_KA, Q_RK, Q_LNW, Q_LNB, Q_CW, _, _, _, Q_CB, Q_BA,
 Q_BX) = range(P_VEC, P_VEC + 17)
NPAIR = P_VEC + 17

K_EYE, K_EYE2, K_HEAD1, K_HEADS = 0, 128, 192, 194
K_D16T, K_O32T, K_D16, K_O32, K_O64, K_LT, K_LE = (322 + 64 * i for i in range(7))
K_RESET = 322 + 64 * 7
NCONST = K_RESET + T
R_COS, R_SIN, R_DECAY = 0, T, 2 * T
NRET = 2 * T + RET_HEADS * T


SERIES = {
    "low_rank_products": "lin_w lin_a lin_g",
    "turned_products": "z_turned b_turned k_turned v_turned",
    "chunk_products": "azb_t azb azk_t arb_t ark_t",
    "power_products": "m2 m2_t m4 m4_t e2 e4 m8 e8",
    "gate_products": "gate_r gate_i",
    "inverse_products": "dd y32 x32 t32_t t32 y64 tt",
    "solved_products": "w1 w2 gg qq",
    "head_statistics": "kk_sum kk_spread y_sum y_var ln_spread",
    "low_rank_factors": "decay_rate iclr g_out",
    "decay_powers": "dec dec_inv dec_before",
    "vectors_by_token": "z_by_token b_by_token k_by_token v_by_token",
    "copied_by_act": "m2_s x2_s m4_s m8_s dd_s y32_s x32_s y64_s w1_s",
    "lru_factors": "lru_r lru_gates lru_tanh lru_a lru_root gelu",
    "masked_products": "nt o32t nn o32 o64 e1 azk arb ark",
    "summed_by_dve": "m2_ts m4_ts e2_s e4_s dt_s t32_ts t32_s tt_s w2_s g_s q_s",
    "chunk_vectors": "kk_ready z_ready b_plain b_ready kd_ready rd_ready rk_ready pc_ready",
    "lru_steps": "lru_iu lru_scale lru_drive lru_h ya_ready",
    "head_outputs": "yc ln_inv yn y_affine y_bonus yb_ready",
}
SERIES_OF = {name: (group, k, len(names.split())) for group, names in SERIES.items()
             for k, name in enumerate(names.split())}


def constants():
    c = np.zeros((P, NCONST), np.float32)
    row, col = np.arange(P)[:, None] % C, np.arange(C)[None, :]
    c[:, K_EYE:K_EYE + P] = np.eye(P)
    c[:, K_EYE2:K_EYE2 + C] = row == col
    head = np.arange(P) // C
    c[:, K_HEAD1:K_HEAD1 + 2] = head[:, None] == np.arange(2)[None, :]
    c[:, K_HEADS:K_HEADS + P] = head[:, None] == head[None, :]
    for at, r, k in ((K_D16T, col, row), (K_D16, row, col)):
        c[:, at:at + C] = (r > k) & (r // 16 == k // 16)
    for at, r, k in ((K_O32T, col, row), (K_O32, row, col)):
        c[:, at:at + C] = (r > k) & (r // 16 != k // 16) & (r // 32 == k // 32)
    c[:, K_O64:K_O64 + C] = (row > col) & (row // 32 != col // 32)
    c[:, K_LT:K_LT + C] = row < col
    c[:, K_LE:K_LE + C] = row <= col
    c[:, K_RESET:] = np.arange(T)[None, :] % C != 0
    r = np.zeros((P, NRET), np.float32)
    inv = (1.0 / (np.float32(10000.0) ** (np.arange(P, dtype=np.float32) / P))).astype(np.float32)
    ang = (inv[:, None] * np.arange(T, dtype=np.float32)[None, :]).astype(np.float32).astype(np.float64)
    r[:, R_COS:R_COS + T] = np.cos(ang)
    r[:, R_SIN:R_SIN + T] = np.sin(ang)
    rel = np.arange(T)[None, :] - np.arange(P)[:, None]
    for h in range(RET_HEADS):
        decay = np.exp(np.log1p(-2.0 ** (-5.0 - h)) * np.maximum(rel, 0)) / 16.0
        r[:, R_DECAY + h * T:R_DECAY + (h + 1) * T] = np.where(rel >= 0, decay, 0.0)
    return c, r


class Turns:

    def __init__(self, kinds):
        self.n = [0] * kinds
        self.per = [0] * kinds
        self.turn = 0

    def loop(self, turn, per):
        self.turn, self.per = turn, per

    def end(self, turns):
        self.n = [n + (turns - 1) * p for n, p in zip(self.n, self.per)]
        self.loop(0, [0] * len(self.n))

    def next(self, kind):
        self.n[kind] += 1
        return self.now(kind)

    def now(self, kind):
        return self.n[kind] + self.turn * self.per[kind] if self.per[kind] else self.n[kind]


def trunk_kernel(nc, x, weights, pairs, vectors, const, ret_const, out):
    with ExitStack() as ctx:
        def sb(name, cols, dt=F32):
            return ctx.enter_context(nc.sbuf_tensor(name, [P] + (cols if isinstance(cols, list) else [cols]), dt))

        sems = {}

        def S(name):
            name = SERIES_OF.get(name, (name,))[0]
            if name not in sems:
                sems[name] = ctx.enter_context(nc.semaphore(name))
            return sems[name]

        def nth(name, n):
            if name not in SERIES_OF:
                return S(name), n
            _, place, size = SERIES_OF[name]
            return S(name), (n - 1) * size + place + 1

        h = sb("h", [KT, T])
        f = sb("f", [KT, T])
        XH = sb("XH", [KT, T], F32R)
        XL = sb("XL", [KT, T], F32R)
        raw = [sb(f"raw{i}", CHUNK) for i in range(2)]
        WH = [sb(f"WH{i}", CHUNK, F32R) for i in range(2)]
        WL = [sb(f"WL{i}", CHUNK, F32R) for i in range(2)]
        cst = sb("cst", NCONST)
        vec = sb("vec", NVEC)
        root = sb("root", 8)
        rstd = sb("rstd", 8)
        epsc = sb("epsc", 2)
        sp = sb("sp", [12, PAIRS])


        ARENA = 90 * 1024
        start = (nc.sbuf_base + 31) // 32 * 32
        sb("arena", ARENA // 4 + 8)

        class Place:

            def __init__(self):
                self.at = start

            def __call__(self, name, cols, dt=F32):
                cols = cols if isinstance(cols, list) else [cols]
                t = nc.alloc_sbuf_tensor_at(name, [P] + cols, dt, offset=self.at)
                self.at += (int(np.prod(cols)) * 4 + 31) // 32 * 32
                assert self.at <= start + ARENA, (name, self.at - start)
                return t

        norm = Place()
        sq, hn = norm("sq", [2, T]), norm("hn", [2, T])
        NORM = norm.at
        ab = Place()
        W = [ab(f"W{i}", T) for i in range(12)]
        yH, yL = ab("yH", [2, T], F32R), ab("yL", [2, T], F32R)
        Ur, Uk, Uv = (ab(n, T + 1) for n in ("Ur", "Uk", "Uv"))
        Uax, Uag = ab("Uax", T + 3), ab("Uag", T)
        lora, gate_in = ab("lora", T), ab("gate_in", T)
        stage, pp = ab("stage", NPAIR), ab("pp", NPAIR)
        BDa, BDx = ab("BDa", P), ab("BDx", P)
        mixdiff = ab("mixdiff", T)
        bonus, gout, Rd = (ab(n, T) for n in ("bonus", "gout", "Rd"))
        Zt, Bt, Kt, Vt, ARB, ARK, X2 = (ab(n, T) for n in ("Zt", "Bt", "Kt", "Vt", "ARB", "ARK", "X2"))
        O32T, O32, O64 = (ab(n, T) for n in ("O32T", "O32", "O64"))
        lax, lra, lix, ldr, lgate = (ab(n, T) for n in ("lax", "lra", "lix", "ldr", "lgate"))
        kkm, kkroot, kkinv, lnroot, lninv, PC = (ab(n, 8) for n in
                                                 ("kkm", "kkroot", "kkinv", "lnroot", "lninv", "PC"))
        ffn = Place()
        ffn.at = NORM
        AH, AL = ffn("AH", [KT, T], F32R), ffn("AL", [KT, T], F32R)
        relu, square = ffn("relu", [2, T]), ffn("square", [2, T])
        re = Place()
        re.at = NORM
        BH, BL = re("BH", [4, T], F32R), re("BL", [4, T], F32R)
        qr, kr = re("qr", [2, T]), re("kr", [2, T])
        Vr, Sc = re("Vr", [TT, T]), re("Sc", [TT, T])
        rc = re("rc", NRET)
        sg, rt, yv = re("sg", [4, T]), re("rt", [4, T]), re("yv", [4, T])

        bank = [ctx.enter_context(nc.psum_tensor(f"bank{i}", [P, T], F32)) for i in range(8)]

        eye = cst[:, K_EYE:K_EYE + P]
        eye2 = cst[:, K_EYE2:K_EYE2 + C]
        heads = cst[:, K_HEADS:K_HEADS + P]
        head1 = cst[:, K_HEAD1:K_HEAD1 + 2]
        ones1 = vec[:, NVEC - 1:NVEC]
        X = [(XH[:, kt, :], XL[:, kt, :]) for kt in range(KT)]
        A = [(AH[:, kt, :], AL[:, kt, :]) for kt in range(KT)]

        def chunked(t):
            return t[:].rearrange("p (c t) -> p c t", t=C)

        def table(k):
            return cst[:, k:k + C][:, None, :].to_broadcast([P, NCH, C])

        def gain(layer, kind, kt):
            i = V_NORM + (layer * 4 + kind) * KT + kt
            return vec[:, i:i + 1]

        def pv(q):
            return pp[:, q:q + 1]

        def chunk(c, i=0, per=0):
            return (c + per * i if per else c), c % 2

        def split_hi(act, c, used=None, part=CHUNK):
            c, par = c
            act.wait_ge(S(f"raw_loaded{par}"), (c - par) * 8 + 16)
            if used is not None:
                act.wait_ge(S(used[0]), used[1])
            nc.scalar.activation(WH[par][:, 0:part], raw[par][:, 0:part], ACT.Copy).then_inc(S("w_hi"), 1)

        def split_lo(dve, c, part=CHUNK):
            c, par = c
            dve.wait_ge(S("w_hi"), c + 1)
            nc.vector.tensor_tensor(WL[par][:, 0:part], raw[par][:, 0:part], WH[par][:, 0:part],
                                    ALU.subtract).then_inc(S("w_lo"), 1)

        def chunk_ready(pe, c):
            pe.wait_ge(S("w_hi"), c[0] + 1)
            pe.wait_ge(S("w_lo"), c[0] + 1)

        def wtile(par, row, col, width):
            o = row * width + col
            return WH[par][:, o:o + P], WL[par][:, o:o + P]

        def unit(pe, use, b, ws, xs, tile_ready=None):
            n = use.next(b)
            if not isinstance(n, int) or n > 1:
                pe.wait_ge(S(f"acc_free{b}"), n - 1)
            for k, ((wh, wl), (xh, xl)) in enumerate(zip(ws, xs)):
                if tile_ready:
                    tile_ready(k)
                pe.matmul(bank[b][:], wh, xh, start=(k == 0), stop=False)
                pe.matmul(bank[b][:], wh, xl, start=False, stop=False)
                mm = pe.matmul(bank[b][:], wl, xh, start=False, stop=(k == len(ws) - 1))
            mm.then_inc(S(f"acc_full{b}"), 1)

        def norm_pe(pe, n):
            for kt in range(KT):
                pe.wait_ge(S("sq_ready"), n * KT + kt + 1)
                for t in range(TT):
                    mm = pe.matmul(bank[6][:, t:t + 1], sq[:, kt % 2, t * P:(t + 1) * P], ones1,
                                   start=(kt == 0 and t == 0), stop=(kt == KT - 1 and t == TT - 1),
                                   skip_group_check=True)
                mm.then_inc(S("sq_used"), 1)
            pe.wait_ge(S("rstd_ready"), n + 1)
            for t in range(TT):
                mm = pe.matmul(bank[7][:, t * P:(t + 1) * P], rstd[:, t:t + 1].to_broadcast([P, P]), eye,
                               start=True, stop=True)
            mm.then_inc(S("rstd_spread"), 1)

        def norm_act(act, n, src, tile_ready):
            for kt in range(KT):
                tile_ready(kt)
                if n or kt >= 2:
                    act.wait_ge(S("sq_used"), n * KT + kt - 1)
                nc.scalar.activation(sq[:, kt % 2, :], src[:, kt, :], ACT.Square).then_inc(S("sq_ready"), 1)
            act.wait_ge(S("sq_used"), (n + 1) * KT)
            nc.scalar.activation(root[:, 0:TT], bank[6][:, 0:TT], ACT.Sqrt, bias=epsc[:, 0:1],
                                 scale=1.0 / D).then_inc(S("root_ready"), 1)

        def norm_dve(dve, n):
            dve.wait_ge(S("root_ready"), n + 1)
            nc.vector.reciprocal(rstd[:, 0:TT], root[:, 0:TT]).then_inc(S("rstd_ready"), 1)
            dve.wait_ge(S("rstd_spread"), n + 1)

        def post_act(act, use, n):
            def tile_ready(kt):
                if kt == 0:
                    for b in range(2):
                        act.wait_ge(S(f"acc_free{b}"), use.now(b))
            norm_act(act, n, f, tile_ready)

        def post_dve(dve, n, m, layer, kind):
            norm_dve(dve, n)
            for kt in range(KT):
                if kt >= 2:
                    dve.wait_ge(S("h_ready"), m * KT + kt - 1)
                nc.vector.scalar_tensor_tensor(hn[:, kt % 2, :], f[:, kt, :], gain(layer, kind, kt),
                                               bank[7][:], ALU.mult, ALU.mult).then_inc(S("post_term"), 1)
                dve.wait_ge(S("post_term"), m * KT + kt + 1)
                nc.vector.tensor_tensor(h[:, kt, :], h[:, kt, :], hn[:, kt % 2, :],
                                        ALU.add).then_inc(S("h_ready"), 1)

        def pre_act(act, n, m):
            def tile_ready(kt):
                if m:
                    act.wait_ge(S("h_ready"), (m - 1) * KT + kt + 1)
                elif kt == 0:
                    act.wait_ge(S("x_loaded"), 16)
            norm_act(act, n, h, tile_ready)
            for kt in range(KT):
                act.wait_ge(S("hn_ready"), m * KT + kt + 1)
                nc.scalar.activation(XH[:, kt, :], hn[:, kt % 2, :], ACT.Copy).then_inc(S("x_hi"), 1)

        def pre_dve(dve, n, m, layer, kind):
            norm_dve(dve, n)
            if m:
                dve.wait_ge(S("h_ready"), m * KT)
            for kt in range(KT + 1):
                if kt < KT:
                    if kt >= 2:
                        dve.wait_ge(S("x_lo"), m * KT + kt - 1)
                    nc.vector.scalar_tensor_tensor(hn[:, kt % 2, :], h[:, kt, :], gain(layer, kind, kt),
                                                   bank[7][:], ALU.mult, ALU.mult).then_inc(S("hn_ready"), 1)
                if kt:
                    dve.wait_ge(S("x_hi"), m * KT + kt)
                    nc.vector.tensor_tensor(XL[:, kt - 1, :], hn[:, (kt - 1) % 2, :], XH[:, kt - 1, :],
                                            ALU.subtract).then_inc(S("x_lo"), 1)

        def x_tiles(pe, m):
            def tile_ready(kt):
                pe.wait_ge(S("x_hi"), m * KT + kt + 1)
                pe.wait_ge(S("x_lo"), m * KT + kt + 1)
            return tile_ready

        def x_ready(pe, m):
            x_tiles(pe, m)(KT - 1)

        def add_to_f(dve, use, b, m):
            n = use.next(b)
            dve.wait_ge(S(f"acc_full{b}"), n)
            nc.vector.tensor_tensor(f[:, m, :], f[:, m, :], bank[b][:], ALU.add).then_inc(S(f"acc_free{b}"), 1)

        def ffn_pe(pe, use, c0, m, layer):
            x_ready(pe, m)
            with pe.Fori(0, QUARTERS) as q:
                use.loop(q, [8, 8])
                done = 8 * QUARTERS * layer + 8 * q
                for j in range(8):
                    c = chunk(c0 + j // 2, q, 8)
                    if j % 2 == 0:
                        chunk_ready(pe, c)
                    unit(pe, use, j % 2, [wtile(c[1], kt, j % 2 * P, 2 * P) for kt in range(KT)], X)

                def a_tile(kt):
                    pe.wait_ge(S("a_hi"), done + kt + 1)
                    pe.wait_ge(S("a_lo"), done + kt + 1)
                for j in range(8):
                    c = chunk(c0 + 4 + j // 2, q, 8)
                    if j % 2 == 0:
                        chunk_ready(pe, c)
                    unit(pe, use, j % 2, [wtile(c[1], kt, j % 2 * P, 2 * P) for kt in range(KT)], A,
                         a_tile if j == 0 else None)
            use.end(QUARTERS)

        def ffn_act(act, use, c0, layer):
            with act.Fori(0, QUARTERS) as q:
                use.loop(q, [8, 8])
                done = 8 * QUARTERS * layer + 8 * q
                for j in range(16):
                    if j % 2 == 0:
                        split_hi(act, chunk(c0 + j // 2 + 1, q, 8), ("acc_full1", use.now(1)))
                    b = j % 2
                    n = use.next(b)
                    if j < 8:
                        act.wait_ge(S(f"acc_full{b}"), n)
                        if j >= 2:
                            act.wait_ge(S("a_lo"), done + j - 1)
                        nc.scalar.activation(relu[:, b, :], bank[b][:], ACT.Relu).then_inc(S(f"acc_free{b}"), 1)
                        act.wait_ge(S(f"acc_free{b}"), n)
                        nc.scalar.activation(AH[:, j, :], relu[:, b, :], ACT.Square).then_inc(S("a_hi"), 1)
            use.end(QUARTERS)

        def ffn_dve(dve, use, c0, layer, k):
            dve.wait_ge(S("f_zero"), k + 1)
            with dve.Fori(0, QUARTERS) as q:
                use.loop(q, [8, 8])
                done = 8 * QUARTERS * layer + 8 * q

                for j in range(8):
                    if j % 2 == 0:
                        split_lo(dve, chunk(c0 + j // 2 + 1, q, 8))
                    b = j % 2
                    n = use.next(b)
                    dve.wait_ge(S(f"acc_free{b}"), n)
                    if j >= 2:
                        dve.wait_ge(S("a_lo"), done + j - 1)
                    nc.vector.tensor_tensor(square[:, b, :], relu[:, b, :], relu[:, b, :],
                                            ALU.mult).then_inc(S("a_square"), 1)
                    dve.wait_ge(S("a_square"), done + j + 1)
                    dve.wait_ge(S("a_hi"), done + j + 1)
                    nc.vector.tensor_tensor(AL[:, j, :], square[:, b, :], AH[:, j, :],
                                            ALU.subtract).then_inc(S("a_lo"), 1)
                for j in range(8):
                    if j % 2 == 0:
                        split_lo(dve, chunk(c0 + 4 + j // 2 + 1, q, 8))
                    add_to_f(dve, use, j % 2, j)
            use.end(QUARTERS)

        UNITS = (("r", 0, 0, 0), ("k", 1, 0, 1), ("v", 0, 1, 0), ("ax", 1, 1, 1), ("ag", 0, 2, 0))
        ROWS = (slice(0, C), slice(C, P))

        def in_unit(pe, use, j, c0, i, per, tile_ready=None):
            name, b, k, half = UNITS[j]
            c = chunk(c0 + k, i, per)
            if half == 0:
                chunk_ready(pe, c)
            width = P if name == "ag" else 2 * P
            unit(pe, use, b, [wtile(c[1], kt, half * P, width) for kt in range(KT)], X, tile_ready)

        def in_evac(act, use, j, c0, i, per, pair):
            name, b, k, half = UNITS[j]
            if half == 0:
                split_hi(act, chunk(c0 + k + 1, i, per), ("acc_full1", use.now(1)), CHUNK // 2 if k == 1 else CHUNK)
            n = use.next(b)
            act.wait_ge(S(f"acc_full{b}"), n)
            if not (isinstance(pair, int) and pair == 0):
                act.wait_ge(*nth({"r": "r_mixed", "k": "k_mixed", "v": "v_mixed", "ax": "lru_in",
                                  "ag": "gelu"}[name], pair))
            dst = {"r": Ur[:, 1:], "k": Uk[:, 1:], "v": Uv[:, 1:], "ax": Uax[:, 3:], "ag": Uag[:]}[name]
            nc.scalar.activation(dst, bank[b][:], ACT.Copy).then_inc(S(f"acc_free{b}"), 1)

        def in_split(dve, j, c0, i, per):
            name, b, k, half = UNITS[j]
            if half == 0:
                split_lo(dve, chunk(c0 + k + 1, i, per), CHUNK // 2 if k == 1 else CHUNK)

        def by_chunk(pe, b, terms, signal, add=False):
            pe.sem_inc(S("waits_passed"), 1)
            for c in range(NCH):
                cols = slice(c * C, (c + 1) * C)
                for rows in ROWS:
                    for k, (lhsT, rhs) in enumerate(terms):
                        rh = rhs[rows, :] if rhs is eye2 else rhs[rows, cols]
                        mm = pe.matmul(bank[b][rows, cols], lhsT[rows, cols], rh,
                                       start=(k == 0), stop=(k == len(terms) - 1))
            mm.then_inc(S(signal), 1)

        def head_sums(pe, b, src, signal):
            for t in range(TT):
                mm = pe.matmul(bank[b][:, 2 * t:2 * t + 2], src[:, t * P:(t + 1) * P], head1,
                               start=(t == 0), stop=(t == TT - 1), skip_group_check=True)
            mm.then_inc(S(signal), 1)

        def head_spread(pe, b, src, signal):
            for t in range(TT):
                for j, rows in enumerate(ROWS):
                    mm = pe.matmul(bank[b][rows, t * P:(t + 1) * P],
                                   src[:, 2 * t + j:2 * t + j + 1].to_broadcast([P, C]), eye,
                                   start=True, stop=True)
            mm.then_inc(S(signal), 1)

        def pair_pe(pe, use, p, out_c, in_c=None):
            n = p + 1

            def fill(j):
                if in_c is not None:
                    in_unit(pe, use, j, in_c[0], in_c[1], in_c[2])

            def need(*names):
                for name in names:
                    pe.wait_ge(*nth(name, n))

            pe.wait_ge(S("pp_ready"), n)
            pe.wait_ge(S("lora_ready"), 2)
            pe.matmul(bank[2][:], pp[0:C, P_W2A2:P_W2A2 + P], lora[0:C, :], start=True, stop=True).then_inc(S("lin_w"), 1)
            pe.matmul(bank[3][:], pp[C:P, P_W2A2:P_W2A2 + P], lora[C:P, :], start=True, stop=True).then_inc(S("lin_a"), 1)
            pe.matmul(bank[4][:], pp[:, P_G2:P_G2 + P], gate_in[:], start=True, stop=True).then_inc(S("lin_g"), 1)
            need("kk_sq")
            head_sums(pe, 5, W[7], "kk_sum")
            fill(0)
            need("kk_inv")
            head_spread(pe, 6, kkinv, "kk_spread")
            need("z_ready", "decay_rate", "iclr", "g_out")
            by_chunk(pe, 4, [(W[5], eye2)], "z_turned")
            need("b_ready")
            by_chunk(pe, 2, [(W[6], W[5])], "azb_t")
            by_chunk(pe, 3, [(W[5], W[6])], "azb")
            need("kk_ready")
            by_chunk(pe, 5, [(W[6], eye2)], "b_turned")
            need("kd_ready")
            by_chunk(pe, 6, [(W[7], eye2)], "k_turned")
            need("v_mixed")
            by_chunk(pe, 7, [(W[2], eye2)], "v_turned")
            need("z_by_token")
            by_chunk(pe, 4, [(W[7], W[5])], "azk_t")
            need("b_by_token", "rd_ready")
            by_chunk(pe, 5, [(W[6], Rd)], "arb_t")
            need("k_by_token")
            by_chunk(pe, 6, [(W[7], Rd)], "ark_t")
            need("v_by_token", "rk_ready")
            pe.matmul(bank[7][:], heads, W[3][:], start=True, stop=True).then_inc(S("rk_sum"), 1)
            need("nt", "nn", "o32t", "o32", "o64")
            by_chunk(pe, 2, [(W[0], W[1])], "m2")
            by_chunk(pe, 3, [(W[1], W[0])], "m2_t")
            need("azk", "bonus")
            by_chunk(pe, 7, [(W[8], Vt)], "x2")
            fill(1)
            need("m2_s", "m2_ts", "e1")
            by_chunk(pe, 2, [(W[10], W[9])], "m4")
            by_chunk(pe, 3, [(W[9], W[10])], "m4_t")
            by_chunk(pe, 4, [(W[9], W[4])], "e2")
            fill(2)
            need("m4_s", "m4_ts", "e2_s")
            by_chunk(pe, 3, [(W[11], W[5])], "e4")
            by_chunk(pe, 2, [(W[3], W[11])], "m8")
            need("lru_in", "ark", "x2_s")
            pe.wait_ge(S("gate_blocks"), 4 * n)
            pe.matmul(bank[6][:], BDa[:], lax[:], start=True, stop=True).then_inc(S("gate_r"), 1)
            pe.matmul(bank[7][:], BDx[:], lax[:], start=True, stop=True).then_inc(S("gate_i"), 1)
            need("m8_s", "e4_s")
            by_chunk(pe, 4, [(W[6], W[7])], "e8")
            fill(3)
            need("dt_s")
            by_chunk(pe, 2, [(W[0], eye2)], "dd")
            by_chunk(pe, 3, [(O32, W[0])], "y32")
            fill(4)
            need("dd_s")
            by_chunk(pe, 4, [(O32T, W[1])], "x32")
            need("y32_s", "arb")
            by_chunk(pe, 5, [(W[1], W[9])], "t32_t")
            need("x32_s", "lru_gates")
            by_chunk(pe, 6, [(W[0], W[10])], "t32")
            need("t32_ts")
            by_chunk(pe, 2, [(O64, W[11])], "y64")
            need("t32_s", "y64_s")
            by_chunk(pe, 3, [(W[3], W[5])], "tt")
            need("tt_s")
            by_chunk(pe, 4, [(W[6], Zt)], "w1")
            by_chunk(pe, 5, [(W[6], X2)], "w2")
            need("w1_s")
            by_chunk(pe, 7, [(W[7], Bt)], "gg")
            by_chunk(pe, 6, [(W[7], ARB)], "qq")
            need("w2_s", "g_s", "q_s")
            pe.sem_inc(S("waits_passed"), 1)
            for c in range(NCH):
                cols = slice(c * C, (c + 1) * C)
                prev = slice((c - 1) * C, c * C)
                if c < NCH - 1:
                    for rows in ROWS:
                        pe.matmul(bank[3 + c % 2][rows, cols], Bt[rows, cols], W[9][rows, cols], start=True, stop=False)
                        mm = pe.matmul(bank[3 + c % 2][rows, cols], Kt[rows, cols], Vt[rows, cols], start=False, stop=(c == 0))
                    if c == 0:
                        mm.then_inc(S("state_full"), 1)
                for rows in ROWS:
                    pe.matmul(bank[2][rows, cols], W[9][rows, cols], ARB[rows, cols], start=True, stop=False)
                    mm = pe.matmul(bank[2][rows, cols], Vt[rows, cols], ARK[rows, cols], start=False, stop=(c == 0))
                if c:
                    pe.wait_ge(S("state"), (NCH - 1) * p + c)
                    pe.sem_inc(S("waits_passed"), 1)
                    if c < NCH - 1:
                        for rows in ROWS:
                            mm = pe.matmul(bank[3 + c % 2][rows, cols], W[11][rows, cols], W[3][rows, prev],
                                           start=False, stop=True)
                        mm.then_inc(S("state_full"), 1)
                    for rows in ROWS:
                        mm = pe.matmul(bank[2][rows, cols], W[3][rows, prev], W[10][rows, cols],
                                       start=False, stop=True)
            mm.then_inc(S("y_heads"), 1)
            need("ys")
            pe.matmul(bank[4][:], heads, W[0][:], start=True, stop=True).then_inc(S("y_sum"), 1)
            need("yc_sq")
            head_sums(pe, 5, W[5], "y_var")
            need("ln_inv")
            head_spread(pe, 6, lninv, "ln_spread")
            c = chunk(*out_c)
            chunk_ready(pe, c)
            Y = [(yH[:, k, :], yL[:, k, :]) for k in range(2)]

            def y_tile(k):
                need(*(("ya_hi", "ya_lo") if k == 0 else ("yb_hi", "yb_lo")))
            for m in range(KT):
                unit(pe, use, m % 2, [wtile(c[1], k, m * P, D) for k in range(2)], Y, y_tile if m == 0 else None)

        def pair_act(act, use, p, out_c, in_c=None):
            n = p + 1

            def need(*names):
                for name in names:
                    act.wait_ge(*nth(name, n))

            def evac(name, dst, b, ready, func=ACT.Copy, **kw):
                need(name)
                nc.scalar.activation(dst[:], bank[b][:], func, **kw).then_inc(S(ready), 1)

            def fill(j):
                if in_c is not None:
                    in_evac(act, use, j, *in_c, p + 1)

            need("pp_ready", "k_mixed")
            nc.scalar.activation(W[7][:], W[1][:], ACT.Square, scale=pv(Q_KK)).then_inc(S("kk_sq"), 1)
            evac("lin_w", W[3], 2, "decay_rate", ACT.Sigmoid, bias=pv(Q_W0))
            evac("lin_a", W[4], 3, "iclr", ACT.Sigmoid, bias=pv(Q_A0))
            evac("lin_g", gout, 4, "g_out")
            need("kk_floor")
            nc.scalar.activation(kkroot[:], kkm[:], ACT.Sqrt).then_inc(S("kk_root"), 1)
            need("cumlog")
            nc.scalar.activation(W[8][:], W[5][:], ACT.Exp, scale=-EXP_HALF).then_inc(S("dec"), 1)
            nc.scalar.activation(W[9][:], W[5][:], ACT.Exp, scale=EXP_HALF).then_inc(S("dec_inv"), 1)
            need("cumlog_before")
            nc.scalar.activation(W[10][:], W[6][:], ACT.Exp, scale=-EXP_HALF).then_inc(S("dec_before"), 1)
            fill(0)
            evac("z_turned", Zt, 4, "z_by_token")
            evac("b_turned", Bt, 5, "b_by_token")
            evac("k_turned", Kt, 6, "k_by_token")
            evac("v_turned", Vt, 7, "v_by_token")
            evac("m2", W[9], 2, "m2_s")
            evac("x2", X2, 7, "x2_s")
            fill(1)
            evac("m4", W[11], 2, "m4_s")
            fill(2)
            need("e4")
            evac("m8", W[6], 2, "m8_s")
            evac("gate_r", lra, 6, "lru_r", ACT.Sigmoid, bias=pv(Q_BA))
            evac("gate_i", lix, 7, "lru_gates", ACT.Sigmoid, bias=pv(Q_BX))
            fill(3)
            need("lru_r")
            nc.scalar.activation(ldr[:], lra[:], ACT.Tanh, scale=sp[:, 10, bass.ds(p, 1)]).then_inc(S("lru_tanh"), 1)
            need("lru_tanh")
            nc.scalar.activation(lra[:], lra[:], ACT.Exp, scale=sp[:, 11, bass.ds(p, 1)]).then_inc(S("lru_a"), 1)
            evac("dd", W[1], 2, "dd_s")
            evac("y32", W[9], 3, "y32_s")
            nc.scalar.activation(ldr[:], ldr[:], ACT.Sqrt).then_inc(S("lru_root"), 1)
            nc.scalar.activation(lgate[:], Uag[:], ACT.Gelu_apprx_tanh).then_inc(S("gelu"), 1)
            fill(4)
            evac("x32", W[10], 4, "x32_s")
            evac("y64", W[5], 2, "y64_s")
            evac("w1", W[7], 4, "w1_s")
            need("ya_ready")
            nc.scalar.activation(yH[:, 0, :], lix[:], ACT.Copy).then_inc(S("ya_hi"), 1)
            evac("y_heads", W[0], 2, "ys")
            need("yc")
            nc.scalar.activation(W[5][:], W[1][:], ACT.Square).then_inc(S("yc_sq"), 1)
            need("y_var")
            nc.scalar.activation(lnroot[:], bank[5][:, 0:8], ACT.Sqrt, bias=epsc[:, 1:2],
                                 scale=1.0 / C).then_inc(S("ln_root"), 1)
            need("yb_ready")
            nc.scalar.activation(yH[:, 1, :], W[7][:], ACT.Copy).then_inc(S("yb_hi"), 1)
            c, i, per = out_c
            split_hi(act, chunk(c + 1, i, per), ("acc_full0", use.now(0)))
            for m in range(KT):
                use.next(m % 2)

        def pair_dve(dve, use, p, out_c, in_c=None):
            n = p + 1

            def need(*names):
                for name in names:
                    dve.wait_ge(*nth(name, n))

            def fill(j):
                if in_c is not None:
                    in_split(dve, j, *in_c)
                    use.next(UNITS[j][1])

            def add(dst, a, b, name, ready):
                need(name)
                nc.vector.tensor_tensor(dst[:], a[:], bank[b][:], ALU.add).then_inc(S(ready), 1)

            def masked(dst, b, k, name, ready):
                need(name)
                nc.vector.tensor_tensor(chunked(dst), chunked(bank[b]), table(k), ALU.mult).then_inc(S(ready), 1)

            def conv(k):
                taps = Uax[:, k:k + T]
                if k == 0:
                    nc.vector.tensor_scalar(lax[:], taps, pv(Q_CW), pv(Q_CB), ALU.mult, ALU.add).then_inc(S("conv"), 1)
                    return
                dve.wait_ge(S("conv"), 3 * p + k)
                nc.vector.scalar_tensor_tensor(lax[:], taps, pv(Q_CW + k), lax[:], ALU.mult,
                                               ALU.add).then_inc(S("lru_in" if k == 3 else "conv"), 1)

            need("pp_ready")
            dve.wait_ge(S("blocks_zero"), 2)
            for dst, k in ((BDa, P_WA), (BDx, P_WX)):
                for j, rows in enumerate(ROWS):
                    nc.vector.tensor_copy(dst[rows, j * C:(j + 1) * C],
                                          pp[rows, k:k + C]).then_inc(S("gate_blocks"), 1)
            mixes = ((Uk, W[1], Q_MUK, "k_mixed"), (Ur, W[0], Q_MUR, "r_mixed"), (Uv, W[2], Q_MUV, "v_mixed"))
            for j, (U, dst, mu, name) in enumerate(mixes):
                if j:
                    need(mixes[j - 1][3])
                nc.vector.tensor_tensor(mixdiff[:], U[:, 0:T], U[:, 1:T + 1], ALU.subtract).then_inc(S("mix_diff"), 1)
                dve.wait_ge(S("mix_diff"), 3 * p + j + 1)
                nc.vector.scalar_tensor_tensor(dst[:], mixdiff[:], pv(mu), U[:, 1:T + 1], ALU.mult,
                                               ALU.add).then_inc(S(name), 1)
            need("kk_sum")
            nc.vector.tensor_scalar(kkm[:], bank[5][:, 0:8], 1e-24, None, ALU.max).then_inc(S("kk_floor"), 1)
            need("decay_rate")
            nc.vector.tensor_tensor_scan(W[5][:], cst[:, K_RESET:K_RESET + T], W[3][:], 0.0, ALU.mult,
                                         ALU.add).then_inc(S("cumlog"), 1)
            need("cumlog")
            nc.vector.tensor_tensor(W[6][:], W[5][:], W[3][:], ALU.subtract).then_inc(S("cumlog_before"), 1)
            need("kk_root")
            nc.vector.reciprocal(kkinv[:], kkroot[:]).then_inc(S("kk_inv"), 1)
            need("iclr")
            nc.vector.tensor_scalar(X2[:], W[4][:], -1.0, pv(Q_KA), ALU.add, ALU.mult).then_inc(S("k_factor"), 1)
            need("k_factor")
            nc.vector.scalar_tensor_tensor(X2[:], X2[:], 1.0, W[1][:], ALU.add, ALU.mult).then_inc(S("k_new"), 1)
            need("kk_spread")
            nc.vector.scalar_tensor_tensor(W[11][:], W[1][:], pv(Q_KK), bank[6][:], ALU.mult,
                                           ALU.mult).then_inc(S("kk_ready"), 1)
            need("kk_ready", "dec_before")
            nc.vector.scalar_tensor_tensor(W[5][:], W[11][:], -1.0, W[10][:], ALU.mult,
                                           ALU.mult).then_inc(S("z_ready"), 1)
            nc.vector.tensor_tensor(mixdiff[:], W[11][:], W[4][:], ALU.mult).then_inc(S("b_plain"), 1)
            need("b_plain")
            nc.vector.tensor_tensor(W[6][:], mixdiff[:], W[9][:], ALU.mult).then_inc(S("b_ready"), 1)
            need("k_new")
            nc.vector.tensor_tensor(W[7][:], X2[:], W[9][:], ALU.mult).then_inc(S("kd_ready"), 1)
            nc.vector.tensor_tensor(Rd[:], W[0][:], W[8][:], ALU.mult).then_inc(S("rd_ready"), 1)
            need("cumlog_before")
            nc.vector.scalar_tensor_tensor(W[3][:], W[0][:], pv(Q_RK), X2[:], ALU.mult,
                                           ALU.mult).then_inc(S("rk_ready"), 1)
            nc.vector.tensor_copy(PC[:], chunked(W[8])[:, :, C - 1]).then_inc(S("pc_ready"), 1)
            fill(0)
            need("rk_ready")
            masked(W[0], 2, K_D16T, "azb_t", "nt")
            masked(O32T, 2, K_O32T, "azb_t", "o32t")
            need("k_new", "kk_ready")
            masked(W[1], 3, K_D16, "azb", "nn")
            masked(O32, 3, K_O32, "azb", "o32")
            masked(O64, 3, K_O64, "azb", "o64")
            need("nt", "b_plain")
            nc.vector.tensor_tensor(chunked(W[4]), chunked(W[0]), table(K_EYE2), ALU.add).then_inc(S("e1"), 1)
            need("pc_ready", "rd_ready")
            masked(W[8], 4, K_LT, "azk_t", "azk")
            masked(ARB, 5, K_LE, "arb_t", "arb")
            masked(ARK, 6, K_LE, "ark_t", "ark")
            need("rk_sum")
            nc.vector.tensor_tensor(bonus[:], W[2][:], bank[7][:], ALU.mult).then_inc(S("bonus"), 1)
            need("z_ready")
            need("m2_t")
            nc.vector.tensor_copy(W[10][:], bank[3][:]).then_inc(S("m2_ts"), 1)
            fill(1)
            for k in range(4):
                conv(k)
            need("m4_t")
            nc.vector.tensor_copy(W[3][:], bank[3][:]).then_inc(S("m4_ts"), 1)
            need("e1")
            add(W[5], W[4], 4, "e2", "e2_s")
            fill(2)
            need("e2_s")
            add(W[7], W[5], 3, "e4", "e4_s")
            need("e4_s")
            add(W[0], W[7], 4, "e8", "dt_s")
            fill(3)
            need("lru_gates", "lru_in")
            nc.vector.tensor_tensor(lix[:], lix[:], lax[:], ALU.mult).then_inc(S("lru_iu"), 1)
            need("lru_a", "lru_root")
            nc.vector.scalar_tensor_tensor(ldr[:], lra[:], 1.0, ldr[:], ALU.add, ALU.mult).then_inc(S("lru_scale"), 1)
            fill(4)
            need("dt_s")
            add(W[11], W[0], 5, "t32_t", "t32_ts")
            need("lru_scale", "lru_iu")
            nc.vector.tensor_tensor(ldr[:], ldr[:], lix[:], ALU.mult).then_inc(S("lru_drive"), 1)
            need("dd_s")
            add(W[3], W[1], 6, "t32", "t32_s")
            need("lru_drive")
            nc.vector.tensor_tensor_scan(lix[:], lra[:], ldr[:], 0.0, ALU.mult, ALU.add).then_inc(S("lru_h"), 1)
            need("t32_ts")
            add(W[6], W[11], 3, "tt", "tt_s")
            need("lru_h", "gelu")
            nc.vector.tensor_tensor(lix[:], lix[:], lgate[:], ALU.mult).then_inc(S("ya_ready"), 1)
            need("w2")
            nc.vector.tensor_copy(W[9][:], bank[5][:]).then_inc(S("w2_s"), 1)
            need("t32_ts", "gg", "tt_s")
            nc.vector.tensor_tensor(chunked(W[11]), chunked(bank[7]), table(K_EYE2), ALU.add).then_inc(S("g_s"), 1)
            need("rd_ready")
            add(W[10], Rd, 6, "qq", "q_s")
            need("ya_hi", "ya_ready")
            nc.vector.tensor_tensor(yL[:, 0, :], lix[:], yH[:, 0, :], ALU.subtract).then_inc(S("ya_lo"), 1)
            for c in range(NCH - 1):
                cols = slice(c * C, (c + 1) * C)
                dve.wait_ge(S("state_full"), (NCH - 1) * p + c + 1)
                nc.vector.tensor_scalar(W[3][:, cols], bank[3 + c % 2][:, cols], PC[:, c:c + 1], None,
                                        ALU.mult).then_inc(S("state"), 1)
            need("ys", "y_sum")
            nc.vector.scalar_tensor_tensor(W[1][:], bank[4][:], -1.0 / C, W[0][:], ALU.mult,
                                           ALU.add).then_inc(S("yc"), 1)
            need("ln_root")
            nc.vector.reciprocal(lninv[:], lnroot[:]).then_inc(S("ln_inv"), 1)
            need("ln_spread", "yc")
            nc.vector.tensor_tensor(W[6][:], W[1][:], bank[6][:], ALU.mult).then_inc(S("yn"), 1)
            need("yn")
            nc.vector.tensor_scalar(W[6][:], W[6][:], pv(Q_LNW), pv(Q_LNB), ALU.mult, ALU.add).then_inc(S("y_affine"), 1)
            need("y_affine", "bonus")
            nc.vector.tensor_tensor(W[6][:], W[6][:], bonus[:], ALU.add).then_inc(S("y_bonus"), 1)
            need("y_bonus", "g_out")
            nc.vector.tensor_tensor(W[7][:], W[6][:], gout[:], ALU.mult).then_inc(S("yb_ready"), 1)
            need("yb_ready", "yb_hi")
            nc.vector.tensor_tensor(yL[:, 1, :], W[7][:], yH[:, 1, :], ALU.subtract).then_inc(S("yb_lo"), 1)
            c, i, per = out_c
            split_lo(dve, chunk(c + 1, i, per))
            dve.wait_ge(S("f_zero"), 1)
            for m in range(KT):
                add_to_f(dve, use, m % 2, m)

        def mixers_ab(eng, use, pair):
            turns = PAIRS - 1
            with eng.Fori(0, turns) as p:
                use.loop(p, [7, 6])
                pair(eng, use, p, (AB_TURN + 3, p, AB_TURN), (AB_TURN, p, AB_TURN))
            use.end(turns)
            pair(eng, use, turns, (AB_TURN + AB_TURN * turns, 0, 0))

        def ret_pe(pe, use, m):
            x_ready(pe, m)
            with pe.Fori(0, RET_HEADS) as hd:
                use.loop(hd, [8, 8])
                n4 = 4 * hd
                for k in range(2):
                    c = chunk(RET_CHUNK0 + k, hd, 8)
                    chunk_ready(pe, c)
                    for j in range(2):
                        unit(pe, use, j, [wtile(c[1], kt, j * P, 2 * P) for kt in range(KT)], X)
                pe.wait_ge(S("y_gated"), n4)
                for half in range(2):
                    c = chunk(RET_CHUNK0 + 2 + half, hd, 8)
                    chunk_ready(pe, c)
                    for k in range(4):
                        kt = half * 4 + k
                        wh, wl = (w[c[1]][:, k * T:(k + 1) * T] for w in (WH, WL))
                        for t in range(TT):
                            tok = slice(t * P, (t + 1) * P)
                            pe.matmul(bank[2 + t][:], XH[:, kt, tok], wh, start=(kt == 0), stop=False)
                            pe.matmul(bank[2 + t][:], XH[:, kt, tok], wl, start=False, stop=False)
                            mm = pe.matmul(bank[2 + t][:], XL[:, kt, tok], wh, start=False, stop=(kt == KT - 1))
                    mm.then_inc(S("v_part"), 1)
                for E in range(4):
                    c = chunk(RET_CHUNK0 + 4 + E // 2, hd, 8)
                    if E % 2 == 0:
                        chunk_ready(pe, c)
                    unit(pe, use, E % 2, [wtile(c[1], kt, E % 2 * P, 2 * P) for kt in range(KT)], X)
                pe.wait_ge(S("qk_rotated"), n4 + 4)
                pe.wait_ge(S("v_out_act"), 2 * hd + 2)
                pe.wait_ge(S("v_out_dve"), 2 * hd + 2)
                for J in range(TT):
                    for k in range(2):
                        mm = pe.matmul(bank[2 + J][:, 0:T - J * P], kr[:, k, J * P:(J + 1) * P], qr[:, k, J * P:],
                                       start=(k == 0), stop=(k == 1))
                    mm.then_inc(S("scores"), 1)
                for E in range(4):
                    for J in range(TT):
                        if E == 0:
                            pe.wait_ge(S("decayed"), n4 + J + 1)
                        mm = pe.matmul(bank[2 + E][:, J * P:], Vr[:, J, E * P:(E + 1) * P], Sc[:, J, 0:T - J * P],
                                       start=(J == 0), stop=(J == TT - 1), skip_group_check=True)
                    mm.then_inc(S("y_full"), 1)
                for E in range(4):
                    pe.wait_ge(S("ysq_ready"), n4 + E + 1)
                    for t in range(TT):
                        mm = pe.matmul(bank[6][:, t:t + 1], sq[:, E % 2, t * P:(t + 1) * P], ones1,
                                       start=(E == 0 and t == 0), stop=(E == 3 and t == TT - 1),
                                       skip_group_check=True)
                    mm.then_inc(S("ysq_used"), 1)
                pe.wait_ge(S("y_inv"), hd + 1)
                for t in range(TT):
                    mm = pe.matmul(bank[7][:, t * P:(t + 1) * P], rstd[:, t:t + 1].to_broadcast([P, P]), eye,
                                   start=True, stop=True)
                mm.then_inc(S("y_spread"), 1)

                def b_tile(k):
                    pe.wait_ge(S("y_hi"), n4 + k + 1)
                    pe.wait_ge(S("y_lo"), n4 + k + 1)
                for j in range(KT):
                    c = chunk(RET_CHUNK0 + 6 + j // 4, hd, 8)
                    if j % 4 == 0:
                        chunk_ready(pe, c)
                    unit(pe, use, j % 2, [wtile(c[1], k, j % 4 * P, T) for k in range(4)],
                         [(BH[:, k, :], BL[:, k, :]) for k in range(4)], b_tile if j == 0 else None)
            use.end(RET_HEADS)

        def ret_act(act, use):
            with act.Fori(0, RET_HEADS) as hd:
                use.loop(hd, [8, 8])
                n4 = 4 * hd
                for k in range(2):
                    split_hi(act, chunk(RET_CHUNK0 + k + 1, hd, 8), ("acc_full1", use.now(1)))
                    use.next(0), use.next(1)
                split_hi(act, chunk(RET_CHUNK0 + 3, hd, 8), ("acc_full1", use.now(1)))
                split_hi(act, chunk(RET_CHUNK0 + 4, hd, 8), ("v_part", 2 * hd + 1))
                act.wait_ge(S("v_part"), 2 * hd + 2)
                for t in range(2):
                    nc.scalar.activation(Vr[:, t, :], bank[2 + t][:], ACT.Copy).then_inc(S("v_out_act"), 1)
                for E in range(4):
                    if E == 0:
                        split_hi(act, chunk(RET_CHUNK0 + 5, hd, 8), ("v_part", 2 * hd + 2))
                    if E == 2:
                        split_hi(act, chunk(RET_CHUNK0 + 6, hd, 8), ("acc_full1", use.now(1)))
                    n = use.next(E % 2)
                    act.wait_ge(S(f"acc_full{E % 2}"), n)
                    act.wait_ge(S("y_gated"), n4)
                    nc.scalar.activation(sg[:, E, :], bank[E % 2][:], ACT.Silu).then_inc(S(f"acc_free{E % 2}"), 1)
                for E in range(4):
                    act.wait_ge(S("y_full"), n4 + E + 1)
                    if E >= 2:
                        act.wait_ge(S("ysq_used"), n4 + E - 1)
                    nc.scalar.activation(sq[:, E % 2, :], bank[2 + E][:], ACT.Square).then_inc(S("ysq_ready"), 1)
                act.wait_ge(S("ysq_used"), n4 + 4)
                nc.scalar.activation(root[:, 0:TT], bank[6][:, 0:TT], ACT.Sqrt, bias=epsc[:, 0:1],
                                     scale=1.0 / RET_DV).then_inc(S("y_root"), 1)
                for E in range(4):
                    act.wait_ge(S("y_ready"), n4 + E + 1)
                    nc.scalar.activation(BH[:, E, :], yv[:, E, :], ACT.Copy).then_inc(S("y_hi"), 1)
                for half in range(2):
                    split_hi(act, chunk(RET_CHUNK0 + 7 + half, hd, 8), ("acc_full1", use.now(1)))
                    for j in range(4):
                        use.next(j % 2)
            use.end(RET_HEADS)

        def ret_dve(dve, use, k_zero):
            cos, sin = rc[:, R_COS:R_COS + T], rc[:, R_SIN:R_SIN + T]
            dve.wait_ge(S("rc_loaded"), 16)
            with dve.Fori(0, RET_HEADS) as hd:
                use.loop(hd, [8, 8])
                n4 = 4 * hd
                for k, dst in ((0, qr), (1, kr)):
                    split_lo(dve, chunk(RET_CHUNK0 + k + 1, hd, 8))
                    n0, n1 = use.next(0), use.next(1)
                    dve.wait_ge(S("acc_full0"), n0)
                    dve.wait_ge(S("acc_full1"), n1)
                    dve.wait_ge(S("qk_rotated"), n4 + 2 * k)
                    nc.vector.tensor_tensor(rt[:, 0, :], bank[0][:], cos, ALU.mult)
                    nc.vector.tensor_tensor(rt[:, 1, :], bank[1][:], sin, ALU.mult)
                    nc.vector.tensor_tensor(rt[:, 2, :], bank[1][:], cos, ALU.mult).then_inc(S("acc_free1"), 1)
                    nc.vector.tensor_tensor(rt[:, 3, :], bank[0][:], sin, ALU.mult).then_inc(S("acc_free0"), 1)
                    dve.wait_ge(S("acc_free1"), n1)
                    dve.wait_ge(S("acc_free0"), n0)
                    nc.vector.tensor_tensor(dst[:, 0, :], rt[:, 0, :], rt[:, 1, :], ALU.subtract).then_inc(S("qk_rotated"), 1)
                    nc.vector.tensor_tensor(dst[:, 1, :], rt[:, 2, :], rt[:, 3, :], ALU.add).then_inc(S("qk_rotated"), 1)
                split_lo(dve, chunk(RET_CHUNK0 + 3, hd, 8))
                split_lo(dve, chunk(RET_CHUNK0 + 4, hd, 8))
                dve.wait_ge(S("v_part"), 2 * hd + 2)
                for t in range(2, 4):
                    nc.vector.tensor_copy(Vr[:, t, :], bank[2 + t][:]).then_inc(S("v_out_dve"), 1)
                split_lo(dve, chunk(RET_CHUNK0 + 5, hd, 8))
                split_lo(dve, chunk(RET_CHUNK0 + 6, hd, 8))
                for E in range(4):
                    n = use.next(E % 2)
                for J in range(TT):
                    dve.wait_ge(S("scores"), n4 + J + 1)
                    nc.vector.tensor_tensor(Sc[:, J, 0:T - J * P], bank[2 + J][:, 0:T - J * P],
                                            rc[:, bass.ds(R_DECAY + T * hd, T - J * P)],
                                            ALU.mult).then_inc(S("decayed"), 1)
                for E in range(4):
                    dve.wait_ge(S("ysq_ready"), n4 + E + 1)
                    if E < 2:
                        dve.wait_ge(S(f"acc_free{E}"), use.now(E))
                    nc.vector.tensor_tensor(yv[:, E, :], bank[2 + E][:], sg[:, E, :], ALU.mult).then_inc(S("y_gated"), 1)
                dve.wait_ge(S("y_root"), hd + 1)
                nc.vector.reciprocal(rstd[:, 0:TT], root[:, 0:TT]).then_inc(S("y_inv"), 1)
                dve.wait_ge(S("y_spread"), hd + 1)
                dve.wait_ge(S("y_gated"), n4 + 4)
                for E in range(5):
                    if E < 4:
                        nc.vector.tensor_tensor(yv[:, E, :], yv[:, E, :], bank[7][:], ALU.mult).then_inc(S("y_ready"), 1)
                    if E:
                        dve.wait_ge(S("y_hi"), n4 + E)
                        nc.vector.tensor_tensor(BL[:, E - 1, :], yv[:, E - 1, :], BH[:, E - 1, :],
                                                ALU.subtract).then_inc(S("y_lo"), 1)
                dve.wait_ge(S("f_zero"), k_zero + 1)
                for half in range(2):
                    split_lo(dve, chunk(RET_CHUNK0 + 7 + half, hd, 8))
                    for j in range(4):
                        add_to_f(dve, use, j % 2, half * 4 + j)
            use.end(RET_HEADS)

        block = ctx.enter_context(nc.Block())

        @block.sync
        def _(sync):
            sync.dma_start(cst[:], const).then_inc(S("const_loaded"), 16)
            sync.dma_start(vec[:], vectors).then_inc(S("vec_loaded"), 16)
            sync.dma_start(h[:], x.rearrange("(k p) t -> p k t", p=P)).then_inc(S("x_loaded"), 16)
            for c in range(2):
                sync.dma_start(raw[c][:], weights[c]).then_inc(S(f"raw_loaded{c}"), 16)
            with sync.Fori(0, ALL_CHUNKS // 2) as i:
                for c in range(2):
                    sync.wait_ge(S("w_lo"), 2 * i + c + 1)
                    sync.dma_start(raw[c][:], weights[bass.ds(2 * i + (2 + c), 1)].rearrange(
                        "a p c -> (a p) c")).then_inc(S(f"raw_loaded{c}"), 16)
            for kt in range(KT):
                sync.wait_ge(S("h_ready"), 3 * KT + kt + 1)
                sync.dma_start(out[kt * P:(kt + 1) * P, :], h[:, kt, :]).then_inc(S("out_stored"), 16)
            sync.wait_ge(S("out_stored"), 16 * KT)
            for c in range(2):
                sync.wait_ge(S(f"raw_loaded{c}"), 16 * (ALL_CHUNKS // 2 + 1))

        @block.gpsimd
        def _(pool):
            nc.gpsimd.memset(epsc[:, 0:1], EPS).then_inc(S("eps"), 1)
            nc.gpsimd.memset(epsc[:, 1:2], LN_EPS).then_inc(S("eps"), 1)
            for U, w in ((Ur, 1), (Uk, 1), (Uv, 1), (Uax, 3)):
                nc.gpsimd.memset(U[:, 0:w], 0.0).then_inc(S("edge_zero"), 1)
            nc.gpsimd.memset(BDa[:], 0.0).then_inc(S("blocks_zero"), 1)
            nc.gpsimd.memset(BDx[:], 0.0).then_inc(S("blocks_zero"), 1)
            nc.gpsimd.memset(f[:], 0.0).then_inc(S("f_zero"), 1)
            pool.wait_ge(S("f_zero"), 1)
            pool.dma_start(stage[:], pairs[0]).then_inc(S("stage_loaded"), 16)

            def take_pair(p, later):
                pool.wait_ge(S("stage_loaded"), 16 * p + 16)
                if later:
                    pool.wait_ge(*nth("y_affine", p))
                    pool.wait_ge(*nth("lru_gates", p))
                    pool.wait_ge(*nth("g_out", p))
                pool.sem_inc(S("waits_passed"), 1)
                nc.gpsimd.tensor_copy(pp[:], stage[:]).then_inc(S("pp_ready"), 1)
                pool.wait_ge(S("pp_ready"), p + 1)

            take_pair(0, False)
            with pool.Fori(1, PAIRS) as p:
                pool.dma_start(stage[:], pairs[bass.ds(p, 1)].rearrange("a p c -> (a p) c")).then_inc(S("stage_loaded"), 16)
                take_pair(p, True)
            pool.wait_ge(S("h_ready"), KT)
            nc.gpsimd.memset(f[:], 0.0).then_inc(S("f_zero"), 1)
            pool.dma_start(rc[:], ret_const).then_inc(S("rc_loaded"), 16)
            for k in range(2, 4):
                pool.wait_ge(S("h_ready"), k * KT)
                nc.gpsimd.memset(f[:], 0.0).then_inc(S("f_zero"), 1)
            pool.wait_ge(S("f_zero"), 4)

        @block.tensor
        def _(pe):
            use = Turns(2)
            pe.wait_ge(S("vec_loaded"), 16)
            pe.wait_ge(S("const_loaded"), 16)
            pe.wait_ge(S("ones_ready"), 1)
            norm_pe(pe, 0)
            tiles = x_tiles(pe, 0)
            for j in range(2):
                if j == 0:
                    chunk_ready(pe, chunk(0))
                unit(pe, use, j, [wtile(0, kt, j * P, 2 * P) for kt in range(KT)], X, tiles if j == 0 else None)
            for j in range(5):
                in_unit(pe, use, j, 1, 0, 0)
            mixers_ab(pe, use, pair_pe)
            norm_pe(pe, 1)
            norm_pe(pe, 2)
            ffn_pe(pe, use, FFN0_CHUNK, 1, 0)
            norm_pe(pe, 3)
            norm_pe(pe, 4)
            ret_pe(pe, use, 2)
            norm_pe(pe, 5)
            norm_pe(pe, 6)
            ffn_pe(pe, use, FFN1_CHUNK, 3, 1)
            norm_pe(pe, 7)

        @block.scalar
        def _(act):
            use = Turns(2)
            act.wait_ge(S("eps"), 2)
            act.wait_ge(S("vec_loaded"), 16)
            act.wait_ge(S("const_loaded"), 16)
            act.wait_ge(S("sp_abs"), 1)
            nc.scalar.activation(sp[:, 2, :], sp[:, 1, :], ACT.Exp, scale=-1.0).then_inc(S("sp_exp"), 1)
            pre_act(act, 0, 0)
            split_hi(act, chunk(0))
            split_hi(act, chunk(1))
            act.wait_ge(S("edge_zero"), 4)
            for j, U in enumerate((Ur, Uk)):
                n = use.next(j)
                act.wait_ge(S(f"acc_full{j}"), n)
                nc.scalar.activation(U[:, 1:], bank[j][:], ACT.Copy).then_inc(S(f"acc_free{j}"), 1)
            act.wait_ge(S("lora_mixed"), 2)
            nc.scalar.activation(lora[0:C, :], lora[0:C, :], ACT.Tanh).then_inc(S("lora_ready"), 1)
            nc.scalar.activation(gate_in[:], gate_in[:], ACT.Sigmoid).then_inc(S("lora_ready"), 1)
            for j in range(5):
                in_evac(act, use, j, 1, 0, 0, 0)
            mixers_ab(act, use, pair_act)
            post_act(act, use, 1)
            pre_act(act, 2, 1)
            ffn_act(act, use, FFN0_CHUNK, 0)
            post_act(act, use, 3)
            pre_act(act, 4, 2)
            ret_act(act, use)
            post_act(act, use, 5)
            pre_act(act, 6, 3)
            ffn_act(act, use, FFN1_CHUNK, 1)
            post_act(act, use, 7)

        @block.vector
        def _(dve):
            use = Turns(2)
            V = nc.vector
            dve.wait_ge(S("vec_loaded"), 16)
            dve.wait_ge(S("const_loaded"), 16)
            V.memset(ones1, 1.0).then_inc(S("ones_ready"), 1)
            lam = vec[:, V_LAM:V_LAM + PAIRS]
            V.tensor_scalar(sp[:, 0, :], lam, -1.0, 0.0, ALU.mult, ALU.max).then_inc(S("sp_max"), 1)
            V.scalar_tensor_tensor(sp[:, 1, :], lam, -1.0, lam, ALU.mult, ALU.max).then_inc(S("sp_abs"), 1)
            steps = [0]

            def step(ins):
                ins.then_inc(S("sp_step"), 1)
                steps[0] += 1
                dve.wait_ge(S("sp_step"), steps[0])
            dve.wait_ge(S("sp_exp"), 1)
            step(V.tensor_scalar(sp[:, 3, :], sp[:, 2, :], 2.0, None, ALU.add))
            step(V.reciprocal(sp[:, 4, :], sp[:, 3, :]))
            step(V.tensor_tensor(sp[:, 5, :], sp[:, 4, :], sp[:, 2, :], ALU.mult))
            step(V.tensor_tensor(sp[:, 6, :], sp[:, 5, :], sp[:, 5, :], ALU.mult))
            step(V.tensor_scalar(sp[:, 7, :], sp[:, 6, :], 1.0 / 15, None, ALU.mult))
            for k in (13, 11, 9, 7, 5, 3):
                step(V.scalar_tensor_tensor(sp[:, 7, :], sp[:, 7, :], 1.0 / k, sp[:, 6, :], ALU.add, ALU.mult))
            step(V.scalar_tensor_tensor(sp[:, 8, :], sp[:, 7, :], 1.0, sp[:, 5, :], ALU.add, ALU.mult))
            dve.wait_ge(S("sp_max"), 1)
            step(V.scalar_tensor_tensor(sp[:, 9, :], sp[:, 8, :], 2.0, sp[:, 0, :], ALU.mult, ALU.add))
            step(V.tensor_scalar(sp[:, 10, :], sp[:, 9, :], LRU_C / 2, None, ALU.mult))
            step(V.tensor_scalar(sp[:, 11, :], sp[:, 9, :], -LRU_C, None, ALU.mult))

            pre_dve(dve, 0, 0, 0, 0)
            split_lo(dve, chunk(0))
            split_lo(dve, chunk(1))
            for j, (U, dst) in enumerate(((Ur, lora), (Uk, gate_in))):
                n = use.next(j)
                dve.wait_ge(S(f"acc_free{j}"), n)
                if j:
                    dve.wait_ge(S("lora_mixed"), 1)
                V.tensor_tensor(mixdiff[:], U[:, 0:T], U[:, 1:T + 1], ALU.subtract).then_inc(S("lora_diff"), 1)
                dve.wait_ge(S("lora_diff"), j + 1)
                V.scalar_tensor_tensor(dst[:], mixdiff[:], vec[:, V_MU_LORA + j:V_MU_LORA + j + 1], U[:, 1:T + 1],
                                       ALU.mult, ALU.add).then_inc(S("lora_mixed"), 1)
            dve.wait_ge(S("lora_mixed"), 2)
            for j in range(5):
                in_split(dve, j, 1, 0, 0)
                use.next(UNITS[j][1])
            for b in range(2):
                dve.wait_ge(S(f"acc_free{b}"), use.now(b))
            mixers_ab(dve, use, pair_dve)
            post_dve(dve, 1, 0, 0, 1)
            pre_dve(dve, 2, 1, 0, 2)
            ffn_dve(dve, use, FFN0_CHUNK, 0, 1)
            post_dve(dve, 3, 1, 0, 3)
            pre_dve(dve, 4, 2, 1, 0)
            ret_dve(dve, use, 2)
            post_dve(dve, 5, 2, 1, 1)
            pre_dve(dve, 6, 3, 1, 2)
            ffn_dve(dve, use, FFN1_CHUNK, 1, 3)
            post_dve(dve, 7, 3, 1, 3)


def tile_rows(w, rows, cols):
    part = w[rows, cols]
    k = part.shape[0] // P
    return part.reshape(k, P, part.shape[1]).transpose(1, 0, 2).reshape(P, -1)


def weight_stream(a):
    s = lambda at, n: slice(at, at + n)
    every = slice(None)
    ab_in, ab_out = a["ab_w_in"][0], a["ab_w_out"][0]
    W2 = D // 2
    chunks = [tile_rows(ab_in, every, s(2 * W2 + 3 * W2, 2 * P))]

    def pair_in(p):
        col = {"ax": p * P, "ag": W2 + p * P, "r": 2 * W2 + p * P, "k": 3 * W2 + p * P, "v": 4 * W2 + p * P}
        for one, two in (("r", "k"), ("v", "ax")):
            both = np.concatenate([ab_in[:, s(col[one], P)], ab_in[:, s(col[two], P)]], axis=1)
            chunks.append(tile_rows(both, every, every))
        ag = tile_rows(ab_in, every, s(col["ag"], P))
        chunks.append(np.concatenate([ag, ag], axis=1))

    def pair_out(p):
        rows = np.concatenate([ab_out[s(p * P, P)], ab_out[s(W2 + p * P, P)]], axis=0)
        chunks.append(tile_rows(rows, every, every))

    pair_in(0)
    for p in range(PAIRS):
        if p + 1 < PAIRS:
            pair_in(p + 1)
        pair_out(p)

    def mlp(layer):
        w1, w2 = a["ffn_w_in"][layer], a["ffn_w_out"][layer]
        for q in range(QUARTERS):
            for j in range(4):
                chunks.append(tile_rows(w1, every, s(q * D + j * 2 * P, 2 * P)))
            for j in range(4):
                chunks.append(tile_rows(w2, s(q * D, D), s(j * 2 * P, 2 * P)))

    mlp(0)
    r_in, r_out = a["ret_w_in"][0], a["ret_w_out"][0]
    for hd in range(RET_HEADS):
        chunks.append(tile_rows(r_in, every, s(hd * 2 * P, 2 * P)))
        chunks.append(tile_rows(r_in, every, s(D + hd * 2 * P, 2 * P)))
        for half in range(2):
            chunks.append(tile_rows(r_in, s(half * D // 2, D // 2), s(2 * D + hd * T, T)))
        for half in range(2):
            chunks.append(tile_rows(r_in, every, s(4 * D + hd * T + half * 2 * P, 2 * P)))
        for half in range(2):
            chunks.append(tile_rows(r_out, s(hd * T, T), s(half * T, T)))
    mlp(1)
    while len(chunks) < 2 * (ALL_CHUNKS // 2) + 2:
        chunks.append(chunks[-1])
    return np.stack(chunks)


def pair_tables(a):
    out = []
    for p in range(PAIRS):
        s = slice(p * P, (p + 1) * P)
        mu = a["rwkv_mu"][0]
        W2 = D // 2
        columns = [a["rwkv_w0"][0][s], a["rwkv_a0"][0][s], a["rwkv_k_k"][0][s], a["rwkv_k_a"][0][s],
                   a["rwkv_r_k"][0][s], a["rwkv_ln_w"][0][s], a["rwkv_ln_b"][0][s],
                   *(a["lru_conv_w"][0][i][s] for i in range(4)), a["lru_conv_b"][0][s],
                   a["lru_ba"][0][s], a["lru_bx"][0][s]]
        columns = [mu[i * W2:(i + 1) * W2][s] for i in range(3)] + columns
        out.append(np.concatenate(
            [np.concatenate([a["rwkv_w2"][0][:, s], a["rwkv_a2"][0][:, s]], axis=0), a["rwkv_g2"][0][:, s],
             a["lru_wa"][0][2 * p:2 * p + 2].reshape(P, C), a["lru_wx"][0][2 * p:2 * p + 2].reshape(P, C),
             np.stack(columns, axis=1)], axis=1))
    return np.stack(out)


def vector_table(a):
    norms = np.stack([a[k] for k in ("norm_mix_pre", "norm_mix_post", "norm_ffn_pre", "norm_ffn_post")], axis=1)
    norms = norms.reshape(2 * 4 * KT, P).T
    mu = a["rwkv_mu"][0][3 * D // 2:].reshape(2, P).T
    lam = a["lru_lambda"][0].reshape(PAIRS, P).T
    return np.concatenate([norms, mu, lam, lam[:, 0:1]], axis=1)


def kernel(**inputs):
    import concourse.bacc as bacc
    from concourse.bass_utils import run_bass_kernel_spmd

    a = {k: np.asarray(v) for k, v in inputs.items()}
    const, ret_const = constants()
    arrays = {
        "x_fm": np.ascontiguousarray(a["x"][0].T),
        "weights": np.ascontiguousarray(weight_stream(a)),
        "pairs": np.ascontiguousarray(pair_tables(a)),
        "vectors": np.ascontiguousarray(vector_table(a)),
        "const": const,
        "ret_const": ret_const,
    }
    nc = bacc.Bacc("TRN2", target_bir_lowering=False, num_devices=1)
    args = [nc.dram_tensor(k, v.shape, F32, kind="ExternalInput").ap() for k, v in arrays.items()]
    out = nc.dram_tensor("out_fm", (D, T), F32, kind="ExternalOutput").ap()
    trunk_kernel(nc, *args, out)
    r = run_bass_kernel_spmd(nc, [arrays], core_ids=[0])
    return np.ascontiguousarray(r.results[0]["out_fm"].T)[None]
```

```python
from contextlib import ExitStack

import numpy as np

import concourse.bass as bass
from concourse import mybir

F32 = mybir.dt.float32
F32R = mybir.dt.float32r
ALU = mybir.AluOpType
ACT = mybir.ActivationFunctionType

P = 128
D = 1024
T = 512
KT = D // P
TT = T // P
FF = 4 * D
EPS = 1e-6
C = 64
NCH = T // C
PAIRS = 4
LRU_C = 8.0
LN_EPS = 64e-5
EXP_HALF = float(np.exp(-0.5))
RET_HEADS = 4
RET_DV = 512
CHUNK = 2048
QUARTERS = 4

AB_CHUNK = 0
AB_TURN = 4
FFN0_CHUNK = AB_CHUNK + 1 + AB_TURN * PAIRS
RET_CHUNK0 = FFN0_CHUNK + 8 * QUARTERS
FFN1_CHUNK = RET_CHUNK0 + 8 * RET_HEADS
ALL_CHUNKS = FFN1_CHUNK + 8 * QUARTERS

V_NORM = 0
V_MU_LORA = 2 * 4 * KT
V_LAM = V_MU_LORA + 2
V_ONE = V_LAM + PAIRS
NVEC = V_ONE + 1

P_W2A2, P_G2, P_WA, P_WX, P_VEC = 0, 128, 256, 320, 384
(Q_MUR, Q_MUK, Q_MUV, Q_W0, Q_A0, Q_KK, Q_KA, Q_RK, Q_LNW, Q_LNB, Q_CW, _, _, _, Q_CB, Q_BA,
 Q_BX) = range(P_VEC, P_VEC + 17)
NPAIR = P_VEC + 17

K_EYE, K_EYE2, K_HEAD1, K_HEADS = 0, 128, 192, 194
K_D16T, K_O32T, K_D16, K_O32, K_O64, K_LT, K_LE = (322 + 64 * i for i in range(7))
K_RESET = 322 + 64 * 7
NCONST = K_RESET + T
R_COS, R_SIN, R_DECAY = 0, T, 2 * T
NRET = 2 * T + RET_HEADS * T


SERIES = {
    "low_rank_products": "lin_w lin_a lin_g",
    "turned_products": "z_turned b_turned k_turned v_turned",
    "chunk_products": "azb_t azb azk_t arb_t ark_t",
    "power_products": "m2 m2_t m4 m4_t e2 e4 m8 e8",
    "gate_products": "gate_r gate_i",
    "inverse_products": "dd y32 x32 t32_t t32 y64 tt",
    "solved_products": "w1 w2 gg qq",
    "head_statistics": "kk_sum kk_spread y_sum y_var ln_spread",
    "low_rank_factors": "decay_rate iclr g_out",
    "decay_powers": "dec dec_inv dec_before",
    "vectors_by_token": "z_by_token b_by_token k_by_token v_by_token",
    "copied_by_act": "m2_s x2_s m4_s m8_s dd_s y32_s x32_s y64_s w1_s",
    "lru_factors": "lru_r lru_gates lru_tanh lru_a lru_root gelu",
    "masked_products": "nt o32t nn o32 o64 e1 azk arb ark",
    "summed_by_dve": "m2_ts m4_ts e2_s e4_s dt_s t32_ts t32_s tt_s w2_s g_s q_s",
    "chunk_vectors": "kk_ready z_ready b_plain b_ready kd_ready rd_ready rk_ready pc_ready",
    "lru_steps": "lru_iu lru_scale lru_drive lru_h ya_ready",
    "head_outputs": "yc ln_inv yn y_affine y_bonus yb_ready",
}
SERIES_OF = {name: (group, k, len(names.split())) for group, names in SERIES.items()
             for k, name in enumerate(names.split())}


def constants():
    c = np.zeros((P, NCONST), np.float32)
    row, col = np.arange(P)[:, None] % C, np.arange(C)[None, :]
    c[:, K_EYE:K_EYE + P] = np.eye(P)
    c[:, K_EYE2:K_EYE2 + C] = row == col
    head = np.arange(P) // C
    c[:, K_HEAD1:K_HEAD1 + 2] = head[:, None] == np.arange(2)[None, :]
    c[:, K_HEADS:K_HEADS + P] = head[:, None] == head[None, :]
    for at, r, k in ((K_D16T, col, row), (K_D16, row, col)):
        c[:, at:at + C] = (r > k) & (r // 16 == k // 16)
    for at, r, k in ((K_O32T, col, row), (K_O32, row, col)):
        c[:, at:at + C] = (r > k) & (r // 16 != k // 16) & (r // 32 == k // 32)
    c[:, K_O64:K_O64 + C] = (row > col) & (row // 32 != col // 32)
    c[:, K_LT:K_LT + C] = row < col
    c[:, K_LE:K_LE + C] = row <= col
    c[:, K_RESET:] = np.arange(T)[None, :] % C != 0
    r = np.zeros((P, NRET), np.float32)
    inv = (1.0 / (np.float32(10000.0) ** (np.arange(P, dtype=np.float32) / P))).astype(np.float32)
    ang = (inv[:, None] * np.arange(T, dtype=np.float32)[None, :]).astype(np.float32).astype(np.float64)
    r[:, R_COS:R_COS + T] = np.cos(ang)
    r[:, R_SIN:R_SIN + T] = np.sin(ang)
    rel = np.arange(T)[None, :] - np.arange(P)[:, None]
    for h in range(RET_HEADS):
        decay = np.exp(np.log1p(-2.0 ** (-5.0 - h)) * np.maximum(rel, 0)) / 16.0
        r[:, R_DECAY + h * T:R_DECAY + (h + 1) * T] = np.where(rel >= 0, decay, 0.0)
    return c, r


class Turns:

    def __init__(self, kinds):
        self.n = [0] * kinds
        self.per = [0] * kinds
        self.turn = 0

    def loop(self, turn, per):
        self.turn, self.per = turn, per

    def end(self, turns):
        self.n = [n + (turns - 1) * p for n, p in zip(self.n, self.per)]
        self.loop(0, [0] * len(self.n))

    def next(self, kind):
        self.n[kind] += 1
        return self.now(kind)

    def now(self, kind):
        return self.n[kind] + self.turn * self.per[kind] if self.per[kind] else self.n[kind]


def trunk_kernel(nc, x, weights, pairs, vectors, const, ret_const, out):
    with ExitStack() as ctx:
        def sb(name, cols, dt=F32):
            return ctx.enter_context(nc.sbuf_tensor(name, [P] + (cols if isinstance(cols, list) else [cols]), dt))

        sems = {}

        def S(name):
            name = SERIES_OF.get(name, (name,))[0]
            if name not in sems:
                sems[name] = ctx.enter_context(nc.semaphore(name))
            return sems[name]

        def nth(name, n):
            if name not in SERIES_OF:
                return S(name), n
            _, place, size = SERIES_OF[name]
            return S(name), (n - 1) * size + place + 1

        h = sb("h", [KT, T])
        f = sb("f", [KT, T])
        XH = sb("XH", [KT, T], F32R)
        XL = sb("XL", [KT, T], F32R)
        raw = [sb(f"raw{i}", CHUNK) for i in range(2)]
        WH = [sb(f"WH{i}", CHUNK, F32R) for i in range(2)]
        WL = [sb(f"WL{i}", CHUNK, F32R) for i in range(2)]
        cst = sb("cst", NCONST)
        vec = sb("vec", NVEC)
        root = sb("root", 8)
        rstd = sb("rstd", 8)
        epsc = sb("epsc", 2)
        sp = sb("sp", [12, PAIRS])


        ARENA = 90 * 1024
        start = (nc.sbuf_base + 31) // 32 * 32
        sb("arena", ARENA // 4 + 8)

        class Place:

            def __init__(self):
                self.at = start

            def __call__(self, name, cols, dt=F32):
                cols = cols if isinstance(cols, list) else [cols]
                t = nc.alloc_sbuf_tensor_at(name, [P] + cols, dt, offset=self.at)
                self.at += (int(np.prod(cols)) * 4 + 31) // 32 * 32
                assert self.at <= start + ARENA, (name, self.at - start)
                return t

        norm = Place()
        sq, hn, sq_sum = norm("sq", [2, T]), norm("hn", [2, T]), norm("sq_sum", T)
        NORM = norm.at
        ab = Place()
        W = [ab(f"W{i}", T) for i in range(12)]
        yH, yL = ab("yH", [2, T], F32R), ab("yL", [2, T], F32R)
        Ur, Uk, Uv = (ab(n, T + 1) for n in ("Ur", "Uk", "Uv"))
        Uax, Uag = ab("Uax", T + 3), ab("Uag", T)
        lora, gate_in = ab("lora", T), ab("gate_in", T)
        stage, pp = ab("stage", NPAIR), ab("pp", NPAIR)
        BDa, BDx = ab("BDa", P), ab("BDx", P)
        mixdiff = ab("mixdiff", T)
        bonus, gout, Rd = (ab(n, T) for n in ("bonus", "gout", "Rd"))
        Zt, Bt, Kt, Vt, ARB, ARK, X2 = (ab(n, T) for n in ("Zt", "Bt", "Kt", "Vt", "ARB", "ARK", "X2"))
        O32T, O32, O64 = (ab(n, T) for n in ("O32T", "O32", "O64"))
        lax, lra, lix, ldr, lgate = (ab(n, T) for n in ("lax", "lra", "lix", "ldr", "lgate"))
        kkm, kkroot, kkinv, lnroot, lninv, PC = (ab(n, 8) for n in
                                                 ("kkm", "kkroot", "kkinv", "lnroot", "lninv", "PC"))
        ffn = Place()
        ffn.at = NORM
        AH, AL = ffn("AH", [KT, T], F32R), ffn("AL", [KT, T], F32R)
        relu, squared = ffn("relu", [2, T]), ffn("squared", [2, T])
        re = Place()
        re.at = NORM
        BH, BL = re("BH", [4, T], F32R), re("BL", [4, T], F32R)
        qr, kr = re("qr", [2, T]), re("kr", [2, T])
        Vr, Sc = re("Vr", [TT, T]), re("Sc", [TT, T])
        rc = re("rc", NRET)
        sg, rt, yv = re("sg", [4, T]), re("rt", [4, T]), re("yv", [4, T])

        bank = [ctx.enter_context(nc.psum_tensor(f"bank{i}", [P, T], F32)) for i in range(8)]

        eye = cst[:, K_EYE:K_EYE + P]
        eye2 = cst[:, K_EYE2:K_EYE2 + C]
        heads = cst[:, K_HEADS:K_HEADS + P]
        head1 = cst[:, K_HEAD1:K_HEAD1 + 2]
        ones1 = vec[:, NVEC - 1:NVEC]
        X = [(XH[:, kt, :], XL[:, kt, :]) for kt in range(KT)]
        A = [(AH[:, kt, :], AL[:, kt, :]) for kt in range(KT)]

        def chunked(t):
            return t[:].rearrange("p (c t) -> p c t", t=C)

        def table(k):
            return cst[:, k:k + C][:, None, :].to_broadcast([P, NCH, C])

        def gain(layer, kind, kt):
            i = V_NORM + (layer * 4 + kind) * KT + kt
            return vec[:, i:i + 1]

        def pv(q):
            return pp[:, q:q + 1]

        def chunk(c, i=0, per=0):
            return (c + per * i if per else c), c % 2

        def split_hi(act, c, part=CHUNK, waits=True):
            c, par = c
            act.wait_ge(S(f"raw_loaded{par}"), (c - par) * 8 + 16)
            if waits and (not isinstance(c, int) or c >= 2):
                act.wait_ge(S("chunk_begun"), c)
            nc.scalar.activation(WH[par][:, 0:part], raw[par][:, 0:part], ACT.Copy).then_inc(S("w_hi"), 1)

        def split_lo(dve, c, part=CHUNK):
            c, par = c
            dve.wait_ge(S("w_hi"), c + 1)
            nc.vector.tensor_tensor(WL[par][:, 0:part], raw[par][:, 0:part], WH[par][:, 0:part],
                                    ALU.subtract).then_inc(S("w_lo"), 1)

        def chunk_ready(pe, c):
            pe.wait_ge(S("w_hi"), c[0] + 1)
            pe.wait_ge(S("w_lo"), c[0] + 1)

        def wtile(par, row, col, width):
            o = row * width + col
            return WH[par][:, o:o + P], WL[par][:, o:o + P]

        def units(pe, use, banks, ws, xs, begins=False, tile_ready=None):
            for b in banks:
                n = use.next(b)
                if not isinstance(n, int) or n > 1:
                    pe.wait_ge(S(f"acc_free{b}"), n - 1)
            sums(pe, banks, ws, xs, None, begins, tile_ready)

        def sums(pe, banks, ws, xs, signal=None, begins=False, tile_ready=None):
            for k, (xh, xl) in enumerate(xs):
                if tile_ready:
                    tile_ready(k)
                for b, w in zip(banks, ws):
                    wh, wl = w[k]
                    mm = pe.matmul(bank[b][:], wh, xh, start=(k == 0), stop=False)
                    if begins and k == 0 and b == banks[0]:
                        mm.then_inc(S("chunk_begun"), 1)
                    pe.matmul(bank[b][:], wh, xl, start=False, stop=False)
                    mm = pe.matmul(bank[b][:], wl, xh, start=False, stop=(k == len(xs) - 1))
                    if k == len(xs) - 1:
                        mm.then_inc(S(signal or f"acc_full{b}"), 1)

        def sums_before(n):
            return n // 2 * (KT + 1) + n % 2 * KT

        def sum_by_token(pe, src, first, last):
            for t in range(TT):
                mm = pe.matmul(bank[6][:, t:t + 1], src[:, t * P:(t + 1) * P], ones1,
                               start=(first and t == 0), stop=(last and t == TT - 1), skip_group_check=True)
            return mm

        def spread_rstd(pe, n):
            pe.wait_ge(S("rstd_ready"), n + 1)
            for t in range(TT):
                mm = pe.matmul(bank[7][:, t * P:(t + 1) * P], rstd[:, t:t + 1].to_broadcast([P, P]), eye,
                               start=True, stop=True)
            mm.then_inc(S("rstd_spread"), 1)

        def input_norm_pe(pe, n):
            for kt in range(KT):
                pe.wait_ge(S("sq_ready"), n * KT + kt + 1)
                sum_by_token(pe, sq[:, kt % 2, :], kt == 0, kt == KT - 1).then_inc(S("sq_used"), 1)
            spread_rstd(pe, n)

        def output_norm_pe(pe, n):
            pe.wait_ge(S("sq_summed"), (n + 1) // 2 * (KT - 2))
            sum_by_token(pe, sq_sum[:], True, False)
            pe.wait_ge(S("sq_ready"), n * KT + KT)
            sum_by_token(pe, sq[:, (KT - 1) % 2, :], False, True).then_inc(S("sq_used"), 1)
            spread_rstd(pe, n)

        def output_norm_pool(pool, n):
            for kt in range(1, KT - 1):
                pool.wait_ge(S("sq_ready"), n * KT + kt + 1)
                done = n // 2 * (KT - 2) + kt - 1
                if done:
                    pool.wait_ge(S("sq_summed"), done)
                nc.gpsimd.tensor_tensor(sq_sum[:], sq[:, 0, :] if kt == 1 else sq_sum[:], sq[:, kt % 2, :],
                                        ALU.add).then_inc(S("sq_summed"), 1)

        def square(act, n, src, kt):
            if kt >= 2 and n % 2:
                act.wait_ge(S("sq_summed"), n // 2 * (KT - 2) + max(kt - 2, 1))
            elif kt >= 2:
                act.wait_ge(S("sq_used"), sums_before(n) + kt - 1)
            nc.scalar.activation(sq[:, kt % 2, :], src[:, kt, :], ACT.Square).then_inc(S("sq_ready"), 1)

        def root_mean(act, n):
            act.wait_ge(S("sq_used"), sums_before(n + 1))
            nc.scalar.activation(root[:, 0:TT], bank[6][:, 0:TT], ACT.Sqrt, bias=epsc[:, 0:1],
                                 scale=1.0 / D).then_inc(S("root_ready"), 1)

        def norm_dve(dve, n):
            dve.wait_ge(S("root_ready"), n + 1)
            nc.vector.reciprocal(rstd[:, 0:TT], root[:, 0:TT]).then_inc(S("rstd_ready"), 1)
            dve.wait_ge(S("rstd_spread"), n + 1)

        def square_f(act, n, kt, use, b):
            act.wait_ge(S(f"acc_free{b}"), use.now(b))
            square(act, n, f, kt)

        def h_is_ready(eng, m, kt):
            eng.wait_ge(S("h_odd" if kt % 2 else "h_even"), m * KT // 2 + kt // 2 + 1)

        def add_to_h(ops, kt):
            ops.tensor_tensor(h[:, kt, :], h[:, kt, :], hn[:, kt % 2, :],
                              ALU.add).then_inc(S("h_odd" if kt % 2 else "h_even"), 1)

        def residual_dve(dve, n, m, layer, kind):
            norm_dve(dve, n)
            for kt in range(KT + 1):
                if kt < KT:
                    if kt >= 2:
                        h_is_ready(dve, m, kt - 2)
                    nc.vector.scalar_tensor_tensor(hn[:, kt % 2, :], f[:, kt, :], gain(layer, kind, kt),
                                                   bank[7][:], ALU.mult, ALU.mult).then_inc(S("post_term"), 1)
                if kt % 2:
                    dve.wait_ge(S("post_term"), m * KT + kt)
                    add_to_h(nc.vector, kt - 1)

        def residual_pool(pool, m):
            for kt in range(1, KT, 2):
                pool.wait_ge(S("post_term"), m * KT + kt + 1)
                add_to_h(nc.gpsimd, kt)

        def second_chunk_act(act, c):
            split_hi(act, chunk(c + 1), waits=False)

        def pre_act(act, n, m):
            for kt in range(KT):
                if m:
                    h_is_ready(act, m - 1, kt)
                elif kt % 4 == 0:
                    act.wait_ge(S(f"x_loaded{kt // 4}"), 16)
                square(act, n, h, kt)
            root_mean(act, n)
            for kt in range(KT):
                act.wait_ge(S("hn_ready"), m * KT + kt + 1)
                nc.scalar.activation(XH[:, kt, :], hn[:, kt % 2, :], ACT.Copy).then_inc(S("x_hi"), 1)

        def x_low(eng, ops, m, kt):
            eng.wait_ge(S("x_hi"), m * KT + kt + 1)
            ops.tensor_tensor(XL[:, kt, :], hn[:, kt % 2, :], XH[:, kt, :],
                              ALU.subtract).then_inc(S(f"x_lo{kt % 2}"), 1)

        def pre_dve(dve, n, m, layer, kind):
            norm_dve(dve, n)
            if m:
                h_is_ready(dve, m - 1, KT - 1)
            for kt in range(KT + 1):
                if kt < KT:
                    if kt >= 2:
                        dve.wait_ge(S(f"x_lo{kt % 2}"), m * KT // 2 + kt // 2)
                    nc.vector.scalar_tensor_tensor(hn[:, kt % 2, :], h[:, kt, :], gain(layer, kind, kt),
                                                   bank[7][:], ALU.mult, ALU.mult).then_inc(S("hn_ready"), 1)
                if kt % 2:
                    x_low(dve, nc.vector, m, kt - 1)

        def pre_pool(pool, m):
            for kt in range(1, KT, 2):
                x_low(pool, nc.gpsimd, m, kt)

        def x_tiles(pe, m):
            def tile_ready(kt):
                pe.wait_ge(S("x_hi"), m * KT + kt + 1)
                pe.wait_ge(S(f"x_lo{kt % 2}"), m * KT // 2 + kt // 2 + 1)
            return tile_ready

        def add_to_f(dve, use, b, m):
            n = use.next(b)
            dve.wait_ge(S(f"acc_full{b}"), n)
            nc.vector.tensor_tensor(f[:, m, :], f[:, m, :], bank[b][:], ALU.add).then_inc(S(f"acc_free{b}"), 1)

        ACCS = 4

        def turns_then_last(eng, use, per, turns, body):
            with eng.Fori(0, turns - 1) as i:
                use.loop(i, per)
                body(i, False)
            use.end(turns - 1)
            body(turns - 1, True)

        def ffn_pe(pe, use, c0, m, layer, n):
            def quarter(q, last):
                done = 8 * QUARTERS * layer + 8 * q

                def a_tile(kt):
                    pe.wait_ge(S("a_hi"), done + kt + 1)
                    pe.wait_ge(S("a_lo"), done + kt + 1)
                for j in range(0, 16, 2):
                    c = chunk(c0 + j // 2, q, 8)
                    chunk_ready(pe, c)
                    ws = [[wtile(c[1], kt, k * P, 2 * P) for kt in range(KT)] for k in range(2)]
                    banks = [j % ACCS, (j + 1) % ACCS]
                    if j == 0:
                        units(pe, use, banks, ws, X, True, x_tiles(pe, m))
                        continue
                    for k in range(2):
                        units(pe, use, banks[k:k + 1], ws[k:k + 1], X if j < 8 else A, k == 0,
                              a_tile if j == 8 and k == 0 else None)
                if last:
                    output_norm_pe(pe, n)
            turns_then_last(pe, use, [4] * ACCS, QUARTERS, quarter)

        def ffn_act(act, use, c0, layer, n):
            def quarter(q, last):
                done = 8 * QUARTERS * layer + 8 * q
                for j in range(16):
                    if j and j % 2 == 0:
                        split_hi(act, chunk(c0 + j // 2 + 1, q, 8))
                    b = j % ACCS
                    u = use.next(b)
                    if j < 8:
                        act.wait_ge(S(f"acc_full{b}"), u)
                        if j >= 2:
                            act.wait_ge(S("a_lo"), done + j - 1)
                        nc.scalar.activation(relu[:, j % 2, :], bank[b][:], ACT.Relu).then_inc(S(f"acc_free{b}"), 1)
                        act.wait_ge(S(f"acc_free{b}"), u)
                        nc.scalar.activation(AH[:, j, :], relu[:, j % 2, :], ACT.Square).then_inc(S("a_hi"), 1)
                    elif last:
                        square_f(act, n, j - 8, use, b)
                if last:
                    root_mean(act, n)
                else:
                    split_hi(act, chunk(c0 + 9, q, 8))
            turns_then_last(act, use, [4] * ACCS, QUARTERS, quarter)

        def ffn_dve(dve, use, c0, layer, k):
            dve.wait_ge(S("f_zero"), k + 1)

            def quarter(q, last):
                done = 8 * QUARTERS * layer + 8 * q
                for j in range(16):
                    if j and j % 2 == 0:
                        split_lo(dve, chunk(c0 + j // 2 + 1, q, 8))
                    b = j % ACCS
                    if j >= 8:
                        add_to_f(dve, use, b, j - 8)
                        continue
                    u = use.next(b)
                    dve.wait_ge(S(f"acc_free{b}"), u)
                    if j >= 2:
                        dve.wait_ge(S("a_lo"), done + j - 1)
                    nc.vector.tensor_tensor(squared[:, j % 2, :], relu[:, j % 2, :], relu[:, j % 2, :],
                                            ALU.mult).then_inc(S("a_square"), 1)
                    dve.wait_ge(S("a_square"), done + j + 1)
                    dve.wait_ge(S("a_hi"), done + j + 1)
                    nc.vector.tensor_tensor(AL[:, j, :], squared[:, j % 2, :], AH[:, j, :],
                                            ALU.subtract).then_inc(S("a_lo"), 1)
                if not last:
                    split_lo(dve, chunk(c0 + 9, q, 8))
            turns_then_last(dve, use, [4] * ACCS, QUARTERS, quarter)

        UNITS = (("r", 0, 0, 0), ("k", 1, 0, 1), ("v", 0, 1, 0), ("ax", 1, 1, 1), ("ag", 0, 2, 0))
        ROWS = (slice(0, C), slice(C, P))

        def in_unit(pe, use, j, c0, i, per, tile_ready=None):
            name, b, k, half = UNITS[j]
            c = chunk(c0 + k, i, per)
            if half == 0:
                chunk_ready(pe, c)
            width = P if name == "ag" else 2 * P
            units(pe, use, [b], [[wtile(c[1], kt, half * P, width) for kt in range(KT)]], X, half == 0, tile_ready)

        def in_evac(act, use, j, c0, i, per, pair):
            name, b, k, half = UNITS[j]
            if half == 0:
                split_hi(act, chunk(c0 + k + 1, i, per), CHUNK // 2 if k == 1 else CHUNK)
            n = use.next(b)
            act.wait_ge(S(f"acc_full{b}"), n)
            if not (isinstance(pair, int) and pair == 0):
                act.wait_ge(*nth({"r": "r_mixed", "k": "k_mixed", "v": "v_mixed", "ax": "lru_in",
                                  "ag": "gelu"}[name], pair))
            dst = {"r": Ur[:, 1:], "k": Uk[:, 1:], "v": Uv[:, 1:], "ax": Uax[:, 3:], "ag": Uag[:]}[name]
            nc.scalar.activation(dst, bank[b][:], ACT.Copy).then_inc(S(f"acc_free{b}"), 1)

        def in_split(dve, j, c0, i, per):
            name, b, k, half = UNITS[j]
            if half == 0:
                split_lo(dve, chunk(c0 + k + 1, i, per), CHUNK // 2 if k == 1 else CHUNK)

        def by_chunk(pe, b, terms, signal, add=False):
            pe.sem_inc(S("waits_passed"), 1)
            for c in range(NCH):
                cols = slice(c * C, (c + 1) * C)
                for rows in ROWS:
                    for k, (lhsT, rhs) in enumerate(terms):
                        rh = rhs[rows, :] if rhs is eye2 else rhs[rows, cols]
                        mm = pe.matmul(bank[b][rows, cols], lhsT[rows, cols], rh,
                                       start=(k == 0), stop=(k == len(terms) - 1))
            mm.then_inc(S(signal), 1)

        def head_sums(pe, b, src, signal):
            for t in range(TT):
                mm = pe.matmul(bank[b][:, 2 * t:2 * t + 2], src[:, t * P:(t + 1) * P], head1,
                               start=(t == 0), stop=(t == TT - 1), skip_group_check=True)
            mm.then_inc(S(signal), 1)

        def head_spread(pe, b, src, signal):
            for t in range(TT):
                for j, rows in enumerate(ROWS):
                    mm = pe.matmul(bank[b][rows, t * P:(t + 1) * P],
                                   src[:, 2 * t + j:2 * t + j + 1].to_broadcast([P, C]), eye,
                                   start=True, stop=True)
            mm.then_inc(S(signal), 1)

        def pair_pe(pe, use, p, out_c, in_c=None):
            n = p + 1

            def fill(j):
                if in_c is not None:
                    in_unit(pe, use, j, in_c[0], in_c[1], in_c[2])

            def need(*names):
                for name in names:
                    pe.wait_ge(*nth(name, n))

            pe.wait_ge(S("pp_ready"), n)
            pe.wait_ge(S("lora_ready"), 2)
            pe.matmul(bank[2][:], pp[0:C, P_W2A2:P_W2A2 + P], lora[0:C, :], start=True, stop=True).then_inc(S("lin_w"), 1)
            pe.matmul(bank[3][:], pp[C:P, P_W2A2:P_W2A2 + P], lora[C:P, :], start=True, stop=True).then_inc(S("lin_a"), 1)
            pe.matmul(bank[4][:], pp[:, P_G2:P_G2 + P], gate_in[:], start=True, stop=True).then_inc(S("lin_g"), 1)
            need("kk_sq")
            head_sums(pe, 5, W[7], "kk_sum")
            fill(0)
            need("kk_inv")
            head_spread(pe, 6, kkinv, "kk_spread")
            fill(1)
            need("z_ready", "decay_rate", "iclr", "g_out")
            by_chunk(pe, 4, [(W[5], eye2)], "z_turned")
            need("b_ready")
            by_chunk(pe, 2, [(W[6], W[5])], "azb_t")
            by_chunk(pe, 3, [(W[5], W[6])], "azb")
            need("kk_ready")
            by_chunk(pe, 5, [(W[6], eye2)], "b_turned")
            need("kd_ready")
            by_chunk(pe, 6, [(W[7], eye2)], "k_turned")
            need("v_mixed")
            by_chunk(pe, 7, [(W[2], eye2)], "v_turned")
            need("z_by_token")
            by_chunk(pe, 4, [(W[7], W[5])], "azk_t")
            need("b_by_token", "rd_ready")
            by_chunk(pe, 5, [(W[6], Rd)], "arb_t")
            need("k_by_token")
            by_chunk(pe, 6, [(W[7], Rd)], "ark_t")
            need("v_by_token", "rk_ready")
            pe.matmul(bank[7][:], heads, W[3][:], start=True, stop=True).then_inc(S("rk_sum"), 1)
            need("nt", "nn", "o32t", "o32", "o64")
            by_chunk(pe, 2, [(W[0], W[1])], "m2")
            by_chunk(pe, 3, [(W[1], W[0])], "m2_t")
            need("azk", "bonus")
            by_chunk(pe, 7, [(W[8], Vt)], "x2")
            fill(2)
            need("m2_s", "m2_ts", "e1")
            by_chunk(pe, 2, [(W[10], W[9])], "m4")
            by_chunk(pe, 3, [(W[9], W[10])], "m4_t")
            by_chunk(pe, 4, [(W[9], W[4])], "e2")
            need("m4_s", "m4_ts", "e2_s")
            by_chunk(pe, 3, [(W[11], W[5])], "e4")
            by_chunk(pe, 2, [(W[3], W[11])], "m8")
            need("lru_in", "ark", "x2_s")
            pe.wait_ge(S("gate_blocks"), 4 * n)
            pe.matmul(bank[6][:], BDa[:], lax[:], start=True, stop=True).then_inc(S("gate_r"), 1)
            pe.matmul(bank[7][:], BDx[:], lax[:], start=True, stop=True).then_inc(S("gate_i"), 1)
            need("m8_s", "e4_s")
            by_chunk(pe, 4, [(W[6], W[7])], "e8")
            need("dt_s")
            by_chunk(pe, 2, [(W[0], eye2)], "dd")
            by_chunk(pe, 3, [(O32, W[0])], "y32")
            need("dd_s")
            by_chunk(pe, 4, [(O32T, W[1])], "x32")
            need("y32_s", "arb")
            by_chunk(pe, 5, [(W[1], W[9])], "t32_t")
            need("x32_s", "lru_gates")
            by_chunk(pe, 6, [(W[0], W[10])], "t32")
            need("t32_ts")
            by_chunk(pe, 2, [(O64, W[11])], "y64")
            need("t32_s", "y64_s")
            by_chunk(pe, 3, [(W[3], W[5])], "tt")
            need("tt_s")
            by_chunk(pe, 4, [(W[6], Zt)], "w1")
            by_chunk(pe, 5, [(W[6], X2)], "w2")
            need("w1_s")
            by_chunk(pe, 7, [(W[7], Bt)], "gg")
            by_chunk(pe, 6, [(W[7], ARB)], "qq")
            need("w2_s", "g_s", "q_s")
            pe.sem_inc(S("waits_passed"), 1)
            for c in range(NCH):
                cols = slice(c * C, (c + 1) * C)
                prev = slice((c - 1) * C, c * C)
                if c < NCH - 1:
                    for rows in ROWS:
                        pe.matmul(bank[3 + c % 2][rows, cols], Bt[rows, cols], W[9][rows, cols], start=True, stop=False)
                        mm = pe.matmul(bank[3 + c % 2][rows, cols], Kt[rows, cols], Vt[rows, cols], start=False, stop=(c == 0))
                    if c == 0:
                        mm.then_inc(S("state_full"), 1)
                for rows in ROWS:
                    pe.matmul(bank[2][rows, cols], W[9][rows, cols], ARB[rows, cols], start=True, stop=False)
                    mm = pe.matmul(bank[2][rows, cols], Vt[rows, cols], ARK[rows, cols], start=False, stop=(c == 0))
                if c:
                    pe.wait_ge(S("state"), (NCH - 1) * p + c)
                    pe.sem_inc(S("waits_passed"), 1)
                    if c < NCH - 1:
                        for rows in ROWS:
                            mm = pe.matmul(bank[3 + c % 2][rows, cols], W[11][rows, cols], W[3][rows, prev],
                                           start=False, stop=True)
                        mm.then_inc(S("state_full"), 1)
                    for rows in ROWS:
                        mm = pe.matmul(bank[2][rows, cols], W[3][rows, prev], W[10][rows, cols],
                                       start=False, stop=True)
            mm.then_inc(S("y_heads"), 1)
            fill(3)
            need("ys")
            pe.matmul(bank[4][:], heads, W[0][:], start=True, stop=True).then_inc(S("y_sum"), 1)
            fill(4)
            need("yc_sq")
            head_sums(pe, 5, W[5], "y_var")
            need("ln_inv")
            head_spread(pe, 6, lninv, "ln_spread")
            c = chunk(*out_c)
            chunk_ready(pe, c)
            Y = [(yH[:, k, :], yL[:, k, :]) for k in range(2)]

            def y_tile(k):
                need(*(("ya_hi", "ya_lo") if k == 0 else ("yb_hi", "yb_lo")))
            last = in_c is None
            for m in range(KT):
                units(pe, use, [m % 2], [[wtile(c[1], k, m * P, D) for k in range(2)]], Y, m == 0,
                      y_tile if m == 0 else None)
            if last:
                output_norm_pe(pe, 1)

        def pair_act(act, use, p, out_c, in_c=None):
            n = p + 1

            def need(*names):
                for name in names:
                    act.wait_ge(*nth(name, n))

            def evac(name, dst, b, ready, func=ACT.Copy, **kw):
                need(name)
                nc.scalar.activation(dst[:], bank[b][:], func, **kw).then_inc(S(ready), 1)

            def fill(j):
                if in_c is not None:
                    in_evac(act, use, j, *in_c, p + 1)

            need("pp_ready", "k_mixed")
            nc.scalar.activation(W[7][:], W[1][:], ACT.Square, scale=pv(Q_KK)).then_inc(S("kk_sq"), 1)
            evac("lin_w", W[3], 2, "decay_rate", ACT.Sigmoid, bias=pv(Q_W0))
            evac("lin_a", W[4], 3, "iclr", ACT.Sigmoid, bias=pv(Q_A0))
            evac("lin_g", gout, 4, "g_out")
            need("kk_floor")
            nc.scalar.activation(kkroot[:], kkm[:], ACT.Sqrt).then_inc(S("kk_root"), 1)
            need("cumlog")
            nc.scalar.activation(W[8][:], W[5][:], ACT.Exp, scale=-EXP_HALF).then_inc(S("dec"), 1)
            nc.scalar.activation(W[9][:], W[5][:], ACT.Exp, scale=EXP_HALF).then_inc(S("dec_inv"), 1)
            need("cumlog_before")
            nc.scalar.activation(W[10][:], W[6][:], ACT.Exp, scale=-EXP_HALF).then_inc(S("dec_before"), 1)
            fill(0)
            fill(1)
            evac("z_turned", Zt, 4, "z_by_token")
            evac("b_turned", Bt, 5, "b_by_token")
            evac("k_turned", Kt, 6, "k_by_token")
            evac("v_turned", Vt, 7, "v_by_token")
            evac("m2", W[9], 2, "m2_s")
            evac("x2", X2, 7, "x2_s")
            fill(2)
            evac("m4", W[11], 2, "m4_s")
            need("e4")
            evac("m8", W[6], 2, "m8_s")
            evac("gate_r", lra, 6, "lru_r", ACT.Sigmoid, bias=pv(Q_BA))
            evac("gate_i", lix, 7, "lru_gates", ACT.Sigmoid, bias=pv(Q_BX))
            need("lru_r")
            nc.scalar.activation(ldr[:], lra[:], ACT.Tanh, scale=sp[:, 10, bass.ds(p, 1)]).then_inc(S("lru_tanh"), 1)
            need("lru_tanh")
            nc.scalar.activation(lra[:], lra[:], ACT.Exp, scale=sp[:, 11, bass.ds(p, 1)]).then_inc(S("lru_a"), 1)
            evac("dd", W[1], 2, "dd_s")
            evac("y32", W[9], 3, "y32_s")
            nc.scalar.activation(ldr[:], ldr[:], ACT.Sqrt).then_inc(S("lru_root"), 1)
            nc.scalar.activation(lgate[:], Uag[:], ACT.Gelu_apprx_tanh).then_inc(S("gelu"), 1)
            evac("x32", W[10], 4, "x32_s")
            evac("y64", W[5], 2, "y64_s")
            evac("w1", W[7], 4, "w1_s")
            need("ya_ready")
            nc.scalar.activation(yH[:, 0, :], lix[:], ACT.Copy).then_inc(S("ya_hi"), 1)
            evac("y_heads", W[0], 2, "ys")
            fill(3)
            need("yc")
            nc.scalar.activation(W[5][:], W[1][:], ACT.Square).then_inc(S("yc_sq"), 1)
            fill(4)
            need("y_var")
            nc.scalar.activation(lnroot[:], bank[5][:, 0:8], ACT.Sqrt, bias=epsc[:, 1:2],
                                 scale=1.0 / C).then_inc(S("ln_root"), 1)
            need("yb_ready")
            nc.scalar.activation(yH[:, 1, :], W[7][:], ACT.Copy).then_inc(S("yb_hi"), 1)
            c, i, per = out_c
            split_hi(act, chunk(c + 1, i, per))
            for m in range(KT):
                use.next(m % 2)
                if in_c is None:
                    square_f(act, 1, m, use, m % 2)
            if in_c is None:
                root_mean(act, 1)

        def pair_dve(dve, use, p, out_c, in_c=None):
            n = p + 1

            def need(*names):
                for name in names:
                    dve.wait_ge(*nth(name, n))

            def fill(j):
                if in_c is not None:
                    in_split(dve, j, *in_c)
                    use.next(UNITS[j][1])

            def add(dst, a, b, name, ready):
                need(name)
                nc.vector.tensor_tensor(dst[:], a[:], bank[b][:], ALU.add).then_inc(S(ready), 1)

            def masked(dst, b, k, name, ready):
                need(name)
                nc.vector.tensor_tensor(chunked(dst), chunked(bank[b]), table(k), ALU.mult).then_inc(S(ready), 1)

            def conv(k):
                taps = Uax[:, k:k + T]
                if k == 0:
                    nc.vector.tensor_scalar(lax[:], taps, pv(Q_CW), pv(Q_CB), ALU.mult, ALU.add).then_inc(S("conv"), 1)
                    return
                dve.wait_ge(S("conv"), 3 * p + k)
                nc.vector.scalar_tensor_tensor(lax[:], taps, pv(Q_CW + k), lax[:], ALU.mult,
                                               ALU.add).then_inc(S("lru_in" if k == 3 else "conv"), 1)

            need("pp_ready")
            dve.wait_ge(S("blocks_zero"), 2)
            for dst, k in ((BDa, P_WA), (BDx, P_WX)):
                for j, rows in enumerate(ROWS):
                    nc.vector.tensor_copy(dst[rows, j * C:(j + 1) * C],
                                          pp[rows, k:k + C]).then_inc(S("gate_blocks"), 1)
            mixes = ((Uk, W[1], Q_MUK, "k_mixed"), (Ur, W[0], Q_MUR, "r_mixed"), (Uv, W[2], Q_MUV, "v_mixed"))
            for j, (U, dst, mu, name) in enumerate(mixes):
                if j:
                    need(mixes[j - 1][3])
                nc.vector.tensor_tensor(mixdiff[:], U[:, 0:T], U[:, 1:T + 1], ALU.subtract).then_inc(S("mix_diff"), 1)
                dve.wait_ge(S("mix_diff"), 3 * p + j + 1)
                nc.vector.scalar_tensor_tensor(dst[:], mixdiff[:], pv(mu), U[:, 1:T + 1], ALU.mult,
                                               ALU.add).then_inc(S(name), 1)
            need("kk_sum")
            nc.vector.tensor_scalar(kkm[:], bank[5][:, 0:8], 1e-24, None, ALU.max).then_inc(S("kk_floor"), 1)
            need("decay_rate")
            nc.vector.tensor_tensor_scan(W[5][:], cst[:, K_RESET:K_RESET + T], W[3][:], 0.0, ALU.mult,
                                         ALU.add).then_inc(S("cumlog"), 1)
            need("cumlog")
            nc.vector.tensor_tensor(W[6][:], W[5][:], W[3][:], ALU.subtract).then_inc(S("cumlog_before"), 1)
            fill(0)
            fill(1)
            need("kk_root")
            nc.vector.reciprocal(kkinv[:], kkroot[:]).then_inc(S("kk_inv"), 1)
            need("iclr")
            nc.vector.tensor_scalar(X2[:], W[4][:], -1.0, pv(Q_KA), ALU.add, ALU.mult).then_inc(S("k_factor"), 1)
            need("k_factor")
            nc.vector.scalar_tensor_tensor(X2[:], X2[:], 1.0, W[1][:], ALU.add, ALU.mult).then_inc(S("k_new"), 1)
            need("kk_spread")
            nc.vector.scalar_tensor_tensor(W[11][:], W[1][:], pv(Q_KK), bank[6][:], ALU.mult,
                                           ALU.mult).then_inc(S("kk_ready"), 1)
            need("kk_ready", "dec_before")
            nc.vector.scalar_tensor_tensor(W[5][:], W[11][:], -1.0, W[10][:], ALU.mult,
                                           ALU.mult).then_inc(S("z_ready"), 1)
            nc.vector.tensor_tensor(mixdiff[:], W[11][:], W[4][:], ALU.mult).then_inc(S("b_plain"), 1)
            need("b_plain")
            nc.vector.tensor_tensor(W[6][:], mixdiff[:], W[9][:], ALU.mult).then_inc(S("b_ready"), 1)
            need("k_new")
            nc.vector.tensor_tensor(W[7][:], X2[:], W[9][:], ALU.mult).then_inc(S("kd_ready"), 1)
            nc.vector.tensor_tensor(Rd[:], W[0][:], W[8][:], ALU.mult).then_inc(S("rd_ready"), 1)
            need("cumlog_before")
            nc.vector.scalar_tensor_tensor(W[3][:], W[0][:], pv(Q_RK), X2[:], ALU.mult,
                                           ALU.mult).then_inc(S("rk_ready"), 1)
            nc.vector.tensor_copy(PC[:], chunked(W[8])[:, :, C - 1]).then_inc(S("pc_ready"), 1)
            need("rk_ready")
            masked(W[0], 2, K_D16T, "azb_t", "nt")
            masked(O32T, 2, K_O32T, "azb_t", "o32t")
            need("k_new", "kk_ready")
            masked(W[1], 3, K_D16, "azb", "nn")
            masked(O32, 3, K_O32, "azb", "o32")
            masked(O64, 3, K_O64, "azb", "o64")
            need("nt", "b_plain")
            nc.vector.tensor_tensor(chunked(W[4]), chunked(W[0]), table(K_EYE2), ALU.add).then_inc(S("e1"), 1)
            need("pc_ready", "rd_ready")
            masked(W[8], 4, K_LT, "azk_t", "azk")
            masked(ARB, 5, K_LE, "arb_t", "arb")
            masked(ARK, 6, K_LE, "ark_t", "ark")
            need("rk_sum")
            nc.vector.tensor_tensor(bonus[:], W[2][:], bank[7][:], ALU.mult).then_inc(S("bonus"), 1)
            need("z_ready")
            need("m2_t")
            nc.vector.tensor_copy(W[10][:], bank[3][:]).then_inc(S("m2_ts"), 1)
            fill(2)
            for k in range(4):
                conv(k)
            need("m4_t")
            nc.vector.tensor_copy(W[3][:], bank[3][:]).then_inc(S("m4_ts"), 1)
            need("e1")
            add(W[5], W[4], 4, "e2", "e2_s")
            need("e2_s")
            add(W[7], W[5], 3, "e4", "e4_s")
            need("e4_s")
            add(W[0], W[7], 4, "e8", "dt_s")
            need("lru_gates", "lru_in")
            nc.vector.tensor_tensor(lix[:], lix[:], lax[:], ALU.mult).then_inc(S("lru_iu"), 1)
            need("lru_a", "lru_root")
            nc.vector.scalar_tensor_tensor(ldr[:], lra[:], 1.0, ldr[:], ALU.add, ALU.mult).then_inc(S("lru_scale"), 1)
            need("dt_s")
            add(W[11], W[0], 5, "t32_t", "t32_ts")
            need("lru_scale", "lru_iu")
            nc.vector.tensor_tensor(ldr[:], ldr[:], lix[:], ALU.mult).then_inc(S("lru_drive"), 1)
            need("dd_s")
            add(W[3], W[1], 6, "t32", "t32_s")
            need("lru_drive")
            nc.vector.tensor_tensor_scan(lix[:], lra[:], ldr[:], 0.0, ALU.mult, ALU.add).then_inc(S("lru_h"), 1)
            need("t32_ts")
            add(W[6], W[11], 3, "tt", "tt_s")
            need("lru_h", "gelu")
            nc.vector.tensor_tensor(lix[:], lix[:], lgate[:], ALU.mult).then_inc(S("ya_ready"), 1)
            need("w2")
            nc.vector.tensor_copy(W[9][:], bank[5][:]).then_inc(S("w2_s"), 1)
            need("t32_ts", "gg", "tt_s")
            nc.vector.tensor_tensor(chunked(W[11]), chunked(bank[7]), table(K_EYE2), ALU.add).then_inc(S("g_s"), 1)
            need("rd_ready")
            add(W[10], Rd, 6, "qq", "q_s")
            need("ya_hi", "ya_ready")
            nc.vector.tensor_tensor(yL[:, 0, :], lix[:], yH[:, 0, :], ALU.subtract).then_inc(S("ya_lo"), 1)
            for c in range(NCH - 1):
                cols = slice(c * C, (c + 1) * C)
                dve.wait_ge(S("state_full"), (NCH - 1) * p + c + 1)
                nc.vector.tensor_scalar(W[3][:, cols], bank[3 + c % 2][:, cols], PC[:, c:c + 1], None,
                                        ALU.mult).then_inc(S("state"), 1)
            fill(3)
            need("ys", "y_sum")
            nc.vector.scalar_tensor_tensor(W[1][:], bank[4][:], -1.0 / C, W[0][:], ALU.mult,
                                           ALU.add).then_inc(S("yc"), 1)
            fill(4)
            need("ln_root")
            nc.vector.reciprocal(lninv[:], lnroot[:]).then_inc(S("ln_inv"), 1)
            need("ln_spread", "yc")
            nc.vector.tensor_tensor(W[6][:], W[1][:], bank[6][:], ALU.mult).then_inc(S("yn"), 1)
            need("yn")
            nc.vector.tensor_scalar(W[6][:], W[6][:], pv(Q_LNW), pv(Q_LNB), ALU.mult, ALU.add).then_inc(S("y_affine"), 1)
            need("y_affine", "bonus")
            nc.vector.tensor_tensor(W[6][:], W[6][:], bonus[:], ALU.add).then_inc(S("y_bonus"), 1)
            need("y_bonus", "g_out")
            nc.vector.tensor_tensor(W[7][:], W[6][:], gout[:], ALU.mult).then_inc(S("yb_ready"), 1)
            need("yb_ready", "yb_hi")
            nc.vector.tensor_tensor(yL[:, 1, :], W[7][:], yH[:, 1, :], ALU.subtract).then_inc(S("yb_lo"), 1)
            c, i, per = out_c
            split_lo(dve, chunk(c + 1, i, per))
            dve.wait_ge(S("f_zero"), 1)
            for m in range(KT):
                add_to_f(dve, use, m % 2, m)

        def mixers_ab(eng, use, pair):
            turns = PAIRS - 1
            with eng.Fori(0, turns) as p:
                use.loop(p, [7, 6, 0, 0])
                pair(eng, use, p, (AB_TURN + 3, p, AB_TURN), (AB_TURN, p, AB_TURN))
            use.end(turns)
            pair(eng, use, turns, (AB_TURN + AB_TURN * turns, 0, 0))

        def ret_pe(pe, use, m, n):
            def head(hd, last):
                n4 = 4 * hd
                c = chunk(RET_CHUNK0, hd, 8)
                chunk_ready(pe, c)
                units(pe, use, [0, 1], [[wtile(c[1], kt, j * P, 2 * P) for kt in range(KT)] for j in range(2)], X,
                      True, x_tiles(pe, m))
                c = chunk(RET_CHUNK0 + 1, hd, 8)
                chunk_ready(pe, c)
                for j in range(2):
                    sums(pe, [6 + j], [[wtile(c[1], kt, j * P, 2 * P) for kt in range(KT)]], X,
                         "keys_full", begins=(j == 0))
                for half in range(2):
                    c = chunk(RET_CHUNK0 + 2 + half, hd, 8)
                    chunk_ready(pe, c)
                    for k in range(4):
                        kt = half * 4 + k
                        wh, wl = (w[c[1]][:, k * T:(k + 1) * T] for w in (WH, WL))
                        for t in range(TT):
                            tok = slice(t * P, (t + 1) * P)
                            mm = pe.matmul(bank[2 + t][:], XH[:, kt, tok], wh, start=(kt == 0), stop=False)
                            if k == 0 and t == 0:
                                mm.then_inc(S("chunk_begun"), 1)
                            pe.matmul(bank[2 + t][:], XH[:, kt, tok], wl, start=False, stop=False)
                            mm = pe.matmul(bank[2 + t][:], XL[:, kt, tok], wh, start=False, stop=(kt == KT - 1))
                mm.then_inc(S("v_full"), 1)

                def gate(E):
                    c = chunk(RET_CHUNK0 + 4 + E // 2, hd, 8)
                    if E % 2 == 0:
                        chunk_ready(pe, c)
                    units(pe, use, [E % 2], [[wtile(c[1], kt, E % 2 * P, 2 * P) for kt in range(KT)]], X, E % 2 == 0)

                gate(0)
                pe.wait_ge(S("qk_rotated"), n4 + 4)
                pe.wait_ge(S("v_out_act"), 2 * hd + 2)
                pe.wait_ge(S("v_out_dve"), 2 * hd + 2)
                for J in range(TT):
                    for k in range(2):
                        mm = pe.matmul(bank[2 + J][:, 0:T - J * P], kr[:, k, J * P:(J + 1) * P], qr[:, k, J * P:],
                                       start=(k == 0), stop=(k == 1))
                    mm.then_inc(S("scores"), 1)
                gate(1)
                for E in range(4):
                    for J in range(TT):
                        if E == 0:
                            pe.wait_ge(S("decayed"), n4 + J + 1)
                        mm = pe.matmul(bank[2 + E][:, J * P:], Vr[:, J, E * P:(E + 1) * P], Sc[:, J, 0:T - J * P],
                                       start=(J == 0), stop=(J == TT - 1), skip_group_check=True)
                    mm.then_inc(S("y_full"), 1)
                gate(2)
                pe.wait_ge(S("ysq_summed"), 2 * hd + 2)
                sum_by_token(pe, sq_sum[:], True, False)
                pe.wait_ge(S("ysq_ready"), n4 + 4)
                sum_by_token(pe, sq[:, 1, :], False, True).then_inc(S("ysq_used"), 1)
                gate(3)
                pe.wait_ge(S("y_inv"), hd + 1)
                for t in range(TT):
                    mm = pe.matmul(bank[7][:, t * P:(t + 1) * P], rstd[:, t:t + 1].to_broadcast([P, P]), eye,
                                   start=True, stop=True)
                mm.then_inc(S("y_spread"), 1)

                def b_tile(k):
                    pe.wait_ge(S("y_hi"), n4 + k + 1)
                    pe.wait_ge(S("y_lo"), n4 + k + 1)
                for j in range(KT):
                    c = chunk(RET_CHUNK0 + 6 + j // 4, hd, 8)
                    if j % 4 == 0:
                        chunk_ready(pe, c)
                    units(pe, use, [j % 2], [[wtile(c[1], k, j % 4 * P, T) for k in range(4)]],
                          [(BH[:, k, :], BL[:, k, :]) for k in range(4)], j % 4 == 0, b_tile if j == 0 else None)
                if last:
                    output_norm_pe(pe, n)
            turns_then_last(pe, use, [7, 7, 0, 0], RET_HEADS, head)

        def ret_act(act, use, n):
            def head(hd, last):
                n4 = 4 * hd
                use.next(0), use.next(1)
                for k in (2, 3, 4):
                    split_hi(act, chunk(RET_CHUNK0 + k, hd, 8))
                act.wait_ge(S("v_full"), hd + 1)
                for t in range(2):
                    nc.scalar.activation(Vr[:, t, :], bank[2 + t][:], ACT.Copy).then_inc(S("v_out_act"), 1)

                def gate(E):
                    act.wait_ge(S(f"acc_full{E % 2}"), use.next(E % 2))
                    nc.scalar.activation(sg[:, E, :], bank[E % 2][:], ACT.Silu).then_inc(S(f"acc_free{E % 2}"), 1)
                split_hi(act, chunk(RET_CHUNK0 + 5, hd, 8))
                gate(0)
                gate(1)
                for E in range(4):
                    act.wait_ge(S("y_full"), n4 + E + 1)
                    if E >= 2:
                        act.wait_ge(S("ysq_summed"), 2 * hd + 1)
                    nc.scalar.activation(sq[:, E % 2, :], bank[2 + E][:], ACT.Square).then_inc(S("ysq_ready"), 1)
                split_hi(act, chunk(RET_CHUNK0 + 6, hd, 8))
                gate(2)
                act.wait_ge(S("ysq_used"), hd + 1)
                nc.scalar.activation(root[:, 0:TT], bank[6][:, 0:TT], ACT.Sqrt, bias=epsc[:, 0:1],
                                     scale=1.0 / RET_DV).then_inc(S("y_root"), 1)
                gate(3)
                for E in range(4):
                    act.wait_ge(S("y_ready"), n4 + E + 1)
                    nc.scalar.activation(BH[:, E, :], yv[:, E, :], ACT.Copy).then_inc(S("y_hi"), 1)
                for half in range(2):
                    split_hi(act, chunk(RET_CHUNK0 + 7 + half, hd, 8))
                    for j in range(4):
                        use.next(j % 2)
                        if last:
                            square_f(act, n, 4 * half + j, use, j % 2)
                if last:
                    root_mean(act, n)
                else:
                    split_hi(act, chunk(RET_CHUNK0 + 9, hd, 8))
            turns_then_last(act, use, [7, 7, 0, 0], RET_HEADS, head)

        def ret_dve(dve, use, k_zero):
            cos, sin = rc[:, R_COS:R_COS + T], rc[:, R_SIN:R_SIN + T]
            dve.wait_ge(S("rc_loaded"), 16)

            def head(hd, last):
                n4 = 4 * hd
                for k, dst in ((0, qr), (1, kr)):
                    if k == 0:
                        n0, n1 = use.next(0), use.next(1)
                        dve.wait_ge(S("acc_full0"), n0)
                        dve.wait_ge(S("acc_full1"), n1)
                        one, two, read = bank[0], bank[1], ("acc_free0", "acc_free1")
                    else:
                        dve.wait_ge(S("keys_full"), 2 * hd + 2)
                        dve.wait_ge(S("qk_rotated"), n4 + 2)
                        one, two, read = bank[6], bank[7], ("keys_read", "keys_read")
                    nc.vector.tensor_tensor(rt[:, 0, :], one[:], cos, ALU.mult)
                    nc.vector.tensor_tensor(rt[:, 1, :], two[:], sin, ALU.mult)
                    nc.vector.tensor_tensor(rt[:, 2, :], two[:], cos, ALU.mult).then_inc(S(read[1]), 1)
                    nc.vector.tensor_tensor(rt[:, 3, :], one[:], sin, ALU.mult).then_inc(S(read[0]), 1)
                    if k == 0:
                        dve.wait_ge(S("acc_free1"), n1)
                        dve.wait_ge(S("acc_free0"), n0)
                    else:
                        dve.wait_ge(S("keys_read"), 2 * hd + 2)
                    nc.vector.tensor_tensor(dst[:, 0, :], rt[:, 0, :], rt[:, 1, :], ALU.subtract).then_inc(S("qk_rotated"), 1)
                    nc.vector.tensor_tensor(dst[:, 1, :], rt[:, 2, :], rt[:, 3, :], ALU.add).then_inc(S("qk_rotated"), 1)
                    split_lo(dve, chunk(RET_CHUNK0 + 2 + k, hd, 8))
                split_lo(dve, chunk(RET_CHUNK0 + 4, hd, 8))
                dve.wait_ge(S("v_full"), hd + 1)
                for t in range(2, 4):
                    nc.vector.tensor_copy(Vr[:, t, :], bank[2 + t][:]).then_inc(S("v_out_dve"), 1)
                split_lo(dve, chunk(RET_CHUNK0 + 5, hd, 8))
                for J in range(TT):
                    dve.wait_ge(S("scores"), n4 + J + 1)
                    nc.vector.tensor_tensor(Sc[:, J, 0:T - J * P], bank[2 + J][:, 0:T - J * P],
                                            rc[:, bass.ds(R_DECAY + T * hd, T - J * P)],
                                            ALU.mult).then_inc(S("decayed"), 1)

                def gated(E):
                    dve.wait_ge(S("ysq_ready"), n4 + E + 1)
                    dve.wait_ge(S(f"acc_free{E % 2}"), use.next(E % 2))
                    nc.vector.tensor_tensor(yv[:, E, :], bank[2 + E][:], sg[:, E, :], ALU.mult).then_inc(S("y_gated"), 1)
                gated(0)
                gated(1)
                split_lo(dve, chunk(RET_CHUNK0 + 6, hd, 8))
                gated(2)
                dve.wait_ge(S("y_root"), hd + 1)
                nc.vector.reciprocal(rstd[:, 0:TT], root[:, 0:TT]).then_inc(S("y_inv"), 1)
                gated(3)
                dve.wait_ge(S("y_spread"), hd + 1)
                dve.wait_ge(S("y_gated"), n4 + 4)
                for E in range(5):
                    if E < 4:
                        nc.vector.tensor_tensor(yv[:, E, :], yv[:, E, :], bank[7][:], ALU.mult).then_inc(S("y_ready"), 1)
                    if E:
                        dve.wait_ge(S("y_hi"), n4 + E)
                        nc.vector.tensor_tensor(BL[:, E - 1, :], yv[:, E - 1, :], BH[:, E - 1, :],
                                                ALU.subtract).then_inc(S("y_lo"), 1)
                dve.wait_ge(S("f_zero"), k_zero + 1)
                for half in range(2):
                    split_lo(dve, chunk(RET_CHUNK0 + 7 + half, hd, 8))
                    for j in range(4):
                        add_to_f(dve, use, j % 2, half * 4 + j)
                if not last:
                    split_lo(dve, chunk(RET_CHUNK0 + 9, hd, 8))
            turns_then_last(dve, use, [7, 7, 0, 0], RET_HEADS, head)

        block = ctx.enter_context(nc.Block())

        @block.sync
        def _(sync):
            half = KT // 2
            for j in range(2):
                sync.dma_start(h[:, j * half:(j + 1) * half, :],
                               x[j * D // 2:(j + 1) * D // 2, :].rearrange("(k p) t -> p k t", p=P)
                               ).then_inc(S(f"x_loaded{j}"), 16)
                if j == 0:
                    sync.dma_start(vec[:], vectors).then_inc(S("vec_loaded"), 16)
                    sync.dma_start(cst[:], const).then_inc(S("const_loaded"), 16)
            for c in range(2):
                sync.dma_start(raw[c][:], weights[c]).then_inc(S(f"raw_loaded{c}"), 16)
            with sync.Fori(0, ALL_CHUNKS // 2) as i:
                for c in range(2):
                    sync.wait_ge(S("w_lo"), 2 * i + c + 1)
                    sync.dma_start(raw[c][:], weights[bass.ds(2 * i + (2 + c), 1)].rearrange(
                        "a p c -> (a p) c")).then_inc(S(f"raw_loaded{c}"), 16)
            for kt in range(KT):
                h_is_ready(sync, 3, kt)
                sync.dma_start(out[kt * P:(kt + 1) * P, :], h[:, kt, :]).then_inc(S("out_stored"), 16)
            sync.wait_ge(S("out_stored"), 16 * KT)
            for c in range(2):
                sync.wait_ge(S(f"raw_loaded{c}"), 16 * (ALL_CHUNKS // 2 + 1))

        @block.gpsimd
        def _(pool):
            nc.gpsimd.memset(epsc[:, 0:1], EPS).then_inc(S("eps"), 1)
            nc.gpsimd.memset(epsc[:, 1:2], LN_EPS).then_inc(S("eps"), 1)
            for U, w in ((Ur, 1), (Uk, 1), (Uv, 1), (Uax, 3)):
                nc.gpsimd.memset(U[:, 0:w], 0.0).then_inc(S("edge_zero"), 1)
            nc.gpsimd.memset(BDa[:], 0.0).then_inc(S("blocks_zero"), 1)
            nc.gpsimd.memset(BDx[:], 0.0).then_inc(S("blocks_zero"), 1)
            nc.gpsimd.memset(f[:], 0.0).then_inc(S("f_zero"), 1)
            pool.wait_ge(S("f_zero"), 1)
            pool.dma_start(stage[:], pairs[0]).then_inc(S("stage_loaded"), 16)

            def take_pair(p, later):
                pool.wait_ge(S("stage_loaded"), 16 * p + 16)
                if later:
                    pool.wait_ge(*nth("y_affine", p))
                    pool.wait_ge(*nth("lru_gates", p))
                    pool.wait_ge(*nth("g_out", p))
                pool.sem_inc(S("waits_passed"), 1)
                nc.gpsimd.tensor_copy(pp[:], stage[:]).then_inc(S("pp_ready"), 1)
                pool.wait_ge(S("pp_ready"), p + 1)

            take_pair(0, False)
            pre_pool(pool, 0)
            with pool.Fori(1, PAIRS) as p:
                pool.dma_start(stage[:], pairs[bass.ds(p, 1)].rearrange("a p c -> (a p) c")).then_inc(S("stage_loaded"), 16)
                take_pair(p, True)
            for k in range(1, 5):
                output_norm_pool(pool, 2 * k - 1)
                residual_pool(pool, k - 1)
                if k == 4:
                    continue
                pre_pool(pool, k)
                h_is_ready(pool, k - 1, KT - 2)
                nc.gpsimd.memset(f[:], 0.0).then_inc(S("f_zero"), 1)
                if k == 1:
                    pool.dma_start(rc[:], ret_const).then_inc(S("rc_loaded"), 16)
                if k == 2:
                    with pool.Fori(0, RET_HEADS) as hd:
                        pool.wait_ge(S("ysq_ready"), 4 * hd + 2)
                        pool.sem_inc(S("waits_passed"), 1)
                        nc.gpsimd.tensor_tensor(sq_sum[:], sq[:, 0, :], sq[:, 1, :], ALU.add).then_inc(S("ysq_summed"), 1)
                        pool.wait_ge(S("ysq_ready"), 4 * hd + 3)
                        pool.wait_ge(S("ysq_summed"), 2 * hd + 1)
                        pool.sem_inc(S("waits_passed"), 1)
                        nc.gpsimd.tensor_tensor(sq_sum[:], sq_sum[:], sq[:, 0, :], ALU.add).then_inc(S("ysq_summed"), 1)
            pool.wait_ge(S("f_zero"), 4)

        @block.tensor
        def _(pe):
            use = Turns(4)
            pe.wait_ge(S("vec_loaded"), 16)
            pe.wait_ge(S("const_loaded"), 16)
            pe.wait_ge(S("ones_ready"), 1)
            input_norm_pe(pe, 0)
            chunk_ready(pe, chunk(0))
            units(pe, use, [0, 1], [[wtile(0, kt, j * P, 2 * P) for kt in range(KT)] for j in range(2)], X, True,
                  x_tiles(pe, 0))
            for j in range(5):
                in_unit(pe, use, j, 1, 0, 0)
            mixers_ab(pe, use, pair_pe)
            input_norm_pe(pe, 2)
            ffn_pe(pe, use, FFN0_CHUNK, 1, 0, 3)
            input_norm_pe(pe, 4)
            ret_pe(pe, use, 2, 5)
            input_norm_pe(pe, 6)
            ffn_pe(pe, use, FFN1_CHUNK, 3, 1, 7)

        @block.scalar
        def _(act):
            use = Turns(4)
            act.wait_ge(S("eps"), 2)
            act.wait_ge(S("vec_loaded"), 16)
            act.wait_ge(S("sp_abs"), 1)
            nc.scalar.activation(sp[:, 2, :], sp[:, 1, :], ACT.Exp, scale=-1.0).then_inc(S("sp_exp"), 1)
            pre_act(act, 0, 0)
            split_hi(act, chunk(0))
            split_hi(act, chunk(1))
            act.wait_ge(S("edge_zero"), 4)
            for j, U in enumerate((Ur, Uk)):
                n = use.next(j)
                act.wait_ge(S(f"acc_full{j}"), n)
                nc.scalar.activation(U[:, 1:], bank[j][:], ACT.Copy).then_inc(S(f"acc_free{j}"), 1)
            act.wait_ge(S("lora_mixed"), 2)
            nc.scalar.activation(lora[0:C, :], lora[0:C, :], ACT.Tanh).then_inc(S("lora_ready"), 1)
            nc.scalar.activation(gate_in[:], gate_in[:], ACT.Sigmoid).then_inc(S("lora_ready"), 1)
            for j in range(5):
                in_evac(act, use, j, 1, 0, 0, 0)
            mixers_ab(act, use, pair_act)
            second_chunk_act(act, FFN0_CHUNK)
            pre_act(act, 2, 1)
            ffn_act(act, use, FFN0_CHUNK, 0, 3)
            second_chunk_act(act, RET_CHUNK0)
            pre_act(act, 4, 2)
            ret_act(act, use, 5)
            second_chunk_act(act, FFN1_CHUNK)
            pre_act(act, 6, 3)
            ffn_act(act, use, FFN1_CHUNK, 1, 7)

        @block.vector
        def _(dve):
            use = Turns(4)
            V = nc.vector
            dve.wait_ge(S("vec_loaded"), 16)
            dve.wait_ge(S("const_loaded"), 16)
            V.memset(ones1, 1.0).then_inc(S("ones_ready"), 1)
            lam = vec[:, V_LAM:V_LAM + PAIRS]
            V.tensor_scalar(sp[:, 0, :], lam, -1.0, 0.0, ALU.mult, ALU.max).then_inc(S("sp_max"), 1)
            V.scalar_tensor_tensor(sp[:, 1, :], lam, -1.0, lam, ALU.mult, ALU.max).then_inc(S("sp_abs"), 1)
            steps = [0]

            def step(ins):
                ins.then_inc(S("sp_step"), 1)
                steps[0] += 1
                dve.wait_ge(S("sp_step"), steps[0])
            dve.wait_ge(S("sp_exp"), 1)
            step(V.tensor_scalar(sp[:, 3, :], sp[:, 2, :], 2.0, None, ALU.add))
            step(V.reciprocal(sp[:, 4, :], sp[:, 3, :]))
            step(V.tensor_tensor(sp[:, 5, :], sp[:, 4, :], sp[:, 2, :], ALU.mult))
            step(V.tensor_tensor(sp[:, 6, :], sp[:, 5, :], sp[:, 5, :], ALU.mult))
            step(V.tensor_scalar(sp[:, 7, :], sp[:, 6, :], 1.0 / 15, None, ALU.mult))
            for k in (13, 11, 9, 7, 5, 3):
                step(V.scalar_tensor_tensor(sp[:, 7, :], sp[:, 7, :], 1.0 / k, sp[:, 6, :], ALU.add, ALU.mult))
            step(V.scalar_tensor_tensor(sp[:, 8, :], sp[:, 7, :], 1.0, sp[:, 5, :], ALU.add, ALU.mult))
            dve.wait_ge(S("sp_max"), 1)
            step(V.scalar_tensor_tensor(sp[:, 9, :], sp[:, 8, :], 2.0, sp[:, 0, :], ALU.mult, ALU.add))
            step(V.tensor_scalar(sp[:, 10, :], sp[:, 9, :], LRU_C / 2, None, ALU.mult))
            step(V.tensor_scalar(sp[:, 11, :], sp[:, 9, :], -LRU_C, None, ALU.mult))

            pre_dve(dve, 0, 0, 0, 0)
            split_lo(dve, chunk(0))
            split_lo(dve, chunk(1))
            for j, (U, dst) in enumerate(((Ur, lora), (Uk, gate_in))):
                n = use.next(j)
                dve.wait_ge(S(f"acc_free{j}"), n)
                if j:
                    dve.wait_ge(S("lora_mixed"), 1)
                V.tensor_tensor(mixdiff[:], U[:, 0:T], U[:, 1:T + 1], ALU.subtract).then_inc(S("lora_diff"), 1)
                dve.wait_ge(S("lora_diff"), j + 1)
                V.scalar_tensor_tensor(dst[:], mixdiff[:], vec[:, V_MU_LORA + j:V_MU_LORA + j + 1], U[:, 1:T + 1],
                                       ALU.mult, ALU.add).then_inc(S("lora_mixed"), 1)
            dve.wait_ge(S("lora_mixed"), 2)
            for j in range(5):
                in_split(dve, j, 1, 0, 0)
                use.next(UNITS[j][1])
            for b in range(2):
                dve.wait_ge(S(f"acc_free{b}"), use.now(b))
            mixers_ab(dve, use, pair_dve)
            residual_dve(dve, 1, 0, 0, 1)
            split_lo(dve, chunk(FFN0_CHUNK + 1))
            pre_dve(dve, 2, 1, 0, 2)
            ffn_dve(dve, use, FFN0_CHUNK, 0, 1)
            residual_dve(dve, 3, 1, 0, 3)
            split_lo(dve, chunk(RET_CHUNK0 + 1))
            pre_dve(dve, 4, 2, 1, 0)
            ret_dve(dve, use, 2)
            residual_dve(dve, 5, 2, 1, 1)
            split_lo(dve, chunk(FFN1_CHUNK + 1))
            pre_dve(dve, 6, 3, 1, 2)
            ffn_dve(dve, use, FFN1_CHUNK, 1, 3)
            residual_dve(dve, 7, 3, 1, 3)


def tile_rows(w, rows, cols):
    part = w[rows, cols]
    k = part.shape[0] // P
    return part.reshape(k, P, part.shape[1]).transpose(1, 0, 2).reshape(P, -1)


def weight_stream(a):
    s = lambda at, n: slice(at, at + n)
    every = slice(None)
    ab_in, ab_out = a["ab_w_in"][0], a["ab_w_out"][0]
    W2 = D // 2
    chunks = [tile_rows(ab_in, every, s(2 * W2 + 3 * W2, 2 * P))]

    def pair_in(p):
        col = {"ax": p * P, "ag": W2 + p * P, "r": 2 * W2 + p * P, "k": 3 * W2 + p * P, "v": 4 * W2 + p * P}
        for one, two in (("r", "k"), ("v", "ax")):
            both = np.concatenate([ab_in[:, s(col[one], P)], ab_in[:, s(col[two], P)]], axis=1)
            chunks.append(tile_rows(both, every, every))
        ag = tile_rows(ab_in, every, s(col["ag"], P))
        chunks.append(np.concatenate([ag, ag], axis=1))

    def pair_out(p):
        rows = np.concatenate([ab_out[s(p * P, P)], ab_out[s(W2 + p * P, P)]], axis=0)
        chunks.append(tile_rows(rows, every, every))

    pair_in(0)
    for p in range(PAIRS):
        if p + 1 < PAIRS:
            pair_in(p + 1)
        pair_out(p)

    def mlp(layer):
        w1, w2 = a["ffn_w_in"][layer], a["ffn_w_out"][layer]
        for q in range(QUARTERS):
            for j in range(4):
                chunks.append(tile_rows(w1, every, s(q * D + j * 2 * P, 2 * P)))
            for j in range(4):
                chunks.append(tile_rows(w2, s(q * D, D), s(j * 2 * P, 2 * P)))

    mlp(0)
    r_in, r_out = a["ret_w_in"][0], a["ret_w_out"][0]
    for hd in range(RET_HEADS):
        chunks.append(tile_rows(r_in, every, s(hd * 2 * P, 2 * P)))
        chunks.append(tile_rows(r_in, every, s(D + hd * 2 * P, 2 * P)))
        for half in range(2):
            chunks.append(tile_rows(r_in, s(half * D // 2, D // 2), s(2 * D + hd * T, T)))
        for half in range(2):
            chunks.append(tile_rows(r_in, every, s(4 * D + hd * T + half * 2 * P, 2 * P)))
        for half in range(2):
            chunks.append(tile_rows(r_out, s(hd * T, T), s(half * T, T)))
    mlp(1)
    while len(chunks) < 2 * (ALL_CHUNKS // 2) + 2:
        chunks.append(chunks[-1])
    return np.stack(chunks)


def pair_tables(a):
    out = []
    for p in range(PAIRS):
        s = slice(p * P, (p + 1) * P)
        mu = a["rwkv_mu"][0]
        W2 = D // 2
        columns = [a["rwkv_w0"][0][s], a["rwkv_a0"][0][s], a["rwkv_k_k"][0][s], a["rwkv_k_a"][0][s],
                   a["rwkv_r_k"][0][s], a["rwkv_ln_w"][0][s], a["rwkv_ln_b"][0][s],
                   *(a["lru_conv_w"][0][i][s] for i in range(4)), a["lru_conv_b"][0][s],
                   a["lru_ba"][0][s], a["lru_bx"][0][s]]
        columns = [mu[i * W2:(i + 1) * W2][s] for i in range(3)] + columns
        out.append(np.concatenate(
            [np.concatenate([a["rwkv_w2"][0][:, s], a["rwkv_a2"][0][:, s]], axis=0), a["rwkv_g2"][0][:, s],
             a["lru_wa"][0][2 * p:2 * p + 2].reshape(P, C), a["lru_wx"][0][2 * p:2 * p + 2].reshape(P, C),
             np.stack(columns, axis=1)], axis=1))
    return np.stack(out)


def vector_table(a):
    norms = np.stack([a[k] for k in ("norm_mix_pre", "norm_mix_post", "norm_ffn_pre", "norm_ffn_post")], axis=1)
    norms = norms.reshape(2 * 4 * KT, P).T
    mu = a["rwkv_mu"][0][3 * D // 2:].reshape(2, P).T
    lam = a["lru_lambda"][0].reshape(PAIRS, P).T
    return np.concatenate([norms, mu, lam, lam[:, 0:1]], axis=1)


def kernel(**inputs):
    import concourse.bacc as bacc
    from concourse.bass_utils import run_bass_kernel_spmd

    a = {k: np.asarray(v) for k, v in inputs.items()}
    const, ret_const = constants()
    arrays = {
        "x_fm": np.ascontiguousarray(a["x"][0].T),
        "weights": np.ascontiguousarray(weight_stream(a)),
        "pairs": np.ascontiguousarray(pair_tables(a)),
        "vectors": np.ascontiguousarray(vector_table(a)),
        "const": const,
        "ret_const": ret_const,
    }
    nc = bacc.Bacc("TRN2", target_bir_lowering=False, num_devices=1)
    args = [nc.dram_tensor(k, v.shape, F32, kind="ExternalInput").ap() for k, v in arrays.items()]
    out = nc.dram_tensor("out_fm", (D, T), F32, kind="ExternalOutput").ap()
    trunk_kernel(nc, *args, out)
    r = run_bass_kernel_spmd(nc, [arrays], core_ids=[0])
    return np.ascontiguousarray(r.results[0]["out_fm"].T)[None]
```

```python
from contextlib import ExitStack

import numpy as np

import concourse.bass as bass
from concourse import mybir

F32 = mybir.dt.float32
F32R = mybir.dt.float32r
ALU = mybir.AluOpType
ACT = mybir.ActivationFunctionType

P = 128
D = 1024
T = 512
KT = D // P
TT = T // P
FF = 4 * D
EPS = 1e-6
C = 64
NCH = T // C
PAIRS = 4
LRU_C = 8.0
LN_EPS = 64e-5
EXP_HALF = float(np.exp(-0.5))
RET_HEADS = 4
RET_DV = 512
CHUNK = 2048
QUARTERS = 4

AB_CHUNK = 0
AB_TURN = 4
FFN0_CHUNK = AB_CHUNK + 1 + AB_TURN * PAIRS
RET_CHUNK0 = FFN0_CHUNK + 8 * QUARTERS
FFN1_CHUNK = RET_CHUNK0 + 8 * RET_HEADS
ALL_CHUNKS = FFN1_CHUNK + 8 * QUARTERS

V_NORM = 0
V_MU_LORA = 2 * 4 * KT
V_LAM = V_MU_LORA + 2
V_MIX = V_LAM + PAIRS
V_ONE = V_MIX + 3 * PAIRS
NVEC = V_ONE + 1

P_W2A2, P_G2, P_WA, P_WX, P_VEC = 0, 128, 256, 320, 384
(Q_W0, Q_A0, Q_KK, Q_KA, Q_RK, Q_CW, _, _, _, Q_CB, Q_BA, Q_BX, Q_LNW,
 Q_LNB) = range(P_VEC, P_VEC + 14)
NPAIR = P_VEC + 14

K_EYE, K_EYE2, K_HEAD1, K_HEADS = 0, 128, 192, 194
K_D16T, K_O32T, K_D16, K_O32, K_O64, K_LT, K_LE = (322 + 64 * i for i in range(7))
K_RESET = 322 + 64 * 7
NCONST = K_RESET + T
R_COS, R_SIN, R_DECAY = 0, T, 2 * T
NRET = 2 * T + RET_HEADS * T


SERIES = {
    "low_rank_products": "lin_w lin_a lin_g",
    "turned_products": "v_turned k_turned z_turned b_turned",
    "chunk_products": "ark_t azb_t azb azk_t arb_t",
    "power_products": "m2 m2_t m4 m4_t e2 e4 m8 e8",
    "gate_products": "gate_r gate_i",
    "inverse_products": "dd y32 x32 t32_t t32 y64 tt",
    "solved_products": "w1 w2 gg qq",
    "head_statistics": "kk_sum kk_spread y_sum y_var ln_spread",
    "low_rank_factors": "decay_rate iclr g_out",
    "decay_powers": "dec_inv dec dec_before",
    "vectors_by_token": "v_by_token k_by_token z_by_token b_by_token",
    "copied_by_act": "m2_s x2_s m4_s m8_s dd_s y32_s x32_s y64_s w1_s",
    "lru_factors": "lru_r lru_gates lru_tanh lru_a lru_root gelu",
    "masked_products": "ark nt nn e1 azk arb o32t o32 o64",
    "summed_by_dve": "m2_ts m4_ts e2_s e4_s dt_s t32_ts t32_s tt_s w2_s g_s q_s",
    "chunk_vectors": "kd_ready rd_ready rk_ready pc_ready kk_ready z_ready b_plain b_ready",
    "lru_steps": "lru_iu lru_scale lru_drive lru_h ya_ready",
    "head_outputs": "yc ln_inv yn y_affine y_bonus yb_ready",
}
SERIES_OF = {name: (group, k, len(names.split())) for group, names in SERIES.items()
             for k, name in enumerate(names.split())}


def constants():
    c = np.zeros((P, NCONST), np.float32)
    row, col = np.arange(P)[:, None] % C, np.arange(C)[None, :]
    c[:, K_EYE:K_EYE + P] = np.eye(P)
    c[:, K_EYE2:K_EYE2 + C] = row == col
    head = np.arange(P) // C
    c[:, K_HEAD1:K_HEAD1 + 2] = head[:, None] == np.arange(2)[None, :]
    c[:, K_HEADS:K_HEADS + P] = head[:, None] == head[None, :]
    for at, r, k in ((K_D16T, col, row), (K_D16, row, col)):
        c[:, at:at + C] = (r > k) & (r // 16 == k // 16)
    for at, r, k in ((K_O32T, col, row), (K_O32, row, col)):
        c[:, at:at + C] = (r > k) & (r // 16 != k // 16) & (r // 32 == k // 32)
    c[:, K_O64:K_O64 + C] = (row > col) & (row // 32 != col // 32)
    c[:, K_LT:K_LT + C] = row < col
    c[:, K_LE:K_LE + C] = row <= col
    c[:, K_RESET:] = np.arange(T)[None, :] % C != 0
    r = np.zeros((P, NRET), np.float32)
    inv = (1.0 / (np.float32(10000.0) ** (np.arange(P, dtype=np.float32) / P))).astype(np.float32)
    ang = (inv[:, None] * np.arange(T, dtype=np.float32)[None, :]).astype(np.float32).astype(np.float64)
    r[:, R_COS:R_COS + T] = np.cos(ang)
    r[:, R_SIN:R_SIN + T] = np.sin(ang)
    rel = np.arange(T)[None, :] - np.arange(P)[:, None]
    for h in range(RET_HEADS):
        decay = np.exp(np.log1p(-2.0 ** (-5.0 - h)) * np.maximum(rel, 0)) / 16.0
        r[:, R_DECAY + h * T:R_DECAY + (h + 1) * T] = np.where(rel >= 0, decay, 0.0)
    return c, r


class Turns:

    def __init__(self, kinds):
        self.n = [0] * kinds
        self.per = [0] * kinds
        self.turn = 0

    def loop(self, turn, per):
        self.turn, self.per = turn, per

    def end(self, turns):
        self.n = [n + (turns - 1) * p for n, p in zip(self.n, self.per)]
        self.loop(0, [0] * len(self.n))

    def next(self, kind):
        self.n[kind] += 1
        return self.now(kind)

    def now(self, kind):
        return self.n[kind] + self.turn * self.per[kind] if self.per[kind] else self.n[kind]


def trunk_kernel(nc, x, weights, pairs, vectors, const, ret_const, out):
    with ExitStack() as ctx:
        def sb(name, cols, dt=F32):
            return ctx.enter_context(nc.sbuf_tensor(name, [P] + (cols if isinstance(cols, list) else [cols]), dt))

        sems = {}

        def S(name):
            name = SERIES_OF.get(name, (name,))[0]
            if name not in sems:
                sems[name] = ctx.enter_context(nc.semaphore(name))
            return sems[name]

        def nth(name, n):
            if name not in SERIES_OF:
                return S(name), n
            _, place, size = SERIES_OF[name]
            return S(name), (n - 1) * size + place + 1

        h = sb("h", [KT, T])
        f = sb("f", [KT, T])
        XH = sb("XH", [KT, T], F32R)
        XL = sb("XL", [KT, T], F32R)
        raw = [sb(f"raw{i}", CHUNK) for i in range(2)]
        WH = [sb(f"WH{i}", CHUNK, F32R) for i in range(2)]
        WL = [sb(f"WL{i}", CHUNK, F32R) for i in range(2)]
        cst = sb("cst", NCONST)
        vec = sb("vec", NVEC)
        rstd = sb("rstd", 8)
        epsc = sb("epsc", 2)
        sp = sb("sp", [12, PAIRS])


        ARENA = 90 * 1024
        start = (nc.sbuf_base + 31) // 32 * 32
        sb("arena", ARENA // 4 + 8)

        class Place:

            def __init__(self):
                self.at = start

            def __call__(self, name, cols, dt=F32):
                cols = cols if isinstance(cols, list) else [cols]
                t = nc.alloc_sbuf_tensor_at(name, [P] + cols, dt, offset=self.at)
                self.at += (int(np.prod(cols)) * 4 + 31) // 32 * 32
                assert self.at <= start + ARENA, (name, self.at - start)
                return t

        norm = Place()
        sq, hn, sq_sum = norm("sq", [2, T]), norm("hn", [2, T]), norm("sq_sum", T)
        root = norm("root", T)
        NORM = norm.at
        ab = Place()
        W = [ab(f"W{i}", T) for i in range(12)]
        yH, yL = ab("yH", [2, T], F32R), ab("yL", [2, T], F32R)
        Ur, Uk, Uv = (ab(n, T + 1) for n in ("Ur", "Uk", "Uv"))
        Uax, Uag = ab("Uax", T + 3), ab("Uag", T)
        lora, gate_in = ab("lora", T), ab("gate_in", T)
        stage, pp = ab("stage", NPAIR), ab("pp", NPAIR)
        BDa, BDx = ab("BDa", P), ab("BDx", P)
        mixdiff = ab("mixdiff", T)
        bonus, gout, Rd = (ab(n, T) for n in ("bonus", "gout", "Rd"))
        Zt, Bt, Kt, Vt, ARB, ARK, X2 = (ab(n, T) for n in ("Zt", "Bt", "Kt", "Vt", "ARB", "ARK", "X2"))
        O32T, O32, O64 = (ab(n, T) for n in ("O32T", "O32", "O64"))
        lax, lra, lix, ldr, lgate = (ab(n, T) for n in ("lax", "lra", "lix", "ldr", "lgate"))
        kkm, kkroot, kkinv, lnroot, lninv, PC = (ab(n, 8) for n in
                                                 ("kkm", "kkroot", "kkinv", "lnroot", "lninv", "PC"))
        ffn = Place()
        ffn.at = NORM
        AH, AL = ffn("AH", [KT, T], F32R), ffn("AL", [KT, T], F32R)
        relu, squared = ffn("relu", [2, T]), ffn("squared", [2, T])
        re = Place()
        re.at = NORM
        BH, BL = re("BH", [4, T], F32R), re("BL", [4, T], F32R)
        qr, kr = re("qr", [2, T]), re("kr", [2, T])
        Vr, Sc = re("Vr", [TT, T]), re("Sc", [TT, T])
        rc = re("rc", NRET)
        sg, rt, yv = re("sg", [4, T]), re("rt", [4, T]), re("yv", [4, T])

        bank = [ctx.enter_context(nc.psum_tensor(f"bank{i}", [P, T], F32)) for i in range(8)]

        eye = cst[:, K_EYE:K_EYE + P]
        eye2 = cst[:, K_EYE2:K_EYE2 + C]
        heads = cst[:, K_HEADS:K_HEADS + P]
        head1 = cst[:, K_HEAD1:K_HEAD1 + 2]
        ones1 = vec[:, NVEC - 1:NVEC]
        X = [(XH[:, kt, :], XL[:, kt, :]) for kt in range(KT)]
        A = [(AH[:, kt, :], AL[:, kt, :]) for kt in range(KT)]

        def chunked(t):
            return t[:].rearrange("p (c t) -> p c t", t=C)

        def table(k):
            return cst[:, k:k + C][:, None, :].to_broadcast([P, NCH, C])

        def gain(layer, kind, kt):
            i = V_NORM + (layer * 4 + kind) * KT + kt
            return vec[:, i:i + 1]

        def pv(q):
            return pp[:, q:q + 1]

        def chunk(c, i=0, per=0):
            return (c + per * i if per else c), c % 2

        def split_hi(act, c, part=CHUNK, waits=True, piece=0, pieces=1):
            c, par = c
            if piece == 0:
                act.wait_ge(S(f"raw_loaded{par}"), (c - par) * 8 + 16)
                if waits and (not isinstance(c, int) or c >= 2):
                    act.wait_ge(S("chunk_begun"), c)
            cols = slice(part * piece // pieces, part * (piece + 1) // pieces)
            ins = nc.scalar.activation(WH[par][:, cols], raw[par][:, cols], ACT.Copy)
            if piece == pieces - 1:
                ins.then_inc(S("w_hi"), 1)

        def split_lo(dve, c, part=CHUNK, piece=0, pieces=1):
            c, par = c
            if piece == 0:
                dve.wait_ge(S("w_hi"), c + 1)
            cols = slice(part * piece // pieces, part * (piece + 1) // pieces)
            ins = nc.vector.tensor_tensor(WL[par][:, cols], raw[par][:, cols], WH[par][:, cols], ALU.subtract)
            if piece == pieces - 1:
                ins.then_inc(S("w_lo"), 1)

        def chunk_ready(pe, c):
            pe.wait_ge(S("w_hi"), c[0] + 1)
            pe.wait_ge(S("w_lo"), c[0] + 1)

        def wtile(par, row, col, width):
            o = row * width + col
            return WH[par][:, o:o + P], WL[par][:, o:o + P]

        def units(pe, use, banks, ws, xs, begins=False, tile_ready=None, part=None):
            for b in banks if part is None or part[0] == 0 else ():
                n = use.next(b)
                if not isinstance(n, int) or n > 1:
                    pe.wait_ge(S(f"acc_free{b}"), n - 1)
            sums(pe, banks, ws, xs, None, begins, tile_ready, part)

        def sums(pe, banks, ws, xs, signal=None, begins=False, tile_ready=None, part=None):
            for k, (xh, xl) in enumerate(xs):
                if part is not None and not part[0] <= k < part[1]:
                    continue
                if tile_ready:
                    tile_ready(k)
                for b, w in zip(banks, ws):
                    wh, wl = w[k]
                    mm = pe.matmul(bank[b][:], wh, xh, start=(k == 0), stop=False)
                    if begins and k == 0 and b == banks[0]:
                        mm.then_inc(S("chunk_begun"), 1)
                    pe.matmul(bank[b][:], wh, xl, start=False, stop=False)
                    mm = pe.matmul(bank[b][:], wl, xh, start=False, stop=(k == len(xs) - 1))
                    if k == len(xs) - 1:
                        mm.then_inc(S(signal or f"acc_full{b}"), 1)

        def sums_before(n):
            return n // 2 * (KT + 1) + n % 2 * KT

        def sum_by_token(pe, src, first, last):
            return pe.matmul(bank[6][0:1, :], ones1, src, start=first, stop=last)

        def turn_root(pe):
            for t in range(TT):
                mm = pe.matmul(bank[6][:, t:t + 1], root[0:1, t * P:(t + 1) * P], ones1[0:1, :],
                               start=True, stop=True)
            return mm

        def spread(pe):
            for t in range(TT):
                mm = pe.matmul(bank[7][:, t * P:(t + 1) * P], rstd[:, t:t + 1].to_broadcast([P, P]), eye,
                               start=True, stop=True)
            return mm

        def spread_rstd(pe, n):
            pe.wait_ge(S("root_ready"), n + 1)
            turn_root(pe).then_inc(S("root_turned"), 1)
            pe.wait_ge(S("rstd_ready"), n + 1)
            spread(pe).then_inc(S("rstd_spread"), 1)

        def input_norm_pe(pe, n):
            for kt in range(KT):
                pe.wait_ge(S("sq_ready"), n * KT + kt + 1)
                sum_by_token(pe, sq[:, kt % 2, :], kt == 0, kt == KT - 1).then_inc(S("sq_used"), 1)
            spread_rstd(pe, n)

        def output_norm_pe(pe, n):
            pe.wait_ge(S("sq_summed"), (n + 1) // 2 * (KT - 2))
            sum_by_token(pe, sq_sum[:], True, False)
            pe.wait_ge(S("sq_ready"), n * KT + KT)
            sum_by_token(pe, sq[:, (KT - 1) % 2, :], False, True).then_inc(S("sq_used"), 1)
            spread_rstd(pe, n)

        def output_norm_pool(pool, n):
            for kt in range(1, KT - 1):
                pool.wait_ge(S("sq_ready"), n * KT + kt + 1)
                done = n // 2 * (KT - 2) + kt - 1
                if done:
                    pool.wait_ge(S("sq_summed"), done)
                nc.gpsimd.tensor_tensor(sq_sum[:], sq[:, 0, :] if kt == 1 else sq_sum[:], sq[:, kt % 2, :],
                                        ALU.add).then_inc(S("sq_summed"), 1)

        def square(act, n, src, kt):
            if kt >= 2 and n % 2:
                act.wait_ge(S("sq_summed"), n // 2 * (KT - 2) + max(kt - 2, 1))
            elif kt >= 2:
                act.wait_ge(S("sq_used"), sums_before(n) + kt - 1)
            nc.scalar.activation(sq[:, kt % 2, :], src[:, kt, :], ACT.Square).then_inc(S("sq_ready"), 1)

        def root_mean(act, n):
            act.wait_ge(S("sq_used"), sums_before(n + 1))
            nc.scalar.activation(root[0:1, :], bank[6][0:1, :], ACT.Sqrt, bias=epsc[0:1, 0:1],
                                 scale=1.0 / D).then_inc(S("root_ready"), 1)

        def norm_dve(dve, n):
            dve.wait_ge(S("root_turned"), n + 1)
            nc.vector.reciprocal(rstd[:, 0:TT], bank[6][:, 0:TT]).then_inc(S("rstd_ready"), 1)
            dve.wait_ge(S("rstd_spread"), n + 1)

        def square_f(act, n, kt, use, b):
            act.wait_ge(S(f"acc_free{b}"), use.now(b))
            square(act, n, f, kt)

        def h_is_ready(eng, m, kt):
            eng.wait_ge(S("h_odd" if kt % 2 else "h_even"), m * KT // 2 + kt // 2 + 1)

        def add_to_h(ops, kt):
            ops.tensor_tensor(h[:, kt, :], h[:, kt, :], hn[:, kt % 2, :],
                              ALU.add).then_inc(S("h_odd" if kt % 2 else "h_even"), 1)

        def residual_dve(dve, n, m, layer, kind):
            norm_dve(dve, n)
            for kt in range(KT + 1):
                if kt < KT:
                    if kt >= 2:
                        h_is_ready(dve, m, kt - 2)
                    nc.vector.scalar_tensor_tensor(hn[:, kt % 2, :], f[:, kt, :], gain(layer, kind, kt),
                                                   bank[7][:], ALU.mult, ALU.mult).then_inc(S("post_term"), 1)
                if kt % 2:
                    dve.wait_ge(S("post_term"), m * KT + kt)
                    add_to_h(nc.vector, kt - 1)

        def residual_pool(pool, m):
            for kt in range(1, KT, 2):
                pool.wait_ge(S("post_term"), m * KT + kt + 1)
                add_to_h(nc.gpsimd, kt)

        def second_chunk_act(act, c):
            split_hi(act, chunk(c + 1), waits=False)

        def pre_act(act, n, m):
            for kt in range(KT):
                if m:
                    h_is_ready(act, m - 1, kt)
                elif kt % 4 == 0:
                    act.wait_ge(S(f"x_loaded{kt // 4}"), 16)
                square(act, n, h, kt)
            root_mean(act, n)
            if m == 0:
                split_hi(act, chunk(0))
            for kt in range(KT):
                act.wait_ge(S("hn_ready"), m * KT + kt + 1)
                nc.scalar.activation(XH[:, kt, :], hn[:, kt % 2, :], ACT.Copy).then_inc(S("x_hi"), 1)

        def x_low(eng, ops, m, kt):
            eng.wait_ge(S("x_hi"), m * KT + kt + 1)
            ops.tensor_tensor(XL[:, kt, :], hn[:, kt % 2, :], XH[:, kt, :],
                              ALU.subtract).then_inc(S(f"x_lo{kt % 2}"), 1)

        def pre_dve(dve, n, m, layer, kind):
            norm_dve(dve, n)
            if m:
                h_is_ready(dve, m - 1, KT - 1)
            else:
                split_lo(dve, chunk(0))
            for kt in range(KT + 1):
                if kt < KT:
                    if kt >= 2:
                        dve.wait_ge(S(f"x_lo{kt % 2}"), m * KT // 2 + kt // 2)
                    nc.vector.scalar_tensor_tensor(hn[:, kt % 2, :], h[:, kt, :], gain(layer, kind, kt),
                                                   bank[7][:], ALU.mult, ALU.mult).then_inc(S("hn_ready"), 1)
                if kt % 2:
                    x_low(dve, nc.vector, m, kt - 1)

        def pre_pool(pool, m):
            for kt in range(1, KT, 2):
                x_low(pool, nc.gpsimd, m, kt)

        def x_tiles(pe, m):
            def tile_ready(kt):
                pe.wait_ge(S("x_hi"), m * KT + kt + 1)
                pe.wait_ge(S(f"x_lo{kt % 2}"), m * KT // 2 + kt // 2 + 1)
            return tile_ready

        def add_to_f(dve, use, b, m):
            n = use.next(b)
            dve.wait_ge(S(f"acc_full{b}"), n)
            nc.vector.tensor_tensor(f[:, m, :], f[:, m, :], bank[b][:], ALU.add).then_inc(S(f"acc_free{b}"), 1)

        ACCS = 4

        def turns_then_last(eng, use, per, turns, body):
            with eng.Fori(0, turns - 1) as i:
                use.loop(i, per)
                body(i, False)
            use.end(turns - 1)
            body(turns - 1, True)

        def ffn_pe(pe, use, c0, m, layer, n):
            def quarter(q, last):
                done = 8 * QUARTERS * layer + 8 * q

                def a_tile(kt):
                    pe.wait_ge(S("a_hi"), done + kt + 1)
                    pe.wait_ge(S("a_lo"), done + kt + 1)
                for j in range(0, 16, 2):
                    c = chunk(c0 + j // 2, q, 8)
                    chunk_ready(pe, c)
                    ws = [[wtile(c[1], kt, k * P, 2 * P) for kt in range(KT)] for k in range(2)]
                    banks = [j % ACCS, (j + 1) % ACCS]
                    if j == 0:
                        units(pe, use, banks, ws, X, True, x_tiles(pe, m))
                        continue
                    for k in range(2):
                        units(pe, use, banks[k:k + 1], ws[k:k + 1], X if j < 8 else A, k == 0,
                              a_tile if j == 8 and k == 0 else None)
                if last:
                    output_norm_pe(pe, n)
            turns_then_last(pe, use, [4] * ACCS, QUARTERS, quarter)

        def ffn_act(act, use, c0, layer, n):
            def quarter(q, last):
                done = 8 * QUARTERS * layer + 8 * q
                for j in range(16):
                    if j and j % 2 == 0:
                        split_hi(act, chunk(c0 + j // 2 + 1, q, 8))
                    b = j % ACCS
                    u = use.next(b)
                    if j < 8:
                        act.wait_ge(S(f"acc_full{b}"), u)
                        if j >= 2:
                            act.wait_ge(S("a_lo"), done + j - 1)
                        nc.scalar.activation(relu[:, j % 2, :], bank[b][:], ACT.Relu).then_inc(S(f"acc_free{b}"), 1)
                        act.wait_ge(S(f"acc_free{b}"), u)
                        nc.scalar.activation(AH[:, j, :], relu[:, j % 2, :], ACT.Square).then_inc(S("a_hi"), 1)
                    elif last:
                        square_f(act, n, j - 8, use, b)
                if last:
                    root_mean(act, n)
                else:
                    split_hi(act, chunk(c0 + 9, q, 8))
            turns_then_last(act, use, [4] * ACCS, QUARTERS, quarter)

        def ffn_dve(dve, use, c0, layer, k):
            dve.wait_ge(S("f_zero"), k + 1)

            def quarter(q, last):
                done = 8 * QUARTERS * layer + 8 * q
                for j in range(16):
                    if j and j % 2 == 0:
                        split_lo(dve, chunk(c0 + j // 2 + 1, q, 8))
                    b = j % ACCS
                    if j >= 8:
                        add_to_f(dve, use, b, j - 8)
                        continue
                    u = use.next(b)
                    dve.wait_ge(S(f"acc_free{b}"), u)
                    if j >= 2:
                        dve.wait_ge(S("a_lo"), done + j - 1)
                    nc.vector.tensor_tensor(squared[:, j % 2, :], relu[:, j % 2, :], relu[:, j % 2, :],
                                            ALU.mult).then_inc(S("a_square"), 1)
                    dve.wait_ge(S("a_square"), done + j + 1)
                    dve.wait_ge(S("a_hi"), done + j + 1)
                    nc.vector.tensor_tensor(AL[:, j, :], squared[:, j % 2, :], AH[:, j, :],
                                            ALU.subtract).then_inc(S("a_lo"), 1)
                if not last:
                    split_lo(dve, chunk(c0 + 9, q, 8))
            turns_then_last(dve, use, [4] * ACCS, QUARTERS, quarter)

        UNITS = (("r", 0, 0, 0), ("k", 1, 0, 1), ("v", 0, 1, 0), ("ax", 1, 1, 1), ("ag", 0, 2, 0))
        ROWS = (slice(0, C), slice(C, P))

        def in_unit(pe, use, j, c0, i, per, part=None):
            name, b, k, half = UNITS[j]
            c = chunk(c0 + k, i, per)
            if half == 0 and (part is None or part[0] == 0):
                chunk_ready(pe, c)
            width = P if name == "ag" else 2 * P
            units(pe, use, [b], [[wtile(c[1], kt, half * P, width) for kt in range(KT)]], X, half == 0,
                  part=part)

        def in_split_hi(act, k, c0, i, per, piece=0, pieces=1):
            split_hi(act, chunk(c0 + k + 1, i, per), CHUNK // 2 if k == 1 else CHUNK, True, piece, pieces)

        def in_evac(act, use, j, pair):
            name, b, k, half = UNITS[j]
            n = use.next(b)
            act.wait_ge(S(f"acc_full{b}"), n)
            if not (isinstance(pair, int) and pair == 0):
                act.wait_ge(*nth({"r": "r_mixed", "k": "k_mixed", "v": "v_mixed", "ax": "lru_in",
                                  "ag": "gelu"}[name], pair))
            dst = {"r": Ur[:, 1:], "k": Uk[:, 1:], "v": Uv[:, 1:], "ax": Uax[:, 3:], "ag": Uag[:]}[name]
            nc.scalar.activation(dst, bank[b][:], ACT.Copy).then_inc(S(f"acc_free{b}"), 1)

        def in_split_lo(dve, k, c0, i, per, piece=0, pieces=1):
            split_lo(dve, chunk(c0 + k + 1, i, per), CHUNK // 2 if k == 1 else CHUNK, piece, pieces)

        def by_chunk(pe, b, terms, signal, add=False):
            pe.sem_inc(S("waits_passed"), 1)
            for c in range(NCH):
                cols = slice(c * C, (c + 1) * C)
                for rows in ROWS:
                    for k, (lhsT, rhs) in enumerate(terms):
                        rh = rhs[rows, :] if rhs is eye2 else rhs[rows, cols]
                        mm = pe.matmul(bank[b][rows, cols], lhsT[rows, cols], rh,
                                       start=(k == 0), stop=(k == len(terms) - 1))
            mm.then_inc(S(signal), 1)

        def head_sums(pe, b, src, signal):
            for t in range(TT):
                mm = pe.matmul(bank[b][:, 2 * t:2 * t + 2], src[:, t * P:(t + 1) * P], head1,
                               start=(t == 0), stop=(t == TT - 1), skip_group_check=True)
            mm.then_inc(S(signal), 1)

        def head_spread(pe, b, src, signal):
            for t in range(TT):
                for j, rows in enumerate(ROWS):
                    mm = pe.matmul(bank[b][rows, t * P:(t + 1) * P],
                                   src[:, 2 * t + j:2 * t + j + 1].to_broadcast([P, C]), eye,
                                   start=True, stop=True)
            mm.then_inc(S(signal), 1)

        def out_unit(pe, use, m, p, out_c):
            c = chunk(*out_c)
            if m == 0:
                chunk_ready(pe, c)

            def y_tile(k):
                for name in ("ya_hi", "ya_lo") if k == 0 else ("yb_hi", "yb_lo"):
                    pe.wait_ge(*nth(name, p + 1))
            units(pe, use, [m % 2], [[wtile(c[1], k, m * P, D) for k in range(2)]],
                  [(yH[:, k, :], yL[:, k, :]) for k in range(2)], m == 0, y_tile if m == 0 else None)

        def vectors_pe(pe, use, p, out_c=None):
            n = p + 1
            left = list(range(KT))

            def out_units(count):
                for _ in range(count if out_c else 0):
                    out_unit(pe, use, left.pop(0), p - 1, out_c)

            def need(*names):
                for name in names:
                    pe.wait_ge(*nth(name, n))

            pe.wait_ge(S("pp_ready"), n)
            pe.wait_ge(S("lora_ready"), 2)
            pe.matmul(bank[2][:], pp[0:C, P_W2A2:P_W2A2 + P], lora[0:C, :], start=True, stop=True).then_inc(S("lin_w"), 1)
            pe.matmul(bank[3][:], pp[C:P, P_W2A2:P_W2A2 + P], lora[C:P, :], start=True, stop=True).then_inc(S("lin_a"), 1)
            pe.matmul(bank[4][:], pp[:, P_G2:P_G2 + P], gate_in[:], start=True, stop=True).then_inc(S("lin_g"), 1)
            out_units(1)
            need("kk_sq")
            head_sums(pe, 5, W[7], "kk_sum")
            out_units(1)
            need("v_mixed")
            by_chunk(pe, 7, [(W[2], eye2)], "v_turned")
            out_units(2)
            need("kd_ready")
            by_chunk(pe, 6, [(W[7], eye2)], "k_turned")
            out_units(1)
            need("kk_inv")
            head_spread(pe, 5, kkinv, "kk_spread")
            need("k_by_token", "rd_ready")
            by_chunk(pe, 6, [(W[7], Rd)], "ark_t")
            need("v_by_token", "rk_ready")
            pe.matmul(bank[7][:], heads, W[3][:], start=True, stop=True).then_inc(S("rk_sum"), 1)
            out_units(1)
            need("z_ready", "decay_rate", "iclr", "g_out")
            by_chunk(pe, 4, [(W[5], eye2)], "z_turned")
            need("b_ready")
            by_chunk(pe, 2, [(W[6], W[5])], "azb_t")
            out_units(1)
            by_chunk(pe, 3, [(W[5], W[6])], "azb")
            by_chunk(pe, 5, [(W[6], eye2)], "b_turned")
            out_units(1)
            need("z_by_token")
            by_chunk(pe, 4, [(W[7], W[5])], "azk_t")
            need("b_by_token")
            by_chunk(pe, 5, [(W[6], Rd)], "arb_t")

        def chain_pe(pe, use, p, in_c=None):
            n = p + 1
            tiles = [(j, k) for j in range(len(UNITS)) for k in range(KT)]

            def fill(count):
                for _ in range(count if in_c else 0):
                    j, k = tiles.pop(0)
                    in_unit(pe, use, j, *in_c, (k, k + 1))

            def need(*names):
                for name in names:
                    pe.wait_ge(*nth(name, n))

            fill(1)
            need("nt", "nn", "ark", "bonus")
            by_chunk(pe, 6, [(W[0], W[1])], "m2")
            by_chunk(pe, 7, [(W[1], W[0])], "m2_t")
            fill(1)
            need("azk")
            by_chunk(pe, 4, [(W[8], Vt)], "x2")
            fill(1)
            need("m2_s", "m2_ts", "e1", "o32t", "o32", "o64")
            by_chunk(pe, 2, [(W[10], W[9])], "m4")
            by_chunk(pe, 3, [(W[9], W[10])], "m4_t")
            fill(1)
            need("x2_s")
            by_chunk(pe, 4, [(W[9], W[4])], "e2")
            fill(1)
            need("m4_s", "m4_ts", "e2_s")
            by_chunk(pe, 3, [(W[11], W[5])], "e4")
            by_chunk(pe, 2, [(W[3], W[11])], "m8")
            fill(2)
            need("m8_s", "e4_s")
            by_chunk(pe, 4, [(W[6], W[7])], "e8")
            fill(2)
            need("dt_s")
            by_chunk(pe, 2, [(W[0], eye2)], "dd")
            by_chunk(pe, 3, [(O32, W[0])], "y32")
            fill(1)
            need("dd_s")
            by_chunk(pe, 4, [(O32T, W[1])], "x32")
            fill(1)
            need("y32_s", "arb")
            by_chunk(pe, 5, [(W[1], W[9])], "t32_t")
            need("x32_s")
            by_chunk(pe, 6, [(W[0], W[10])], "t32")
            fill(2)
            need("t32_ts")
            by_chunk(pe, 2, [(O64, W[11])], "y64")
            fill(2)
            need("t32_s", "y64_s")
            by_chunk(pe, 3, [(W[3], W[5])], "tt")
            fill(2)
            need("tt_s")
            by_chunk(pe, 4, [(W[6], Zt)], "w1")
            fill(1)
            by_chunk(pe, 5, [(W[6], X2)], "w2")
            need("w1_s")
            by_chunk(pe, 7, [(W[7], Bt)], "gg")
            fill(1)
            by_chunk(pe, 6, [(W[7], ARB)], "qq")
            fill(2)
            need("w2_s", "g_s", "q_s")
            need("lru_in")
            pe.wait_ge(S("gate_blocks"), 4 * n)
            pe.matmul(bank[5][:], BDa[:], lax[:], start=True, stop=True).then_inc(S("gate_r"), 1)
            pe.matmul(bank[6][:], BDx[:], lax[:], start=True, stop=True).then_inc(S("gate_i"), 1)
            pe.sem_inc(S("waits_passed"), 1)
            for c in range(NCH):
                cols = slice(c * C, (c + 1) * C)
                prev = slice((c - 1) * C, c * C)
                if c < NCH - 1:
                    for rows in ROWS:
                        pe.matmul(bank[3 + c % 2][rows, cols], Bt[rows, cols], W[9][rows, cols], start=True, stop=False)
                        mm = pe.matmul(bank[3 + c % 2][rows, cols], Kt[rows, cols], Vt[rows, cols], start=False, stop=(c == 0))
                    if c == 0:
                        mm.then_inc(S("state_full"), 1)
                for rows in ROWS:
                    pe.matmul(bank[2][rows, cols], W[9][rows, cols], ARB[rows, cols], start=True, stop=False)
                    mm = pe.matmul(bank[2][rows, cols], Vt[rows, cols], ARK[rows, cols], start=False, stop=(c == 0))
                if c:
                    fill(1)
                    pe.wait_ge(S("state"), (NCH - 1) * p + c)
                    pe.sem_inc(S("waits_passed"), 1)
                    if c < NCH - 1:
                        for rows in ROWS:
                            mm = pe.matmul(bank[3 + c % 2][rows, cols], W[11][rows, cols], W[3][rows, prev],
                                           start=False, stop=True)
                        mm.then_inc(S("state_full"), 1)
                    for rows in ROWS:
                        mm = pe.matmul(bank[2][rows, cols], W[3][rows, prev], W[10][rows, cols],
                                       start=False, stop=True)
            mm.then_inc(S("y_heads"), 1)
            fill(2)
            need("ys")
            pe.matmul(bank[4][:], heads, W[0][:], start=True, stop=True).then_inc(S("y_sum"), 1)
            fill(3)
            need("yc_sq", "lru_gates")
            head_sums(pe, 5, W[5], "y_var")
            fill(4)
            need("ln_inv")
            head_spread(pe, 6, lninv, "ln_spread")
            fill(3)
            assert in_c is None or not tiles

        def vectors_act(act, use, p, out_c=None):
            n = p + 1

            def need(*names):
                for name in names:
                    act.wait_ge(*nth(name, n))

            def evac(name, dst, b, ready, func=ACT.Copy, **kw):
                need(name)
                nc.scalar.activation(dst[:], bank[b][:], func, **kw).then_inc(S(ready), 1)

            def split(piece):
                if out_c:
                    split_hi(act, chunk(out_c[0] + 1, *out_c[1:]), piece=piece, pieces=2)

            if out_c:
                for m in range(KT):
                    use.next(m % 2)
                for name in ("yb_hi", "yb_lo"):
                    act.wait_ge(*nth(name, p))
            need("pp_ready", "k_mixed")
            nc.scalar.activation(W[7][:], W[1][:], ACT.Square, scale=pv(Q_KK)).then_inc(S("kk_sq"), 1)
            evac("lin_w", W[3], 2, "decay_rate", ACT.Sigmoid, bias=pv(Q_W0))
            evac("lin_a", W[4], 3, "iclr", ACT.Sigmoid, bias=pv(Q_A0))
            evac("lin_g", gout, 4, "g_out")
            need("cumlog")
            nc.scalar.activation(W[9][:], W[5][:], ACT.Exp, scale=EXP_HALF).then_inc(S("dec_inv"), 1)
            nc.scalar.activation(W[8][:], W[5][:], ACT.Exp, scale=-EXP_HALF).then_inc(S("dec"), 1)
            need("cumlog_before")
            nc.scalar.activation(W[10][:], W[6][:], ACT.Exp, scale=-EXP_HALF).then_inc(S("dec_before"), 1)
            split(0)
            need("kk_floor")
            nc.scalar.activation(kkroot[:], kkm[:], ACT.Sqrt).then_inc(S("kk_root"), 1)
            evac("v_turned", Vt, 7, "v_by_token")
            evac("k_turned", Kt, 6, "k_by_token")
            split(1)
            evac("z_turned", Zt, 4, "z_by_token")
            evac("b_turned", Bt, 5, "b_by_token")

        def chain_act(act, use, p, in_c=None):
            n = p + 1

            def need(*names):
                for name in names:
                    act.wait_ge(*nth(name, n))

            def evac(name, dst, b, ready, func=ACT.Copy, **kw):
                need(name)
                nc.scalar.activation(dst[:], bank[b][:], func, **kw).then_inc(S(ready), 1)

            def split(k, piece=0, pieces=1):
                if in_c:
                    in_split_hi(act, k, *in_c, piece, pieces)

            def copy_out(j):
                if in_c:
                    in_evac(act, use, j, p + 1)

            evac("m2", W[9], 6, "m2_s")
            evac("x2", X2, 4, "x2_s")
            split(0, 0, 4)
            split(0, 1, 4)
            evac("m4", W[11], 2, "m4_s")
            split(0, 2, 4)
            split(0, 3, 4)
            need("e4")
            evac("m8", W[6], 2, "m8_s")
            evac("dd", W[1], 2, "dd_s")
            evac("y32", W[9], 3, "y32_s")
            copy_out(0)
            evac("x32", W[10], 4, "x32_s")
            evac("y64", W[5], 2, "y64_s")
            copy_out(1)
            evac("w1", W[7], 4, "w1_s")
            evac("gate_r", lra, 5, "lru_r", ACT.Sigmoid, bias=pv(Q_BA))
            evac("gate_i", lix, 6, "lru_gates", ACT.Sigmoid, bias=pv(Q_BX))
            need("lru_r")
            nc.scalar.activation(ldr[:], lra[:], ACT.Tanh, scale=sp[:, 10, bass.ds(p, 1)]).then_inc(S("lru_tanh"), 1)
            need("lru_tanh")
            nc.scalar.activation(lra[:], lra[:], ACT.Exp, scale=sp[:, 11, bass.ds(p, 1)]).then_inc(S("lru_a"), 1)
            nc.scalar.activation(ldr[:], ldr[:], ACT.Sqrt).then_inc(S("lru_root"), 1)
            nc.scalar.activation(lgate[:], Uag[:], ACT.Gelu_apprx_tanh).then_inc(S("gelu"), 1)
            split(1)
            copy_out(2)
            evac("y_heads", W[0], 2, "ys")
            need("yc")
            nc.scalar.activation(W[5][:], W[10][:], ACT.Square).then_inc(S("yc_sq"), 1)
            copy_out(3)
            need("ya_ready")
            nc.scalar.activation(yH[:, 0, :], lix[:], ACT.Copy).then_inc(S("ya_hi"), 1)
            need("y_var")
            nc.scalar.activation(lnroot[:], bank[5][:, 0:8], ACT.Sqrt, bias=epsc[:, 1:2],
                                 scale=1.0 / C).then_inc(S("ln_root"), 1)
            split(2)
            copy_out(4)
            need("yb_ready")
            nc.scalar.activation(yH[:, 1, :], W[7][:], ACT.Copy).then_inc(S("yb_hi"), 1)

        MIXES = ((Uk, W[1], 1, "k_mixed"), (Ur, W[0], 0, "r_mixed"), (Uv, W[2], 2, "v_mixed"))

        def shift_mix(dve, p, j):
            U, dst, k, name = MIXES[j]
            mu = V_MIX + k * PAIRS + p
            if j:
                dve.wait_ge(*nth(MIXES[j - 1][3], p + 1))
            nc.vector.tensor_tensor(mixdiff[:], U[:, 0:T], U[:, 1:T + 1], ALU.subtract).then_inc(S("mix_diff"), 1)
            dve.wait_ge(S("mix_diff"), 3 * p + j + 1)
            nc.vector.scalar_tensor_tensor(dst[:], mixdiff[:], vec[:, bass.ds(mu, 1)], U[:, 1:T + 1], ALU.mult,
                                           ALU.add).then_inc(S(name), 1)

        def vectors_dve(dve, use, p, out_c=None):
            n = p + 1

            def need(*names):
                for name in names:
                    dve.wait_ge(*nth(name, n))

            def masked(dst, b, k, name, ready):
                need(name)
                nc.vector.tensor_tensor(chunked(dst), chunked(bank[b]), table(k), ALU.mult).then_inc(S(ready), 1)

            left = list(range(KT))

            def add_out(count):
                for _ in range(count if out_c else 0):
                    m = left.pop(0)
                    add_to_f(dve, use, m % 2, m)

            def split(piece):
                if out_c:
                    split_lo(dve, chunk(out_c[0] + 1, *out_c[1:]), piece=piece, pieces=2)

            dve.wait_ge(S("f_zero"), 1)
            need("decay_rate")
            nc.vector.tensor_tensor_scan(W[5][:], cst[:, K_RESET:K_RESET + T], W[3][:], 0.0, ALU.mult,
                                         ALU.add).then_inc(S("cumlog"), 1)
            need("cumlog")
            nc.vector.tensor_tensor(W[6][:], W[5][:], W[3][:], ALU.subtract).then_inc(S("cumlog_before"), 1)
            add_out(1)
            need("kk_sum")
            nc.vector.tensor_scalar(kkm[:], bank[5][:, 0:8], 1e-24, None, ALU.max).then_inc(S("kk_floor"), 1)
            need("iclr")
            nc.vector.tensor_scalar(X2[:], W[4][:], -1.0, pv(Q_KA), ALU.add, ALU.mult).then_inc(S("k_factor"), 1)
            need("k_factor")
            nc.vector.scalar_tensor_tensor(X2[:], X2[:], 1.0, W[1][:], ALU.add, ALU.mult).then_inc(S("k_new"), 1)
            need("k_new", "dec_inv")
            nc.vector.tensor_tensor(W[7][:], X2[:], W[9][:], ALU.mult).then_inc(S("kd_ready"), 1)
            add_out(2)
            need("kk_root")
            nc.vector.reciprocal(kkinv[:], kkroot[:]).then_inc(S("kk_inv"), 1)
            need("dec")
            nc.vector.tensor_tensor(Rd[:], W[0][:], W[8][:], ALU.mult).then_inc(S("rd_ready"), 1)
            need("cumlog_before")
            nc.vector.scalar_tensor_tensor(W[3][:], W[0][:], pv(Q_RK), X2[:], ALU.mult,
                                           ALU.mult).then_inc(S("rk_ready"), 1)
            nc.vector.tensor_copy(PC[:], chunked(W[8])[:, :, C - 1]).then_inc(S("pc_ready"), 1)
            add_out(2)
            need("kk_spread")
            nc.vector.scalar_tensor_tensor(W[11][:], W[1][:], pv(Q_KK), bank[5][:], ALU.mult,
                                           ALU.mult).then_inc(S("kk_ready"), 1)
            need("kk_ready", "dec_before")
            nc.vector.scalar_tensor_tensor(W[5][:], W[11][:], -1.0, W[10][:], ALU.mult,
                                           ALU.mult).then_inc(S("z_ready"), 1)
            nc.vector.tensor_tensor(mixdiff[:], W[11][:], W[4][:], ALU.mult).then_inc(S("b_plain"), 1)
            need("b_plain")
            nc.vector.tensor_tensor(W[6][:], mixdiff[:], W[9][:], ALU.mult).then_inc(S("b_ready"), 1)
            split(0)
            masked(ARK, 6, K_LE, "ark_t", "ark")
            need("rk_sum")
            nc.vector.tensor_tensor(bonus[:], W[2][:], bank[7][:], ALU.mult).then_inc(S("bonus"), 1)
            add_out(1)
            masked(W[0], 2, K_D16T, "azb_t", "nt")
            masked(W[1], 3, K_D16, "azb", "nn")
            add_out(1)
            split(1)
            need("nt", "b_plain")
            nc.vector.tensor_tensor(chunked(W[4]), chunked(W[0]), table(K_EYE2), ALU.add).then_inc(S("e1"), 1)
            need("pc_ready", "rd_ready")
            masked(W[8], 4, K_LT, "azk_t", "azk")
            add_out(1)

        def chain_dve(dve, use, p, in_c=None):
            n = p + 1

            def need(*names):
                for name in names:
                    dve.wait_ge(*nth(name, n))

            def add(dst, a, b, name, ready):
                need(name)
                nc.vector.tensor_tensor(dst[:], a[:], bank[b][:], ALU.add).then_inc(S(ready), 1)

            def masked(dst, b, k, name, ready):
                need(name)
                nc.vector.tensor_tensor(chunked(dst), chunked(bank[b]), table(k), ALU.mult).then_inc(S(ready), 1)

            def conv(k):
                taps = Uax[:, k:k + T]
                if k == 0:
                    nc.vector.tensor_scalar(lax[:], taps, pv(Q_CW), pv(Q_CB), ALU.mult, ALU.add).then_inc(S("conv"), 1)
                    return
                dve.wait_ge(S("conv"), 3 * p + k)
                nc.vector.scalar_tensor_tensor(lax[:], taps, pv(Q_CW + k), lax[:], ALU.mult,
                                               ALU.add).then_inc(S("lru_in" if k == 3 else "conv"), 1)

            copied = []
            if in_c:
                for _, b, _, _ in UNITS:
                    copied.append((b, use.next(b)))

            def mix(j):
                if in_c:
                    b, count = copied[MIXES[j][2]]
                    dve.wait_ge(S(f"acc_free{b}"), count)
                    shift_mix(dve, p + 1, j)

            def split(k, piece=0, pieces=1):
                if in_c:
                    in_split_lo(dve, k, *in_c, piece, pieces)

            masked(ARB, 5, K_LE, "arb_t", "arb")
            masked(O32T, 2, K_O32T, "azb_t", "o32t")
            masked(O32, 3, K_O32, "azb", "o32")
            masked(O64, 3, K_O64, "azb", "o64")
            need("m2_t")
            nc.vector.tensor_copy(W[10][:], bank[7][:]).then_inc(S("m2_ts"), 1)
            dve.wait_ge(S("blocks_zero"), 2)
            for dst, k in ((BDa, P_WA), (BDx, P_WX)):
                for j, rows in enumerate(ROWS):
                    nc.vector.tensor_copy(dst[rows, j * C:(j + 1) * C],
                                          pp[rows, k:k + C]).then_inc(S("gate_blocks"), 1)
            for k in range(4):
                conv(k)
            need("m4_t")
            nc.vector.tensor_copy(W[3][:], bank[3][:]).then_inc(S("m4_ts"), 1)
            need("e1")
            add(W[5], W[4], 4, "e2", "e2_s")
            split(0, 0, 4)
            need("e2_s")
            add(W[7], W[5], 3, "e4", "e4_s")
            split(0, 1, 4)
            need("e4_s")
            add(W[0], W[7], 4, "e8", "dt_s")
            split(0, 2, 4)
            split(0, 3, 4)
            need("dt_s")
            add(W[11], W[0], 5, "t32_t", "t32_ts")
            need("dd_s")
            add(W[3], W[1], 6, "t32", "t32_s")
            need("t32_ts")
            add(W[6], W[11], 3, "tt", "tt_s")
            need("w2")
            nc.vector.tensor_copy(W[9][:], bank[5][:]).then_inc(S("w2_s"), 1)
            need("t32_ts", "gg", "tt_s")
            nc.vector.tensor_tensor(chunked(W[11]), chunked(bank[7]), table(K_EYE2), ALU.add).then_inc(S("g_s"), 1)
            need("rd_ready")
            add(W[10], Rd, 6, "qq", "q_s")
            for c in range(NCH - 1):
                cols = slice(c * C, (c + 1) * C)
                dve.wait_ge(S("state_full"), (NCH - 1) * p + c + 1)
                nc.vector.tensor_scalar(W[3][:, cols], bank[3 + c % 2][:, cols], PC[:, c:c + 1], None,
                                        ALU.mult).then_inc(S("state"), 1)
                if c == 4:
                    need("lru_gates", "lru_in")
                    nc.vector.tensor_tensor(lix[:], lix[:], lax[:], ALU.mult).then_inc(S("lru_iu"), 1)
            split(1)
            need("lru_a", "lru_root")
            nc.vector.scalar_tensor_tensor(ldr[:], lra[:], 1.0, ldr[:], ALU.add, ALU.mult).then_inc(S("lru_scale"), 1)
            need("lru_scale", "lru_iu")
            nc.vector.tensor_tensor(ldr[:], ldr[:], lix[:], ALU.mult).then_inc(S("lru_drive"), 1)
            need("ys", "y_sum")
            nc.vector.scalar_tensor_tensor(W[10][:], bank[4][:], -1.0 / C, W[0][:], ALU.mult,
                                           ALU.add).then_inc(S("yc"), 1)
            need("lru_drive")
            nc.vector.tensor_tensor_scan(lix[:], lra[:], ldr[:], 0.0, ALU.mult, ALU.add).then_inc(S("lru_h"), 1)
            need("lru_h", "gelu")
            nc.vector.tensor_tensor(lix[:], lix[:], lgate[:], ALU.mult).then_inc(S("ya_ready"), 1)
            mix(0)
            need("ln_root")
            nc.vector.reciprocal(lninv[:], lnroot[:]).then_inc(S("ln_inv"), 1)
            mix(1)
            need("ya_hi", "ya_ready")
            nc.vector.tensor_tensor(yL[:, 0, :], lix[:], yH[:, 0, :], ALU.subtract).then_inc(S("ya_lo"), 1)
            split(2)
            need("ln_spread", "yc")
            nc.vector.tensor_tensor(W[6][:], W[10][:], bank[6][:], ALU.mult).then_inc(S("yn"), 1)
            need("yn", "norm_vectors")
            nc.vector.tensor_scalar(W[6][:], W[6][:], pv(Q_LNW), pv(Q_LNB), ALU.mult, ALU.add).then_inc(S("y_affine"), 1)
            need("y_affine", "bonus")
            nc.vector.tensor_tensor(W[6][:], W[6][:], bonus[:], ALU.add).then_inc(S("y_bonus"), 1)
            need("y_bonus", "g_out")
            nc.vector.tensor_tensor(W[7][:], W[6][:], gout[:], ALU.mult).then_inc(S("yb_ready"), 1)
            need("yb_ready", "yb_hi")
            nc.vector.tensor_tensor(yL[:, 1, :], W[7][:], yH[:, 1, :], ALU.subtract).then_inc(S("yb_lo"), 1)
            mix(2)

        def last_out_pe(pe, use, p, out_c):
            for m in range(KT):
                out_unit(pe, use, m, p, out_c)
            output_norm_pe(pe, 1)

        def last_out_act(act, use, p, out_c):
            split_hi(act, chunk(out_c[0] + 1))
            for m in range(KT):
                use.next(m % 2)
                square_f(act, 1, m, use, m % 2)
            root_mean(act, 1)

        def last_out_dve(dve, use, p, out_c):
            split_lo(dve, chunk(out_c[0] + 1))
            for m in range(KT):
                add_to_f(dve, use, m % 2, m)

        def mixers_ab(eng, use, start, chain, last_out):
            turns = PAIRS - 1
            start(eng, use, 0)
            with eng.Fori(0, turns) as p:
                use.loop(p, [7, 6, 0, 0])
                chain(eng, use, p, (AB_TURN, p, AB_TURN))
                start(eng, use, p + 1, (AB_TURN + 3, p, AB_TURN))
            use.end(turns)
            chain(eng, use, turns)
            last_out(eng, use, turns, (AB_TURN + AB_TURN * turns, 0, 0))

        RET_OUT = [2, 3, 0, 1, 0, 1, 0, 1]

        def ret_pe(pe, use, m, n):
            def head(hd, last):
                n4 = 4 * hd
                c = chunk(RET_CHUNK0, hd, 8)
                chunk_ready(pe, c)
                units(pe, use, [0, 1], [[wtile(c[1], kt, j * P, 2 * P) for kt in range(KT)] for j in range(2)], X,
                      True, x_tiles(pe, m))
                c = chunk(RET_CHUNK0 + 1, hd, 8)
                chunk_ready(pe, c)
                for j in range(2):
                    sums(pe, [6 + j], [[wtile(c[1], kt, j * P, 2 * P) for kt in range(KT)]], X,
                         "keys_full", begins=(j == 0))
                for half in range(2):
                    c = chunk(RET_CHUNK0 + 2 + half, hd, 8)
                    chunk_ready(pe, c)
                    for k in range(4):
                        kt = half * 4 + k
                        wh, wl = (w[c[1]][:, k * T:(k + 1) * T] for w in (WH, WL))
                        for t in range(TT):
                            tok = slice(t * P, (t + 1) * P)
                            mm = pe.matmul(bank[2 + t][:], XH[:, kt, tok], wh, start=(kt == 0), stop=False)
                            if k == 0 and t == 0:
                                mm.then_inc(S("chunk_begun"), 1)
                            pe.matmul(bank[2 + t][:], XH[:, kt, tok], wl, start=False, stop=False)
                            mm = pe.matmul(bank[2 + t][:], XL[:, kt, tok], wh, start=False, stop=(kt == KT - 1))
                mm.then_inc(S("v_full"), 1)

                def gate(E, part=None):
                    c = chunk(RET_CHUNK0 + 4 + E // 2, hd, 8)
                    if E % 2 == 0:
                        chunk_ready(pe, c)
                    units(pe, use, [E % 2], [[wtile(c[1], kt, E % 2 * P, 2 * P) for kt in range(KT)]], X, E % 2 == 0,
                          part=part)

                gate(0)
                pe.wait_ge(S("qk_rotated"), n4 + 4)
                pe.wait_ge(S("v_out_act"), 2 * hd + 2)
                pe.wait_ge(S("v_out_dve"), 2 * hd + 2)
                for J in range(TT):
                    for k in range(2):
                        mm = pe.matmul(bank[2 + J][:, 0:T - J * P], kr[:, k, J * P:(J + 1) * P], qr[:, k, J * P:],
                                       start=(k == 0), stop=(k == 1))
                    mm.then_inc(S("scores"), 1)
                gate(1)
                for E in range(4):
                    for J in range(TT):
                        if E == 0:
                            pe.wait_ge(S("decayed"), n4 + J + 1)
                        mm = pe.matmul(bank[2 + E][:, J * P:], Vr[:, J, E * P:(E + 1) * P], Sc[:, J, 0:T - J * P],
                                       start=(J == 0), stop=(J == TT - 1), skip_group_check=True)
                    mm.then_inc(S("y_full"), 1)
                gate(2)
                pe.wait_ge(S("ysq_summed"), 2 * hd + 2)
                sum_by_token(pe, sq_sum[:], True, False)
                pe.wait_ge(S("ysq_ready"), n4 + 4)
                sum_by_token(pe, sq[:, 1, :], False, True).then_inc(S("ysq_used"), 1)
                gate(3, (0, 2))
                pe.wait_ge(S("y_root"), hd + 1)
                pe.sem_inc(S("waits_passed"), 1)
                turn_root(pe).then_inc(S("y_root_turned"), 1)
                gate(3, (2, 4))
                pe.wait_ge(S("y_inv"), hd + 1)
                spread(pe).then_inc(S("y_spread"), 1)
                gate(3, (4, KT))

                def b_tile(k):
                    pe.wait_ge(S("y_hi"), n4 + k + 1)
                    pe.wait_ge(S("y_lo"), n4 + k + 1)
                B = [(BH[:, k, :], BL[:, k, :]) for k in range(4)]
                for j in range(0, KT, 2):
                    c = chunk(RET_CHUNK0 + 6 + j // 4, hd, 8)
                    if j % 4 == 0:
                        chunk_ready(pe, c)
                    ws = [[wtile(c[1], k, (j + i) % 4 * P, T) for k in range(4)] for i in range(2)]
                    if j == 0:
                        units(pe, use, RET_OUT[0:2], ws, B, True, b_tile)
                    else:
                        for i in range(2):
                            units(pe, use, [RET_OUT[j + i]], [ws[i]], B, j % 4 == 0 and i == 0)
                if last:
                    output_norm_pe(pe, n)
            turns_then_last(pe, use, [6, 6, 1, 1], RET_HEADS, head)

        def ret_act(act, use, n):
            def head(hd, last):
                n4 = 4 * hd
                use.next(0), use.next(1)
                for k in (2, 3, 4):
                    split_hi(act, chunk(RET_CHUNK0 + k, hd, 8))
                act.wait_ge(S("v_full"), hd + 1)
                for t in range(2):
                    nc.scalar.activation(Vr[:, t, :], bank[2 + t][:], ACT.Copy).then_inc(S("v_out_act"), 1)

                def gate(E):
                    act.wait_ge(S(f"acc_full{E % 2}"), use.next(E % 2))
                    nc.scalar.activation(sg[:, E, :], bank[E % 2][:], ACT.Silu).then_inc(S(f"acc_free{E % 2}"), 1)
                split_hi(act, chunk(RET_CHUNK0 + 5, hd, 8))
                gate(0)
                gate(1)
                for E in range(4):
                    act.wait_ge(S("y_full"), n4 + E + 1)
                    if E >= 2:
                        act.wait_ge(S("ysq_summed"), 2 * hd + 1)
                    nc.scalar.activation(sq[:, E % 2, :], bank[2 + E][:], ACT.Square).then_inc(S("ysq_ready"), 1)
                split_hi(act, chunk(RET_CHUNK0 + 6, hd, 8))
                gate(2)
                act.wait_ge(S("ysq_used"), hd + 1)
                nc.scalar.activation(root[0:1, :], bank[6][0:1, :], ACT.Sqrt, bias=epsc[0:1, 0:1],
                                     scale=1.0 / RET_DV).then_inc(S("y_root"), 1)
                for E in range(4):
                    if E == 3:
                        gate(3)
                    act.wait_ge(S("y_ready"), n4 + E + 1)
                    nc.scalar.activation(BH[:, E, :], yv[:, E, :], ACT.Copy).then_inc(S("y_hi"), 1)
                for half in range(2):
                    split_hi(act, chunk(RET_CHUNK0 + 7 + half, hd, 8))
                    for j in range(4):
                        b = RET_OUT[4 * half + j]
                        use.next(b)
                        if last:
                            square_f(act, n, 4 * half + j, use, b)
                if last:
                    root_mean(act, n)
                else:
                    split_hi(act, chunk(RET_CHUNK0 + 9, hd, 8))
            turns_then_last(act, use, [6, 6, 1, 1], RET_HEADS, head)

        def ret_dve(dve, use, k_zero):
            cos, sin = rc[:, R_COS:R_COS + T], rc[:, R_SIN:R_SIN + T]
            dve.wait_ge(S("rc_loaded"), 16)

            def head(hd, last):
                n4 = 4 * hd
                for k, dst in ((0, qr), (1, kr)):
                    if k == 0:
                        n0, n1 = use.next(0), use.next(1)
                        dve.wait_ge(S("acc_full0"), n0)
                        dve.wait_ge(S("acc_full1"), n1)
                        one, two, read = bank[0], bank[1], ("acc_free0", "acc_free1")
                    else:
                        dve.wait_ge(S("keys_full"), 2 * hd + 2)
                        dve.wait_ge(S("qk_rotated"), n4 + 2)
                        one, two, read = bank[6], bank[7], ("keys_read", "keys_read")
                    nc.vector.tensor_tensor(rt[:, 0, :], one[:], cos, ALU.mult)
                    nc.vector.tensor_tensor(rt[:, 1, :], two[:], sin, ALU.mult)
                    nc.vector.tensor_tensor(rt[:, 2, :], two[:], cos, ALU.mult).then_inc(S(read[1]), 1)
                    nc.vector.tensor_tensor(rt[:, 3, :], one[:], sin, ALU.mult).then_inc(S(read[0]), 1)
                    if k == 0:
                        dve.wait_ge(S("acc_free1"), n1)
                        dve.wait_ge(S("acc_free0"), n0)
                    else:
                        dve.wait_ge(S("keys_read"), 2 * hd + 2)
                    nc.vector.tensor_tensor(dst[:, 0, :], rt[:, 0, :], rt[:, 1, :], ALU.subtract).then_inc(S("qk_rotated"), 1)
                    nc.vector.tensor_tensor(dst[:, 1, :], rt[:, 2, :], rt[:, 3, :], ALU.add).then_inc(S("qk_rotated"), 1)
                    split_lo(dve, chunk(RET_CHUNK0 + 2 + k, hd, 8))
                split_lo(dve, chunk(RET_CHUNK0 + 4, hd, 8))
                dve.wait_ge(S("v_full"), hd + 1)
                for t in range(2, 4):
                    nc.vector.tensor_copy(Vr[:, t, :], bank[2 + t][:]).then_inc(S("v_out_dve"), 1)
                split_lo(dve, chunk(RET_CHUNK0 + 5, hd, 8))
                for J in range(TT):
                    dve.wait_ge(S("scores"), n4 + J + 1)
                    nc.vector.tensor_tensor(Sc[:, J, 0:T - J * P], bank[2 + J][:, 0:T - J * P],
                                            rc[:, bass.ds(R_DECAY + T * hd, T - J * P)],
                                            ALU.mult).then_inc(S("decayed"), 1)

                def gated(E):
                    dve.wait_ge(S("ysq_ready"), n4 + E + 1)
                    dve.wait_ge(S(f"acc_free{E % 2}"), use.next(E % 2))
                    nc.vector.tensor_tensor(yv[:, E, :], bank[2 + E][:], sg[:, E, :], ALU.mult).then_inc(S("y_gated"), 1)
                gated(0)
                gated(1)
                split_lo(dve, chunk(RET_CHUNK0 + 6, hd, 8))
                gated(2)
                dve.wait_ge(S("y_root_turned"), hd + 1)
                nc.vector.reciprocal(rstd[:, 0:TT], bank[6][:, 0:TT]).then_inc(S("y_inv"), 1)
                dve.wait_ge(S("y_spread"), hd + 1)
                for E in range(5):
                    if E == 3:
                        gated(3)
                    if E < 4:
                        dve.wait_ge(S("y_gated"), n4 + E + 1)
                        nc.vector.tensor_tensor(yv[:, E, :], yv[:, E, :], bank[7][:], ALU.mult).then_inc(S("y_ready"), 1)
                    if E:
                        dve.wait_ge(S("y_hi"), n4 + E)
                        nc.vector.tensor_tensor(BL[:, E - 1, :], yv[:, E - 1, :], BH[:, E - 1, :],
                                                ALU.subtract).then_inc(S("y_lo"), 1)
                dve.wait_ge(S("f_zero"), k_zero + 1)
                for half in range(2):
                    split_lo(dve, chunk(RET_CHUNK0 + 7 + half, hd, 8))
                    for j in range(4):
                        add_to_f(dve, use, RET_OUT[4 * half + j], half * 4 + j)
                if not last:
                    split_lo(dve, chunk(RET_CHUNK0 + 9, hd, 8))
            turns_then_last(dve, use, [6, 6, 1, 1], RET_HEADS, head)

        block = ctx.enter_context(nc.Block())

        @block.sync
        def _(sync):
            half = KT // 2
            for j in range(2):
                sync.dma_start(h[:, j * half:(j + 1) * half, :],
                               x[j * D // 2:(j + 1) * D // 2, :].rearrange("(k p) t -> p k t", p=P)
                               ).then_inc(S(f"x_loaded{j}"), 16)
                if j == 0:
                    sync.dma_start(vec[:], vectors).then_inc(S("vec_loaded"), 16)
                    sync.dma_start(cst[:], const).then_inc(S("const_loaded"), 16)
            for c in range(2):
                sync.dma_start(raw[c][:], weights[c]).then_inc(S(f"raw_loaded{c}"), 16)
            with sync.Fori(0, ALL_CHUNKS // 2) as i:
                for c in range(2):
                    sync.wait_ge(S("w_lo"), 2 * i + c + 1)
                    sync.dma_start(raw[c][:], weights[bass.ds(2 * i + (2 + c), 1)].rearrange(
                        "a p c -> (a p) c")).then_inc(S(f"raw_loaded{c}"), 16)
            for kt in range(KT):
                h_is_ready(sync, 3, kt)
                sync.dma_start(out[kt * P:(kt + 1) * P, :], h[:, kt, :]).then_inc(S("out_stored"), 16)
            sync.wait_ge(S("out_stored"), 16 * KT)
            for c in range(2):
                sync.wait_ge(S(f"raw_loaded{c}"), 16 * (ALL_CHUNKS // 2 + 1))

        @block.gpsimd
        def _(pool):
            nc.gpsimd.memset(epsc[:, 0:1], EPS).then_inc(S("eps"), 1)
            nc.gpsimd.memset(epsc[:, 1:2], LN_EPS).then_inc(S("eps"), 1)
            for U, w in ((Ur, 1), (Uk, 1), (Uv, 1), (Uax, 3)):
                nc.gpsimd.memset(U[:, 0:w], 0.0).then_inc(S("edge_zero"), 1)
            nc.gpsimd.memset(BDa[:], 0.0).then_inc(S("blocks_zero"), 1)
            nc.gpsimd.memset(BDx[:], 0.0).then_inc(S("blocks_zero"), 1)
            nc.gpsimd.memset(f[:], 0.0).then_inc(S("f_zero"), 1)
            pool.wait_ge(S("f_zero"), 1)
            pool.dma_start(stage[:], pairs[0]).then_inc(S("stage_loaded"), 16)

            def take_pair(p, later):
                pool.wait_ge(S("stage_loaded"), 16 * p + 16)
                if later:
                    pool.wait_ge(*nth("lru_gates", p))
                pool.sem_inc(S("waits_passed"), 1)
                nc.gpsimd.tensor_copy(pp[:, 0:Q_LNW], stage[:, 0:Q_LNW]).then_inc(S("pp_ready"), 1)
                if later:
                    pool.wait_ge(*nth("y_affine", p))
                    pool.sem_inc(S("waits_passed"), 1)
                nc.gpsimd.tensor_copy(pp[:, Q_LNW:], stage[:, Q_LNW:]).then_inc(S("norm_vectors"), 1)
                pool.wait_ge(S("pp_ready"), p + 1)
                pool.wait_ge(S("norm_vectors"), p + 1)

            take_pair(0, False)
            pre_pool(pool, 0)
            with pool.Fori(1, PAIRS) as p:
                pool.dma_start(stage[:], pairs[bass.ds(p, 1)].rearrange("a p c -> (a p) c")).then_inc(S("stage_loaded"), 16)
                take_pair(p, True)
            for k in range(1, 5):
                output_norm_pool(pool, 2 * k - 1)
                residual_pool(pool, k - 1)
                if k == 4:
                    continue
                pre_pool(pool, k)
                h_is_ready(pool, k - 1, KT - 2)
                nc.gpsimd.memset(f[:], 0.0).then_inc(S("f_zero"), 1)
                if k == 1:
                    pool.dma_start(rc[:], ret_const).then_inc(S("rc_loaded"), 16)
                if k == 2:
                    with pool.Fori(0, RET_HEADS) as hd:
                        pool.wait_ge(S("ysq_ready"), 4 * hd + 2)
                        pool.sem_inc(S("waits_passed"), 1)
                        nc.gpsimd.tensor_tensor(sq_sum[:], sq[:, 0, :], sq[:, 1, :], ALU.add).then_inc(S("ysq_summed"), 1)
                        pool.wait_ge(S("ysq_ready"), 4 * hd + 3)
                        pool.wait_ge(S("ysq_summed"), 2 * hd + 1)
                        pool.sem_inc(S("waits_passed"), 1)
                        nc.gpsimd.tensor_tensor(sq_sum[:], sq_sum[:], sq[:, 0, :], ALU.add).then_inc(S("ysq_summed"), 1)
            pool.wait_ge(S("f_zero"), 4)

        @block.tensor
        def _(pe):
            use = Turns(4)
            pe.wait_ge(S("vec_loaded"), 16)
            pe.wait_ge(S("const_loaded"), 16)
            pe.wait_ge(S("ones_ready"), 1)
            input_norm_pe(pe, 0)
            chunk_ready(pe, chunk(0))
            units(pe, use, [0, 1], [[wtile(0, kt, j * P, 2 * P) for kt in range(KT)] for j in range(2)], X, True,
                  x_tiles(pe, 0))
            for j in range(5):
                in_unit(pe, use, j, 1, 0, 0)
            mixers_ab(pe, use, vectors_pe, chain_pe, last_out_pe)
            input_norm_pe(pe, 2)
            ffn_pe(pe, use, FFN0_CHUNK, 1, 0, 3)
            input_norm_pe(pe, 4)
            ret_pe(pe, use, 2, 5)
            input_norm_pe(pe, 6)
            ffn_pe(pe, use, FFN1_CHUNK, 3, 1, 7)

        @block.scalar
        def _(act):
            use = Turns(4)
            act.wait_ge(S("eps"), 2)
            act.wait_ge(S("vec_loaded"), 16)
            act.wait_ge(S("sp_abs"), 1)
            nc.scalar.activation(sp[:, 2, :], sp[:, 1, :], ACT.Exp, scale=-1.0).then_inc(S("sp_exp"), 1)
            pre_act(act, 0, 0)
            split_hi(act, chunk(1))
            act.wait_ge(S("edge_zero"), 4)
            for j, U in enumerate((Ur, Uk)):
                n = use.next(j)
                act.wait_ge(S(f"acc_full{j}"), n)
                nc.scalar.activation(U[:, 1:], bank[j][:], ACT.Copy).then_inc(S(f"acc_free{j}"), 1)
            act.wait_ge(S("lora_mixed"), 2)
            nc.scalar.activation(lora[0:C, :], lora[0:C, :], ACT.Tanh).then_inc(S("lora_ready"), 1)
            nc.scalar.activation(gate_in[:], gate_in[:], ACT.Sigmoid).then_inc(S("lora_ready"), 1)
            for j in range(5):
                if j % 2 == 0:
                    in_split_hi(act, j // 2, 1, 0, 0)
                in_evac(act, use, j, 0)
            mixers_ab(act, use, vectors_act, chain_act, last_out_act)
            second_chunk_act(act, FFN0_CHUNK)
            pre_act(act, 2, 1)
            ffn_act(act, use, FFN0_CHUNK, 0, 3)
            second_chunk_act(act, RET_CHUNK0)
            pre_act(act, 4, 2)
            ret_act(act, use, 5)
            second_chunk_act(act, FFN1_CHUNK)
            pre_act(act, 6, 3)
            ffn_act(act, use, FFN1_CHUNK, 1, 7)

        @block.vector
        def _(dve):
            use = Turns(4)
            V = nc.vector
            dve.wait_ge(S("vec_loaded"), 16)
            dve.wait_ge(S("const_loaded"), 16)
            V.memset(ones1, 1.0).then_inc(S("ones_ready"), 1)
            lam = vec[:, V_LAM:V_LAM + PAIRS]
            V.tensor_scalar(sp[:, 0, :], lam, -1.0, 0.0, ALU.mult, ALU.max).then_inc(S("sp_max"), 1)
            V.scalar_tensor_tensor(sp[:, 1, :], lam, -1.0, lam, ALU.mult, ALU.max).then_inc(S("sp_abs"), 1)
            steps = [0]

            def step(ins):
                ins.then_inc(S("sp_step"), 1)
                steps[0] += 1
                dve.wait_ge(S("sp_step"), steps[0])
            dve.wait_ge(S("sp_exp"), 1)
            step(V.tensor_scalar(sp[:, 3, :], sp[:, 2, :], 2.0, None, ALU.add))
            step(V.reciprocal(sp[:, 4, :], sp[:, 3, :]))
            step(V.tensor_tensor(sp[:, 5, :], sp[:, 4, :], sp[:, 2, :], ALU.mult))
            step(V.tensor_tensor(sp[:, 6, :], sp[:, 5, :], sp[:, 5, :], ALU.mult))
            step(V.tensor_scalar(sp[:, 7, :], sp[:, 6, :], 1.0 / 15, None, ALU.mult))
            for k in (13, 11, 9, 7, 5, 3):
                step(V.scalar_tensor_tensor(sp[:, 7, :], sp[:, 7, :], 1.0 / k, sp[:, 6, :], ALU.add, ALU.mult))
            step(V.scalar_tensor_tensor(sp[:, 8, :], sp[:, 7, :], 1.0, sp[:, 5, :], ALU.add, ALU.mult))
            dve.wait_ge(S("sp_max"), 1)
            step(V.scalar_tensor_tensor(sp[:, 9, :], sp[:, 8, :], 2.0, sp[:, 0, :], ALU.mult, ALU.add))
            step(V.tensor_scalar(sp[:, 10, :], sp[:, 9, :], LRU_C / 2, None, ALU.mult))
            step(V.tensor_scalar(sp[:, 11, :], sp[:, 9, :], -LRU_C, None, ALU.mult))

            pre_dve(dve, 0, 0, 0, 0)
            split_lo(dve, chunk(1))
            for j, (U, dst) in enumerate(((Ur, lora), (Uk, gate_in))):
                n = use.next(j)
                dve.wait_ge(S(f"acc_free{j}"), n)
                if j:
                    dve.wait_ge(S("lora_mixed"), 1)
                V.tensor_tensor(mixdiff[:], U[:, 0:T], U[:, 1:T + 1], ALU.subtract).then_inc(S("lora_diff"), 1)
                dve.wait_ge(S("lora_diff"), j + 1)
                V.scalar_tensor_tensor(dst[:], mixdiff[:], vec[:, V_MU_LORA + j:V_MU_LORA + j + 1], U[:, 1:T + 1],
                                       ALU.mult, ALU.add).then_inc(S("lora_mixed"), 1)
            dve.wait_ge(S("lora_mixed"), 2)
            for j in range(5):
                if j % 2 == 0:
                    in_split_lo(dve, j // 2, 1, 0, 0)
                use.next(UNITS[j][1])
            for b in range(2):
                dve.wait_ge(S(f"acc_free{b}"), use.now(b))
            for j in range(3):
                shift_mix(dve, 0, j)
            mixers_ab(dve, use, vectors_dve, chain_dve, last_out_dve)
            residual_dve(dve, 1, 0, 0, 1)
            split_lo(dve, chunk(FFN0_CHUNK + 1))
            pre_dve(dve, 2, 1, 0, 2)
            ffn_dve(dve, use, FFN0_CHUNK, 0, 1)
            residual_dve(dve, 3, 1, 0, 3)
            split_lo(dve, chunk(RET_CHUNK0 + 1))
            pre_dve(dve, 4, 2, 1, 0)
            ret_dve(dve, use, 2)
            residual_dve(dve, 5, 2, 1, 1)
            split_lo(dve, chunk(FFN1_CHUNK + 1))
            pre_dve(dve, 6, 3, 1, 2)
            ffn_dve(dve, use, FFN1_CHUNK, 1, 3)
            residual_dve(dve, 7, 3, 1, 3)


def tile_rows(w, rows, cols):
    part = w[rows, cols]
    k = part.shape[0] // P
    return part.reshape(k, P, part.shape[1]).transpose(1, 0, 2).reshape(P, -1)


def weight_stream(a):
    s = lambda at, n: slice(at, at + n)
    every = slice(None)
    ab_in, ab_out = a["ab_w_in"][0], a["ab_w_out"][0]
    W2 = D // 2
    chunks = [tile_rows(ab_in, every, s(2 * W2 + 3 * W2, 2 * P))]

    def pair_in(p):
        col = {"ax": p * P, "ag": W2 + p * P, "r": 2 * W2 + p * P, "k": 3 * W2 + p * P, "v": 4 * W2 + p * P}
        for one, two in (("r", "k"), ("v", "ax")):
            both = np.concatenate([ab_in[:, s(col[one], P)], ab_in[:, s(col[two], P)]], axis=1)
            chunks.append(tile_rows(both, every, every))
        ag = tile_rows(ab_in, every, s(col["ag"], P))
        chunks.append(np.concatenate([ag, ag], axis=1))

    def pair_out(p):
        rows = np.concatenate([ab_out[s(p * P, P)], ab_out[s(W2 + p * P, P)]], axis=0)
        chunks.append(tile_rows(rows, every, every))

    pair_in(0)
    for p in range(PAIRS):
        if p + 1 < PAIRS:
            pair_in(p + 1)
        pair_out(p)

    def mlp(layer):
        w1, w2 = a["ffn_w_in"][layer], a["ffn_w_out"][layer]
        for q in range(QUARTERS):
            for j in range(4):
                chunks.append(tile_rows(w1, every, s(q * D + j * 2 * P, 2 * P)))
            for j in range(4):
                chunks.append(tile_rows(w2, s(q * D, D), s(j * 2 * P, 2 * P)))

    mlp(0)
    r_in, r_out = a["ret_w_in"][0], a["ret_w_out"][0]
    for hd in range(RET_HEADS):
        chunks.append(tile_rows(r_in, every, s(hd * 2 * P, 2 * P)))
        chunks.append(tile_rows(r_in, every, s(D + hd * 2 * P, 2 * P)))
        for half in range(2):
            chunks.append(tile_rows(r_in, s(half * D // 2, D // 2), s(2 * D + hd * T, T)))
        for half in range(2):
            chunks.append(tile_rows(r_in, every, s(4 * D + hd * T + half * 2 * P, 2 * P)))
        for half in range(2):
            chunks.append(tile_rows(r_out, s(hd * T, T), s(half * T, T)))
    mlp(1)
    while len(chunks) < 2 * (ALL_CHUNKS // 2) + 2:
        chunks.append(chunks[-1])
    return np.stack(chunks)


def pair_tables(a):
    out = []
    for p in range(PAIRS):
        s = slice(p * P, (p + 1) * P)
        columns = [a["rwkv_w0"][0][s], a["rwkv_a0"][0][s], a["rwkv_k_k"][0][s], a["rwkv_k_a"][0][s],
                   a["rwkv_r_k"][0][s], *(a["lru_conv_w"][0][i][s] for i in range(4)), a["lru_conv_b"][0][s],
                   a["lru_ba"][0][s], a["lru_bx"][0][s], a["rwkv_ln_w"][0][s], a["rwkv_ln_b"][0][s]]
        out.append(np.concatenate(
            [np.concatenate([a["rwkv_w2"][0][:, s], a["rwkv_a2"][0][:, s]], axis=0), a["rwkv_g2"][0][:, s],
             a["lru_wa"][0][2 * p:2 * p + 2].reshape(P, C), a["lru_wx"][0][2 * p:2 * p + 2].reshape(P, C),
             np.stack(columns, axis=1)], axis=1))
    return np.stack(out)


def vector_table(a):
    norms = np.stack([a[k] for k in ("norm_mix_pre", "norm_mix_post", "norm_ffn_pre", "norm_ffn_post")], axis=1)
    norms = norms.reshape(2 * 4 * KT, P).T
    mu = a["rwkv_mu"][0][3 * D // 2:].reshape(2, P).T
    lam = a["lru_lambda"][0].reshape(PAIRS, P).T
    mix = a["rwkv_mu"][0][:3 * D // 2].reshape(3 * PAIRS, P).T
    return np.concatenate([norms, mu, lam, mix, lam[:, 0:1]], axis=1)


def kernel(**inputs):
    import concourse.bacc as bacc
    from concourse.bass_utils import run_bass_kernel_spmd

    a = {k: np.asarray(v) for k, v in inputs.items()}
    const, ret_const = constants()
    arrays = {
        "x_fm": np.ascontiguousarray(a["x"][0].T),
        "weights": np.ascontiguousarray(weight_stream(a)),
        "pairs": np.ascontiguousarray(pair_tables(a)),
        "vectors": np.ascontiguousarray(vector_table(a)),
        "const": const,
        "ret_const": ret_const,
    }
    nc = bacc.Bacc("TRN2", target_bir_lowering=False, num_devices=1)
    args = [nc.dram_tensor(k, v.shape, F32, kind="ExternalInput").ap() for k, v in arrays.items()]
    out = nc.dram_tensor("out_fm", (D, T), F32, kind="ExternalOutput").ap()
    trunk_kernel(nc, *args, out)
    r = run_bass_kernel_spmd(nc, [arrays], core_ids=[0])
    return np.ascontiguousarray(r.results[0]["out_fm"].T)[None]
```
